# Optimizing a Trainium2 kernel written in Bass

```python
import math
import jax, jax.numpy as jnp
from jax import lax
import numpy as np

D_MODEL = 1024
BATCH = 1
SEQ = 256
DEPTH = 1
DEC_BATCH = 1
DEC_SEQ = 1024
PAST_LEN = 128

GLA_HEADS = 4
GLA_DK = 64
GLA_DV = 128
GLA_QK_WIDTH = GLA_HEADS * GLA_DK
GLA_WIDTH = GLA_HEADS * GLA_DV
GLA_GATE_RANK = 16
GLA_GATE_TAU = 16.0
GLA_CHUNK = 64
RWKV_HEAD = 64
RWKV_WIDTH = D_MODEL - GLA_WIDTH
RWKV_HEADS = RWKV_WIDTH // RWKV_HEAD
RWKV_DECAY_RANK = 64
RWKV_AAA_RANK = 64
RWKV_GATE_RANK = 128
RWKV_GN_EPS = 64e-5
MIX_WIDTH = GLA_WIDTH + RWKV_WIDTH
GLA_SPLITS = (GLA_QK_WIDTH, GLA_QK_WIDTH, GLA_WIDTH, GLA_WIDTH, GLA_GATE_RANK, GLA_GATE_RANK)
RWKV_SPLITS = (RWKV_WIDTH, RWKV_WIDTH, RWKV_WIDTH, RWKV_DECAY_RANK, RWKV_DECAY_RANK, RWKV_AAA_RANK, RWKV_GATE_RANK)
GLA_COLS = sum(GLA_SPLITS)
RWKV_COLS = sum(RWKV_SPLITS)
IN_COLS = GLA_COLS + RWKV_COLS
D_FF = 2816
MEM_TOKENS = 256
MEM_HEADS = 4
MEM_HEAD_DIM = D_MODEL // MEM_HEADS
LN_EPS = 1e-5
DEEPNORM_ALPHA = (2.0 * DEPTH) ** 0.25
DEEPNORM_BETA = (8.0 * DEPTH) ** -0.25

kernel_name = 'hybrid_gla_rwkv7_macaron_encoder'

def _split(t, sizes):
    offs = np.cumsum(np.array(sizes))[:-1].tolist()
    return jnp.split(t, offs, axis=-1)

def _layer_norm(x, g, b, eps=LN_EPS):
    xf = x.astype(jnp.float32)
    mu = jnp.mean(xf, axis=-1, keepdims=True)
    var = jnp.mean(jnp.square(xf - mu), axis=-1, keepdims=True)
    return ((xf - mu) * lax.rsqrt(var + eps) * g + b).astype(x.dtype)

def _swiglu(x, w_in, w_out):
    gate, up = jnp.split(x @ w_in, 2, axis=-1)
    return (jax.nn.silu(gate) * up) @ w_out

def _gla_chunked(q, k, v, log_a):
    B, T, H, DK = q.shape
    DV = v.shape[-1]
    C = GLA_CHUNK
    n = T // C

    def blocks(t):
        return t.reshape(B, n, C, H, t.shape[-1]).transpose(0, 3, 1, 2, 4)

    q, k, v, log_a = blocks(q), blocks(k), blocks(v), blocks(log_a)
    b = jnp.cumsum(log_a, axis=3)
    b_last = b[:, :, :, -1:, :]
    b_ref = 0.5 * b_last
    scores = jnp.einsum('bhncd,bhnsd->bhncs', q * jnp.exp(b - b_ref), k * jnp.exp(b_ref - b))
    prefix_mask = jnp.tril(jnp.ones((C, C), dtype=bool))
    scores = jnp.where(prefix_mask, scores, 0.0)
    o_intra = jnp.einsum('bhncs,bhnse->bhnce', scores, v)
    kv = jnp.einsum('bhncd,bhnce->nbhde', k * jnp.exp(b_last - b), v)
    chunk_decay = jnp.exp(b_last[:, :, :, 0, :]).transpose(2, 0, 1, 3)

    def step(S, inp):
        dec, kv_n = inp
        return dec[..., None] * S + kv_n, S

    _, S_prev = lax.scan(step, jnp.zeros((B, H, DK, DV), jnp.float32), (chunk_decay, kv))
    o_inter = jnp.einsum('bhncd,nbhde->bhnce', q * jnp.exp(b), S_prev)
    o = o_intra + o_inter
    return o.transpose(0, 2, 3, 1, 4).reshape(B, T, H, DV)

def _rwkv7_scan(r, decay, k, v, kk, a, reverse):
    B, T, H, N = r.shape
    xs = tuple(t.transpose(1, 0, 2, 3) for t in (r, decay, k, v, kk, a))

    def step(S, inp):
        r_t, w_t, k_t, v_t, kk_t, a_t = inp
        sa = jnp.einsum('bhij,bhj->bhi', S, -kk_t)
        S = (S * w_t[:, :, None, :] + sa[..., None] * (kk_t * a_t)[:, :, None, :]
             + v_t[..., None] * k_t[:, :, None, :])
        y = jnp.einsum('bhij,bhj->bhi', S, r_t)
        return S, y

    _, y = lax.scan(step, jnp.zeros((B, H, N, N), jnp.float32), xs, reverse=reverse)
    return y.transpose(1, 0, 2, 3)

def _token_mix(h, w_in, gla_gate_up_fwd, gla_gate_b_fwd, gla_gate_up_bwd, gla_gate_b_bwd, gla_norm_g,
               rwkv_mu_prev, rwkv_mu_next, rwkv_w0_fwd, rwkv_w_up_fwd, rwkv_w0_bwd, rwkv_w_up_bwd,
               rwkv_a0, rwkv_a_up, rwkv_g_up, rwkv_k_k, rwkv_k_a, rwkv_r_k, rwkv_lnx_g, rwkv_lnx_b, w_out):
    B, T, _ = h.shape
    f32 = jnp.float32
    proj = h @ w_in
    gla_p, rw_p = proj[..., :GLA_COLS], proj[..., GLA_COLS:]

    def heads(t, d):
        return t.astype(f32).reshape(B, T, -1, d)

    flip = lambda t: jnp.flip(t, axis=1)

    q, k, v, g, gd_f, gd_b = _split(gla_p, GLA_SPLITS)
    q = heads(q, GLA_DK) * (GLA_DK ** -0.5)
    k = heads(k, GLA_DK)
    v = heads(v, GLA_DV)
    la_f = heads(jax.nn.log_sigmoid(gd_f @ gla_gate_up_fwd + gla_gate_b_fwd), GLA_DK) / GLA_GATE_TAU
    la_b = heads(jax.nn.log_sigmoid(gd_b @ gla_gate_up_bwd + gla_gate_b_bwd), GLA_DK) / GLA_GATE_TAU
    o = _gla_chunked(q, k, v, la_f) + flip(_gla_chunked(flip(q), flip(k), flip(v), flip(la_b)))
    o = o * lax.rsqrt(jnp.mean(jnp.square(o), axis=-1, keepdims=True) + LN_EPS)
    o = o.reshape(B, T, GLA_WIDTH) * gla_norm_g * jax.nn.silu(g.astype(f32))

    prev = jnp.pad(rw_p[:, :-1], ((0, 0), (1, 0), (0, 0)))
    nxt = jnp.pad(rw_p[:, 1:], ((0, 0), (0, 1), (0, 0)))
    rw = rw_p + rwkv_mu_prev * (prev - rw_p) + rwkv_mu_next * (nxt - rw_p)
    r, kr, vr, wd_f, wd_b, ad, gd = _split(rw, RWKV_SPLITS)

    def decay(wd, w0, up):
        w = -jax.nn.softplus(-(w0 + jnp.tanh(wd) @ up).astype(f32)) - 0.5
        return heads(jnp.exp(-jnp.exp(w)), RWKV_HEAD)

    dec_f = decay(wd_f, rwkv_w0_fwd, rwkv_w_up_fwd)
    dec_b = decay(wd_b, rwkv_w0_bwd, rwkv_w_up_bwd)
    a = jax.nn.sigmoid((rwkv_a0 + ad @ rwkv_a_up).astype(f32))
    gate = (jax.nn.sigmoid(gd) @ rwkv_g_up).astype(f32)
    kr = kr.astype(f32)
    kk = heads(kr * rwkv_k_k, RWKV_HEAD)
    kk = kk / jnp.maximum(jnp.sqrt(jnp.sum(jnp.square(kk), axis=-1, keepdims=True)), 1e-12)
    k2 = heads(kr * (1.0 + (a - 1.0) * rwkv_k_a), RWKV_HEAD)
    rH = heads(r, RWKV_HEAD)
    vH = heads(vr, RWKV_HEAD)
    aH = heads(a, RWKV_HEAD)
    y = (_rwkv7_scan(rH, dec_f, k2, vH, kk, aH, reverse=False)
         + _rwkv7_scan(rH, dec_b, k2, vH, kk, aH, reverse=True))
    mu = jnp.mean(y, axis=-1, keepdims=True)
    var = jnp.mean(jnp.square(y - mu), axis=-1, keepdims=True)
    y = ((y - mu) * lax.rsqrt(var + RWKV_GN_EPS)).reshape(B, T, RWKV_WIDTH) * rwkv_lnx_g + rwkv_lnx_b
    bonus = (jnp.sum(rH * k2 * rwkv_r_k, axis=-1, keepdims=True) * vH).reshape(B, T, RWKV_WIDTH)
    y = (y + bonus) * gate

    mixed = jnp.concatenate([o, y], axis=-1).astype(h.dtype)
    return mixed @ w_out

def _memory_attn(h, mem, mem_ln_g, mem_ln_b, w_q, w_kv, w_o):
    B, T, _ = h.shape
    M = mem.shape[1]
    m = _layer_norm(mem, mem_ln_g, mem_ln_b)
    q = (h @ w_q).reshape(B, T, MEM_HEADS, MEM_HEAD_DIM)
    k, v = jnp.split(m @ w_kv, 2, axis=-1)
    k = k.reshape(B, M, MEM_HEADS, MEM_HEAD_DIM)
    v = v.reshape(B, M, MEM_HEADS, MEM_HEAD_DIM)
    s = jnp.einsum('bthd,bmhd->bhtm', q, k).astype(jnp.float32) * (MEM_HEAD_DIM ** -0.5)
    p = jax.nn.softmax(s, axis=-1).astype(v.dtype)
    o = jnp.einsum('bhtm,bmhd->bthd', p, v).reshape(B, T, D_MODEL)
    return o @ w_o

def setup_inputs(seed: int = 0) -> dict:
    key = jax.random.key(seed)
    keys = iter(jax.random.split(key, 64))
    f32 = jnp.float32
    L = DEPTH

    def nrm(shape, scale):
        return scale * jax.random.normal(next(keys), shape, f32)

    def gain(n):
        return 1.0 + nrm((L, n), 0.02)

    def bias(n):
        return nrm((L, n), 0.02)

    d = D_MODEL
    return {
        'x_prompt': nrm((BATCH, SEQ, d), 1.0),
        'x_sample': nrm((DEC_BATCH, DEC_SEQ, d), 1.0),
        'mem_prompt': nrm((BATCH, MEM_TOKENS, d), 1.0),
        'mem_sample': nrm((DEC_BATCH, MEM_TOKENS, d), 1.0),
        'ffn1_w_in': nrm((L, d, 2 * D_FF), d ** -0.5),
        'ffn1_w_out': nrm((L, D_FF, d), DEEPNORM_BETA * D_FF ** -0.5),
        'ln_ffn1_g': gain(d),
        'ln_ffn1_b': bias(d),
        'mix_w_in': nrm((L, d, IN_COLS), d ** -0.5),
        'gla_gate_up_fwd': nrm((L, GLA_GATE_RANK, GLA_QK_WIDTH), GLA_GATE_RANK ** -0.5),
        'gla_gate_b_fwd': nrm((L, GLA_QK_WIDTH), 0.1),
        'gla_gate_up_bwd': nrm((L, GLA_GATE_RANK, GLA_QK_WIDTH), GLA_GATE_RANK ** -0.5),
        'gla_gate_b_bwd': nrm((L, GLA_QK_WIDTH), 0.1),
        'gla_norm_g': gain(GLA_WIDTH),
        'rwkv_mu_prev': jax.random.uniform(next(keys), (L, RWKV_COLS), f32, 0.1, 0.5),
        'rwkv_mu_next': jax.random.uniform(next(keys), (L, RWKV_COLS), f32, 0.1, 0.5),
        'rwkv_w0_fwd': -2.0 + nrm((L, RWKV_WIDTH), 0.5),
        'rwkv_w_up_fwd': nrm((L, RWKV_DECAY_RANK, RWKV_WIDTH), 0.1 * RWKV_DECAY_RANK ** -0.5),
        'rwkv_w0_bwd': -2.0 + nrm((L, RWKV_WIDTH), 0.5),
        'rwkv_w_up_bwd': nrm((L, RWKV_DECAY_RANK, RWKV_WIDTH), 0.1 * RWKV_DECAY_RANK ** -0.5),
        'rwkv_a0': nrm((L, RWKV_WIDTH), 0.1),
        'rwkv_a_up': nrm((L, RWKV_AAA_RANK, RWKV_WIDTH), 0.5 * RWKV_AAA_RANK ** -0.5),
        'rwkv_g_up': nrm((L, RWKV_GATE_RANK, RWKV_WIDTH), RWKV_GATE_RANK ** -0.5),
        'rwkv_k_k': 0.85 + nrm((L, RWKV_WIDTH), 0.05),
        'rwkv_k_a': 1.0 + nrm((L, RWKV_WIDTH), 0.05),
        'rwkv_r_k': nrm((L, RWKV_HEADS, RWKV_HEAD), 0.1),
        'rwkv_lnx_g': gain(RWKV_WIDTH),
        'rwkv_lnx_b': bias(RWKV_WIDTH),
        'mix_w_out': nrm((L, MIX_WIDTH, d), DEEPNORM_BETA * MIX_WIDTH ** -0.5),
        'ln_mix_g': gain(d),
        'ln_mix_b': bias(d),
        'mem_ln_g': gain(d),
        'mem_ln_b': bias(d),
        'ca_w_q': nrm((L, d, d), d ** -0.5),
        'ca_w_kv': nrm((L, d, 2 * d), d ** -0.5),
        'ca_w_o': nrm((L, d, d), DEEPNORM_BETA * d ** -0.5),
        'ln_ca_g': gain(d),
        'ln_ca_b': bias(d),
        'ffn2_w_in': nrm((L, d, 2 * D_FF), d ** -0.5),
        'ffn2_w_out': nrm((L, D_FF, d), DEEPNORM_BETA * D_FF ** -0.5),
        'ln_ffn2_g': gain(d),
        'ln_ffn2_b': bias(d),
    }

def reference(x_prompt, x_sample, mem_prompt, mem_sample,
              ffn1_w_in, ffn1_w_out, ln_ffn1_g, ln_ffn1_b,
              mix_w_in, gla_gate_up_fwd, gla_gate_b_fwd, gla_gate_up_bwd, gla_gate_b_bwd, gla_norm_g,
              rwkv_mu_prev, rwkv_mu_next, rwkv_w0_fwd, rwkv_w_up_fwd, rwkv_w0_bwd, rwkv_w_up_bwd,
              rwkv_a0, rwkv_a_up, rwkv_g_up, rwkv_k_k, rwkv_k_a, rwkv_r_k, rwkv_lnx_g, rwkv_lnx_b,
              mix_w_out, ln_mix_g, ln_mix_b,
              mem_ln_g, mem_ln_b, ca_w_q, ca_w_kv, ca_w_o, ln_ca_g, ln_ca_b,
              ffn2_w_in, ffn2_w_out, ln_ffn2_g, ln_ffn2_b):
    alpha = DEEPNORM_ALPHA

    def layer(x, mem, l):
        x = _layer_norm(alpha * x + 0.5 * _swiglu(x, ffn1_w_in[l], ffn1_w_out[l]), ln_ffn1_g[l], ln_ffn1_b[l])
        tm = _token_mix(x, mix_w_in[l], gla_gate_up_fwd[l], gla_gate_b_fwd[l], gla_gate_up_bwd[l],
                        gla_gate_b_bwd[l], gla_norm_g[l], rwkv_mu_prev[l], rwkv_mu_next[l],
                        rwkv_w0_fwd[l], rwkv_w_up_fwd[l], rwkv_w0_bwd[l], rwkv_w_up_bwd[l],
                        rwkv_a0[l], rwkv_a_up[l], rwkv_g_up[l], rwkv_k_k[l], rwkv_k_a[l], rwkv_r_k[l],
                        rwkv_lnx_g[l], rwkv_lnx_b[l], mix_w_out[l])
        x = _layer_norm(alpha * x + tm, ln_mix_g[l], ln_mix_b[l])
        ca = _memory_attn(x, mem, mem_ln_g[l], mem_ln_b[l], ca_w_q[l], ca_w_kv[l], ca_w_o[l])
        x = _layer_norm(alpha * x + ca, ln_ca_g[l], ln_ca_b[l])
        x = _layer_norm(alpha * x + 0.5 * _swiglu(x, ffn2_w_in[l], ffn2_w_out[l]), ln_ffn2_g[l], ln_ffn2_b[l])
        return x

    y_prompt = x_prompt
    y_sample = x_sample
    for l in range(DEPTH):
        y_prompt = layer(y_prompt, mem_prompt, l)
        y_sample = layer(y_sample, mem_sample, l)
    return (y_prompt, y_sample)


_drawn_inputs = setup_inputs


def setup_inputs(seed=0):
    import zlib

    import numpy as np

    out = dict(_drawn_inputs(seed))
    spreads = {}
    factors = {'gla_gate_up_fwd': 3.686,
     'gla_gate_b_fwd': 8.0,
     'gla_gate_up_bwd': 3.911,
     'gla_gate_b_bwd': 8.0,
     'gla_norm_g': 8.0,
     'rwkv_w_up_fwd': 8.0,
     'rwkv_w_up_bwd': 8.0,
     'rwkv_a0': 6.499,
     'rwkv_k_k': 8.0,
     'rwkv_k_a': 4.818,
     'rwkv_r_k': 2.877,
     'rwkv_lnx_g': 8.0,
     'rwkv_lnx_b': 8.0,
     'ln_mix_g': 2.906,
     'ln_mix_b': 2.746,
     'mem_ln_g': 8.0,
     'mem_ln_b': 26.175,
     'ln_ca_b': 2.69,
     'ln_ffn2_b': 2.893}
    for name, (base, spread) in spreads.items():
        noise = np.random.default_rng([zlib.crc32(name.encode()), seed]).standard_normal(out[name].shape)
        drawn = base * np.exp(spread * noise) if base else spread * noise
        out[name] = __import__('jax').numpy.asarray(drawn.astype(out[name].dtype))
    for name, factor in factors.items():
        out[name] = (out[name] * factor).astype(out[name].dtype)
    return out
```

```python
from contextlib import ExitStack

import numpy as np

import concourse.bass as bass
from concourse import mybir

ALU = mybir.AluOpType
ACT = mybir.ActivationFunctionType
F32 = mybir.dt.float32
F32R = mybir.dt.float32r
U32 = mybir.dt.uint32

P = 128
D = 1024
KT = D // P
T_PROMPT, T_SAMPLE = 256, 1024
T = T_PROMPT + T_SAMPLE
D_FF = 2816
FT = D_FF // P
BANK = 512
TOKEN_CHUNKS = ((0, 512), (512, 512), (1024, 256))
ALPHA = 2.0 ** 0.25
LN_EPS = 1e-5
NT = 256

GLA_DK, GLA_DV, GLA_TAU = 64, 128, 16.0
C = 64
N_CHUNKS = T // C
SEQ_CHUNKS = ((0, T_PROMPT // C), (T_PROMPT // C, T_SAMPLE // C))
Q_TILE, K_TILE, V_TILE, G_TILE = 0, 2, 4, 8
R_TILE, KR_TILE, VR_TILE = 12, 16, 20
DECAY_TILE, LOW_TILE, GATE_TILE = 24, 25, 26
MIX_TILES = 27
RWKV_GN_EPS = 64e-5
KK_EPS = 1e-12
LEVELS = 6
DECAY_UNIT = float(np.exp(-0.5))
G_COL = 5 * C
PACK = G_COL + 2 * (C + 1)
MEM_T = 512

VEC_NAMES = ("ln_ffn1_g", "ln_ffn1_b", "ln_mix_g", "ln_mix_b", "mem_ln_g", "mem_ln_b",
             "ln_ca_g", "ln_ca_b", "ln_ffn2_g", "ln_ffn2_b")
VEC = {n: KT * i for i, n in enumerate(VEC_NAMES)}
GLA_B = KT * len(VEC_NAMES)
GLA_G = GLA_B + 4
MU_TILES = 15
MU_PREV = GLA_G + 4
MU_NEXT = MU_PREV + MU_TILES
W0 = MU_NEXT + MU_TILES
A0, K_K, K_A, R_K, LNX_G, LNX_B = (W0 + 8 + 4 * i for i in range(6))


class Memory:

    def __init__(self, nc, ctx, tag):
        self.nc, self.ctx, self.tag, self.sems = nc, ctx, tag, []
        ctx.callback(self.clear_semaphores)

    def clear_semaphores(self):
        if self.sems:
            with self.nc.Block() as block:
                @block.sync
                def _(sp):
                    for s in self.sems:
                        sp.sem_clear(s)

    def sb(self, name, shape, dt=F32):
        return self.ctx.enter_context(self.nc.sbuf_tensor(f"{self.tag}_{name}", shape, dt))

    def psum(self):
        return self.ctx.enter_context(self.nc.psum_tensor(f"{self.tag}_psum", [P, 8 * BANK], F32))

    def sem(self, name):
        s = self.ctx.enter_context(self.nc.semaphore(f"{self.tag}_{name}"))
        self.sems.append(s)
        return s


def load_phase(nc, x_d, vec_d, x32, xh, xl, vecs):
    with ExitStack() as ctx:
        m = Memory(nc, ctx, "load")
        x_in = [m.sem(f"x_in{k}") for k in range(KT)]
        vec_in, high, low = m.sem("vec_in"), m.sem("high"), m.sem("low")
        block = ctx.enter_context(nc.Block())

        @block.sync
        def _(sp):
            for k in range(KT):
                sp.dma_start(x32[:, k, :], x_d[:, k, :]).then_inc(x_in[k], 16)
            sp.dma_start(vecs[:], vec_d).then_inc(vec_in, 16)
            sp.wait_ge(vec_in, 16)

        @block.scalar
        def _(act):
            for k in range(KT):
                act.wait_ge(x_in[k], 16)
                nc.scalar.copy(xh[:, k, :], x32[:, k, :]).then_inc(high, 1)

        @block.vector
        def _(dve):
            for k in range(KT):
                dve.wait_ge(high, k + 1)
                nc.vector.tensor_tensor(xl[:, k, :], x32[:, k, :], xh[:, k, :], ALU.subtract).then_inc(low, 1)
                dve.wait_ge(low, k + 1)
                nc.vector.tensor_scalar(x32[:, k, :], x32[:, k, :], 2 * ALPHA, None, ALU.mult)


def ffn_phase(nc, tag, w_in_d, w_out_d, xh, xl, acc):
    with ExitStack() as ctx:
        m = Memory(nc, ctx, tag)
        raw_in = m.sb("raw_in", [P, 2 * KT * P])
        raw_out = m.sb("raw_out", [P, D])
        wi_h = m.sb("wi_h", [P, 2, 2 * KT * P], F32R)
        wi_l = m.sb("wi_l", [P, 2, 2 * KT * P], F32R)
        wo_h = m.sb("wo_h", [P, 2, D], F32R)
        wo_l = m.sb("wo_l", [P, 2, D], F32R)
        hid = m.sb("hid", [P, T])
        hid_h = m.sb("hid_h", [P, T], F32R)
        hid_l = m.sb("hid_l", [P, T], F32R)
        ps = m.psum()
        gate_at, up_at, out_at = 0, 3 * BANK, 6 * BANK
        in_loaded, out_loaded = m.sem("in_loaded"), m.sem("out_loaded")
        wi_high, wi_split = m.sem("wi_high"), m.sem("wi_split")
        wo_high, wo_split = m.sem("wo_high"), m.sem("wo_split")
        gate_done, up_done, out_done = m.sem("gate_done"), m.sem("up_done"), m.sem("out_done")
        silu_done, hid_done, hid_high, hid_split = m.sem("silu_done"), m.sem("hid_done"), m.sem("hid_high"), m.sem("hid_split")
        added = m.sem("added")
        OUTS = KT * len(TOKEN_CHUNKS)
        WAIT_GROUPS = 4
        PER_GROUP = OUTS // (2 * KT - WAIT_GROUPS)
        block = ctx.enter_context(nc.Block())

        def pairs(engine, step):
            with engine.Fori(0, (FT - 2) // 2) as i:
                for u in (1, 2):
                    step(2 * i + u, u % 2)
            step(FT - 1, (FT - 1) % 2)

        @block.sync
        def _(sp):
            def load(f, first=False):
                if not first:
                    sp.wait_ge(wi_split, f)
                sp.dma_start(raw_in[:], w_in_d[f]).then_inc(in_loaded, 16)
                if not first:
                    sp.wait_ge(wo_split, f)
                sp.dma_start(raw_out[:], w_out_d[f]).then_inc(out_loaded, 16)

            load(0, first=True)
            with sp.Fori(1, FT) as f:
                load(f)

        @block.tensor
        def _(pe):
            def project(f, slot, n):
                g, k = n // KT, n % KT
                at, cols = (gate_at, up_at)[g], slice(n * P, (n + 1) * P)
                for j, (w, x) in enumerate(((wi_h, xh), (wi_h, xl), (wi_l, xh))):
                    for c, (t0, tn) in enumerate(TOKEN_CHUNKS):
                        mm = nc.tensor.matmul(ps[:, at + c * BANK:at + c * BANK + tn], w[:, slot, cols], x[:, k, t0:t0 + tn],
                                              start=(k == 0 and j == 0), stop=(k == KT - 1 and j == 2))
                if k == KT - 1:
                    mm.then_inc((gate_done, up_done)[g], 1)

            def expand(f, slot, s):
                o, (t0, tn) = s // 3, TOKEN_CHUNKS[s % 3]
                pe.wait_ge(added, OUTS * f + s + 1)
                at = out_at + s % 2 * BANK
                for j, (w, h) in enumerate(((wo_h, hid_h), (wo_h, hid_l), (wo_l, hid_h))):
                    mm = nc.tensor.matmul(ps[:, at:at + tn], w[:, slot, o * P:(o + 1) * P], h[:, t0:t0 + tn],
                                          start=(j == 0), stop=(j == 2))
                mm.then_inc(out_done, 1)

            def step(f, slot):
                pe.wait_ge(wi_split, f + 1)
                for n in range(2 * KT):
                    if n % KT == 0:
                        pe.wait_ge((silu_done, hid_done)[n // KT], f)
                    project(f, slot, n)
                    if n == WAIT_GROUPS:
                        pe.wait_ge(hid_split, f)
                        pe.wait_ge(wo_split, f)
                    if n >= WAIT_GROUPS:
                        for s in range((n - WAIT_GROUPS) * PER_GROUP, (n - WAIT_GROUPS + 1) * PER_GROUP):
                            expand(f - 1, 1 - slot, s)

            pe.wait_ge(wi_split, 1)
            for n in range(2 * KT):
                project(0, 0, n)
            pairs(pe, step)
            pe.wait_ge(hid_split, FT)
            for s in range(OUTS):
                expand(FT - 1, (FT - 1) % 2, s)

        @block.scalar
        def _(act):
            def split_in(f, slot):
                act.wait_ge(in_loaded, 16 * (f + 1))
                nc.scalar.copy(wi_h[:, slot, :], raw_in[:]).then_inc(wi_high, 1)

            def split_out(f, slot):
                act.wait_ge(out_loaded, 16 * (f + 1))
                nc.scalar.copy(wo_h[:, slot, :], raw_out[:]).then_inc(wo_high, 1)

            def activate(f):
                act.wait_ge(gate_done, f + 1)
                nc.scalar.activation(hid[:], ps[:, gate_at:gate_at + T], ACT.Silu).then_inc(silu_done, 1)

            def high_part(f):
                act.wait_ge(hid_done, f + 1)
                nc.scalar.copy(hid_h[:], hid[:]).then_inc(hid_high, 1)

            def step(f, slot, last=False):
                high_part(f - 1)
                if not last:
                    split_in(f + 1, 1 - slot)
                act.wait_ge(hid_split, f)
                split_out(f, slot)
                activate(f)
                act.wait_ge(out_done, OUTS * f)

            split_in(0, 0)
            split_out(0, 0)
            split_in(1, 1)
            activate(0)
            with act.Fori(0, (FT - 2) // 2) as i:
                for u in (1, 2):
                    step(2 * i + u, u % 2)
            step(FT - 1, (FT - 1) % 2, last=True)
            high_part(FT - 1)

        @block.vector
        def _(dve):
            def split_in(f, slot):
                dve.wait_ge(wi_high, f + 1)
                nc.vector.tensor_tensor(wi_l[:, slot, :], raw_in[:], wi_h[:, slot, :], ALU.subtract).then_inc(wi_split, 1)

            def split_out(f, slot):
                dve.wait_ge(wo_high, f + 1)
                nc.vector.tensor_tensor(wo_l[:, slot, :], raw_out[:], wo_h[:, slot, :], ALU.subtract).then_inc(wo_split, 1)

            def accumulate(f):
                for s in range(OUTS):
                    o, (t0, tn) = s // 3, TOKEN_CHUNKS[s % 3]
                    dve.wait_ge(out_done, OUTS * f + s + 1)
                    at = out_at + s % 2 * BANK
                    nc.vector.tensor_tensor(acc[:, o, t0:t0 + tn], acc[:, o, t0:t0 + tn], ps[:, at:at + tn],
                                            ALU.add).then_inc(added, 1)

            def hidden(f):
                dve.wait_ge(up_done, f + 1)
                dve.wait_ge(silu_done, f + 1)
                nc.vector.tensor_tensor(hid[:], hid[:], ps[:, up_at:up_at + T], ALU.mult).then_inc(hid_done, 1)
                dve.wait_ge(hid_high, f + 1)
                nc.vector.tensor_tensor(hid_l[:], hid[:], hid_h[:], ALU.subtract).then_inc(hid_split, 1)

            def step(f, slot, last=False):
                hidden(f - 1)
                if not last:
                    split_in(f + 1, 1 - slot)
                split_out(f, slot)
                accumulate(f - 1)

            dve.sem_inc(added, 2)
            split_in(0, 0)
            split_out(0, 0)
            split_in(1, 1)
            with dve.Fori(0, (FT - 2) // 2) as i:
                for u in (1, 2):
                    step(2 * i + u, u % 2)
            step(FT - 1, (FT - 1) % 2, last=True)
            hidden(FT - 1)
            accumulate(FT - 1)


def linear_phase(nc, tag, w_d, n_tiles, xh, xl, chunks, mode, dest, spill=None):
    tokens = sum(n for _, n in chunks)
    with ExitStack() as ctx:
        m = Memory(nc, ctx, tag)
        raw = m.sb("raw", [P, 2, KT * P])
        w_h = m.sb("w_h", [P, 2, KT * P], F32R)
        w_l = m.sb("w_l", [P, 2, KT * P], F32R)
        stage = m.sb("stage", [P, 2, tokens]) if mode == "store" else None
        ps = m.psum()
        loaded = [m.sem(f"loaded{u}") for u in range(2)]
        high, split, product, emptied = m.sem("high"), m.sem("split"), m.sem("product"), m.sem("emptied")
        stored, spilled = [m.sem(f"stored{u}") for u in range(2)], m.sem("spilled")
        block = ctx.enter_context(nc.Block())

        def steps(engine, step, last=n_tiles):
            step(0, 0, 0, True)
            step(1, 1, 0, True)
            with engine.Fori(1, last // 2) as i:
                step(2 * i, 0, i, False)
                step(2 * i + 1, 1, i, False)
            if last % 2:
                step(last - 1, 0, last // 2, False)

        @block.sync
        def _(sp):
            def move(n, u, half, first):
                if not first:
                    sp.wait_ge(split, n - 1)
                sp.dma_start(raw[:, u, :], w_d[n]).then_inc(loaded[u], 16)
                if spill is not None and first and u == 1:
                    sp.dma_start(spill[1], spill[0]).then_inc(spilled, 16)

            steps(sp, move)
            if spill is not None:
                sp.wait_ge(spilled, 16)

        @block.tensor
        def _(pe):
            def product_of(n, u, half, first):
                pe.wait_ge(split, n + 1)
                pe.wait_ge(emptied, n + 1)
                for k in range(KT):
                    for j, (w, x) in enumerate(((w_h, xh), (w_h, xl), (w_l, xh))):
                        for c, (t0, tn) in enumerate(chunks):
                            at = (3 * u + c) * BANK
                            mm = nc.tensor.matmul(ps[:, at:at + tn], w[:, u, k * P:(k + 1) * P], x[:, k, t0:t0 + tn],
                                                  start=(k == 0 and j == 0), stop=(k == KT - 1 and j == 2))
                mm.then_inc(product, 1)

            steps(pe, product_of)

        @block.scalar
        def _(act):
            def high_part(n, u, half):
                act.wait_ge(loaded[u], 16 * (half + 1))
                nc.scalar.copy(w_h[:, u, :], raw[:, u, :]).then_inc(high, 1)

            def empty(n, u, half, first):
                act.wait_ge(product, n + 1)
                if mode == "store":
                    if not first:
                        act.wait_ge(stored[u], 16 * half)
                    nc.scalar.copy(stage[:, u, :], ps[:, 3 * u * BANK:3 * u * BANK + tokens]).then_inc(emptied, 1)
                    act.wait_ge(emptied, n + 3)
                    act.dma_start(dest[n], stage[:, u, :]).then_inc(stored[u], 16)
                elif mode == "keep":
                    nc.scalar.copy(dest[:, n, :], ps[:, 3 * u * BANK:3 * u * BANK + tokens]).then_inc(emptied, 1)

            def step(n, u, half, first):
                empty(n, u, half, first)
                high_part(n + 2, u, half + 1)

            high_part(0, 0, 0)
            high_part(1, 1, 0)
            steps(act, step, n_tiles - 2)
            empty(n_tiles - 2, n_tiles % 2, (n_tiles - 2) // 2, False)
            empty(n_tiles - 1, (n_tiles - 1) % 2, (n_tiles - 1) // 2, False)
            if mode == "store":
                act.wait_ge(stored[0], 16 * ((n_tiles + 1) // 2))
                act.wait_ge(stored[1], 16 * (n_tiles // 2))

        @block.vector
        def _(dve):
            dve.sem_inc(emptied, 2)

            def low_part(n, u, half, first=False):
                dve.wait_ge(high, n + 1)
                nc.vector.tensor_tensor(w_l[:, u, :], raw[:, u, :], w_h[:, u, :], ALU.subtract).then_inc(split, 1)

            def add(n, u, half, first):
                dve.wait_ge(product, n + 1)
                nc.vector.tensor_tensor(dest[:, n, :], dest[:, n, :], ps[:, 3 * u * BANK:3 * u * BANK + tokens],
                                        ALU.add).then_inc(emptied, 1)

            def step(n, u, half, first):
                low_part(n, u, half)
                if mode == "add":
                    add(n, u, half, first)

            steps(dve, step)


def norm_phase(nc, tag, acc, ones, vecs, gain, bias, tokens=T, scale=1.0, xh=None, xl=None, after=1.0, out_d=None):
    steps = tokens // NT
    with ExitStack() as ctx:
        m = Memory(nc, ctx, tag)
        squares = m.sb("squares", [P, 2, KT, NT])
        rstd = m.sb("rstd", [P, 2, NT])
        consts = m.sb("consts", [P, 2])
        ps = m.psum()
        mean_done, centred, squared, var_done = m.sem("mean_done"), m.sem("centred"), m.sem("squared"), m.sem("var_done")
        log_done, rstd_done, scaled, affine_a, affine_v = m.sem("log_done"), m.sem("rstd_done"), m.sem("scaled"), m.sem("affine_a"), m.sem("affine_v")
        high, low, const_set, stored = m.sem("high"), m.sem("low"), m.sem("const_set"), m.sem("stored")
        HALF = KT // 2
        block = ctx.enter_context(nc.Block())

        def tok(s):
            return slice(s * NT, (s + 1) * NT)

        def mean_ps(s):
            return ps[:, s % 2 * BANK:s % 2 * BANK + NT]

        def var_ps(s):
            return ps[:, (2 + s % 2) * BANK:(2 + s % 2) * BANK + NT]

        @block.tensor
        def _(pe):
            def mean(s):
                if s >= 2:
                    pe.wait_ge(centred, s - 1)
                for k in range(KT):
                    mm = nc.tensor.matmul(mean_ps(s), ones[:], acc[:, k, tok(s)], start=(k == 0), stop=(k == KT - 1))
                mm.then_inc(mean_done, 1)

            mean(0)
            for s in range(steps):
                if s + 1 < steps:
                    mean(s + 1)
                pe.wait_ge(squared, s + 1)
                if s >= 2:
                    pe.wait_ge(log_done, s - 1)
                for k in range(KT):
                    mm = nc.tensor.matmul(var_ps(s), ones[:], squares[:, s % 2, k, :], start=(k == 0), stop=(k == KT - 1))
                mm.then_inc(var_done, 1)

        @block.vector
        def _(dve):
            nc.vector.memset(consts[:, 0:1], LN_EPS).then_inc(const_set, 1)
            nc.vector.memset(consts[:, 1:2], float(np.log(scale))).then_inc(const_set, 1)

            def centre(s):
                dve.wait_ge(mean_done, s + 1)
                nc.vector.tensor_tensor(acc[:, :, tok(s)], acc[:, :, tok(s)],
                                        mean_ps(s).unsqueeze(1).broadcast_to([P, KT, NT]), ALU.subtract).then_inc(centred, 1)

            def normalise(s):
                dve.wait_ge(rstd_done, s + 1)
                dve.wait_ge(squared, s + 1)
                nc.vector.tensor_tensor(acc[:, :, tok(s)], acc[:, :, tok(s)],
                                        rstd[:, s % 2, :].unsqueeze(1).broadcast_to([P, KT, NT]), ALU.mult).then_inc(scaled, 1)
                dve.wait_ge(scaled, s + 1)
                for k in range(HALF, KT):
                    nc.vector.tensor_scalar(acc[:, k, tok(s)], acc[:, k, tok(s)], vecs[:, gain + k:gain + k + 1],
                                            vecs[:, bias + k:bias + k + 1], ALU.mult, ALU.add).then_inc(affine_v, 1)

            def finish(s):
                dve.wait_ge(low, s + 1)
                dve.wait_ge(high, s + 1)
                if after != 1.0:
                    nc.vector.tensor_scalar(acc[:, :, tok(s)], acc[:, :, tok(s)], after, None, ALU.mult)

            centre(0)
            for s in range(steps):
                if s + 1 < steps:
                    centre(s + 1)
                normalise(s)
                if s >= 1 and out_d is None:
                    finish(s - 1)
            if out_d is None:
                finish(steps - 1)

        @block.scalar
        def _(act):
            act.wait_ge(const_set, 2)

            def square(s):
                act.wait_ge(centred, s + 1)
                if s >= 2:
                    act.wait_ge(var_done, s - 1)
                nc.scalar.activation(squares[:, s % 2], acc[:, :, tok(s)], ACT.Square).then_inc(squared, 1)

            square(0)
            for s in range(steps):
                act.wait_ge(var_done, s + 1)
                if s >= 2:
                    act.wait_ge(scaled, s - 1)
                nc.scalar.activation(rstd[:, s % 2, :], var_ps(s), ACT.Ln, bias=consts[:, 0:1],
                                     scale=scale * scale).then_inc(log_done, 1)
                act.wait_ge(log_done, s + 1)
                nc.scalar.activation(rstd[:, s % 2, :], rstd[:, s % 2, :], ACT.Exp, bias=consts[:, 1:2],
                                     scale=-0.5).then_inc(rstd_done, 1)
                if s + 1 < steps:
                    square(s + 1)
                act.wait_ge(scaled, s + 1)
                for k in range(HALF):
                    nc.scalar.activation(acc[:, k, tok(s)], acc[:, k, tok(s)], ACT.Identity,
                                         bias=vecs[:, bias + k:bias + k + 1],
                                         scale=vecs[:, gain + k:gain + k + 1]).then_inc(affine_a, 1)
                if out_d is None:
                    act.wait_ge(affine_v, HALF * (s + 1))
                    act.wait_ge(affine_a, HALF * (s + 1))
                    nc.scalar.copy(xh[:, :, tok(s)], acc[:, :, tok(s)]).then_inc(high, 1)

        if out_d is None:
            @block.gpsimd
            def _(pool):
                for s in range(steps):
                    pool.wait_ge(high, s + 1)
                    nc.gpsimd.tensor_tensor(xl[:, :, tok(s)], acc[:, :, tok(s)], xh[:, :, tok(s)],
                                            ALU.subtract).then_inc(low, 1)
        else:
            @block.sync
            def _(sp):
                for s in range(steps):
                    sp.wait_ge(affine_a, HALF * (s + 1))
                    sp.wait_ge(affine_v, HALF * (s + 1))
                    sp.dma_start(out_d[:, :, tok(s)], acc[:, :, tok(s)]).then_inc(stored, 16)
                sp.wait_ge(stored, 16 * steps)


def gla_prepare_phase(nc, a, proj_d, vecs, v, q_in, k_in, q_st, k_out, decay):
    with ExitStack() as ctx:
        m = Memory(nc, ctx, "glap")
        q, k = m.sb("q", [P, 2, T]), m.sb("k", [P, 2, T])
        low = m.sb("low", [P, T])
        up = m.sb("up", [P, 4 * P])
        keep = m.sb("keep", [P, T])
        b1, b2, run = m.sb("b1", [P, T]), m.sb("b2", [P, T]), m.sb("run", [P, T])
        e = [m.sb(f"e{i}", [P, T]) for i in range(2)] + [run, b2]
        ps = m.psum()
        loaded, v_loaded, logit = m.sem("loaded"), m.sem("v_loaded"), m.sem("logit")
        split, soft, summed, centred, expd = m.sem("split"), m.sem("soft"), m.sem("summed"), m.sem("centred"), m.sem("expd")
        done_v, done_p, step_v, step_a, scaled = m.sem("done_v"), m.sem("done_p"), m.sem("step_v"), m.sem("step_a"), m.sem("scaled")
        units = [(d, t) for d in range(2) for t in range(2)]
        block = ctx.enter_context(nc.Block())

        @block.sync
        def _(sp):
            loads = [(low, proj_d[LOW_TILE]), (up, a["gla_up"]), (keep, a["keep"])]
            loads += [(q[:, t], proj_d[Q_TILE + t]) for t in range(2)] + [(k[:, t], proj_d[K_TILE + t]) for t in range(2)]
            for dst, src in loads:
                sp.dma_start(dst if isinstance(dst, bass.AP) else dst[:], src).then_inc(loaded, 16)
            for t in range(4):
                sp.dma_start(v[:, t], proj_d[V_TILE + t]).then_inc(v_loaded, 16)
            sp.wait_ge(v_loaded, 64)

        @block.tensor
        def _(pe):
            pe.wait_ge(loaded, 16 * 7)
            for n, (d, t) in enumerate(units):
                if n >= 2:
                    pe.wait_ge(step_a, 2 * n - 3)
                for c, (t0, tn) in enumerate(TOKEN_CHUNKS):
                    at = (3 * (n % 2) + c) * BANK
                    mm = nc.tensor.matmul(ps[:, at:at + tn], up[:, (2 * d + t) * P:(2 * d + t + 1) * P],
                                          low[:, t0:t0 + tn], start=True, stop=True)
                mm.then_inc(logit, 1)

        @block.vector
        def _(dve):
            dve.wait_ge(loaded, 16 * 7)
            nc.vector.tensor_scalar(q[:], q[:], GLA_DK ** -0.5, None, ALU.mult).then_inc(scaled, 1)
            dve.wait_ge(scaled, 1)
            for n, (d, t) in enumerate(units):
                bias = vecs[:, GLA_B + 2 * d + t:GLA_B + 2 * d + t + 1]
                z = ps[:, 3 * (n % 2) * BANK:3 * (n % 2) * BANK + T]
                dve.wait_ge(logit, n + 1)
                if n >= 1:
                    dve.wait_ge(expd, 4 * n)
                    dve.wait_ge(done_p, 2 * n)
                    dve.wait_ge(done_v, 2 * n)
                nc.vector.tensor_scalar(b2[:], z, bias, 0.0, ALU.add, ALU.min).then_inc(split, 1)
                dve.wait_ge(soft, n + 1)
                dve.wait_ge(split, n + 1)
                nc.vector.tensor_tensor(b2[:], b2[:], b1[:], ALU.subtract).then_inc(step_v, 1)
                dve.wait_ge(step_v, 3 * n + 1)
                if d == 0:
                    nc.vector.tensor_tensor_scan(run[:], keep[:], b2[:], 0.0, ALU.mult, ALU.add).then_inc(summed, 1)
                else:
                    nc.vector.tensor_tensor_scan(run[:, ::-1], keep[:], b2[:, ::-1], 0.0, ALU.mult, ALU.add).then_inc(summed, 1)
                dve.wait_ge(summed, n + 1)
                chunks = run[:].rearrange("p (c t) -> p c t", t=C)
                end = C - 1 if d == 0 else 0
                last = chunks[:, :, end:end + 1].broadcast_to([P, N_CHUNKS, C])
                nc.vector.scalar_tensor_tensor(b1[:].rearrange("p (c t) -> p c t", t=C), last, -0.5, chunks,
                                               ALU.mult, ALU.add).then_inc(step_v, 1)
                nc.vector.tensor_tensor(b2[:].rearrange("p (c t) -> p c t", t=C), last, chunks,
                                        ALU.subtract).then_inc(step_v, 1)
                dve.wait_ge(expd, 4 * n + 3)
                nc.vector.tensor_tensor(q_in[d][:, t], q[:, t], e[0][:], ALU.mult).then_inc(done_v, 1)
                nc.vector.tensor_tensor(q_st[d][:, t], q[:, t], e[2][:], ALU.mult).then_inc(done_v, 1)

        @block.gpsimd
        def _(pool):
            pool.wait_ge(loaded, 16 * 7)
            for n, (d, t) in enumerate(units):
                pool.wait_ge(expd, 4 * n + 4)
                nc.gpsimd.tensor_tensor(k_in[d][:, t], k[:, t], e[1][:], ALU.mult).then_inc(done_p, 1)
                nc.gpsimd.tensor_tensor(k_out[d][:, t], k[:, t], e[3][:], ALU.mult).then_inc(done_p, 1)

        @block.scalar
        def _(act):
            for n, (d, t) in enumerate(units):
                end = C - 1 if d == 0 else 0
                act.wait_ge(split, n + 1)
                nc.scalar.activation(b1[:], ps[:, 3 * (n % 2) * BANK:3 * (n % 2) * BANK + T], ACT.Abs,
                                     bias=vecs[:, GLA_B + 2 * d + t:GLA_B + 2 * d + t + 1]).then_inc(step_a, 1)
                act.wait_ge(step_a, 2 * n + 1)
                nc.scalar.activation(b1[:], b1[:], ACT.Exp, scale=-1.0).then_inc(step_a, 1)
                act.wait_ge(step_a, 2 * n + 2)
                nc.scalar.activation(b1[:], b1[:], ACT.Ln, bias=1.0).then_inc(soft, 1)
                act.wait_ge(step_v, 3 * n + 3)
                if n >= 1:
                    act.wait_ge(done_v, 2 * n)
                    act.wait_ge(done_p, 2 * n)
                act.wait_ge(summed, n + 1)
                nc.scalar.activation(decay[d][:, t], run[:].rearrange("p (c t) -> p c t", t=C)[:, :, end],
                                     ACT.Exp, scale=1 / GLA_TAU)
                nc.scalar.activation(e[0][:], b1[:], ACT.Exp, scale=1 / GLA_TAU).then_inc(expd, 1)
                nc.scalar.activation(e[1][:], b1[:], ACT.Exp, scale=-1 / GLA_TAU).then_inc(expd, 1)
                act.wait_ge(expd, 4 * n + 1)
                nc.scalar.activation(e[2][:], run[:], ACT.Exp, scale=1 / GLA_TAU).then_inc(expd, 1)
                nc.scalar.activation(e[3][:], b2[:], ACT.Exp, scale=1 / GLA_TAU).then_inc(expd, 1)


def gla_scan_phase(nc, v, q_in, k_in, q_st, k_out, decay, out, consts):
    with ExitStack() as ctx:
        m = Memory(nc, ctx, "glas")
        per_dir = lambda name, shape: [m.sb(f"{name}{d}", shape) for d in range(2)]
        k_pair, qs_pair, s_pair = per_dir("k_pair", [P, 2, 2, C]), per_dir("qs_pair", [P, 2, 2, C]), per_dir("s_pair", [P, 2, 2, C])
        q_now = per_dir("q_now", [P, 2, C])
        v_now, ko_pair = per_dir("v_now", [P, 4, C]), per_dir("ko_pair", [P, 2, 2, C])
        v_rows, kt_pair = per_dir("v_rows", [P, 2, P]), per_dir("kt_pair", [P, 2, 2, C])
        state = per_dir("state", [P, 2, P])
        mark = m.sb("mark", [P, 2])
        ps = m.psum()
        ident, pair_mask = consts["ident"], consts["pair"]
        bank = lambda d, i: ps[:, (4 * d + i) * BANK:(4 * d + i + 1) * BANK]
        V_AT, K_AT, S_AT, O_AT = range(4)
        each = lambda name: [m.sem(f"{name}{d}") for d in range(2)]
        zeroed, paired, staged, turned_v, turned_k, rows_v, rows_k = m.sem("zeroed"), each("paired"), each("staged"), each("turned_v"), each("turned_k"), each("rows_v"), each("rows_k")
        scored, masked, outed, added, taken, updated = each("scored"), each("masked"), each("outed"), each("added"), each("taken"), each("updated")
        cleared, out_zeroed = m.sem("cleared"), m.sem("out_zeroed")
        block = ctx.enter_context(nc.Block())

        def sequences(engine, step, start=None):
            for s, (c0, cn) in enumerate(SEQ_CHUNKS):
                if start is not None:
                    start(s, c0)
                step(c0, (c0, c0 + cn - 1), c0 == 0)
                with engine.Fori(1, cn) as i:
                    step(i + c0, (i + c0, i * -1 + (c0 + cn - 1)), False)

        @block.gpsimd
        def _(pool):
            for d in range(2):
                nc.gpsimd.memset(s_pair[d][:], 0.0).then_inc(zeroed, 1)

            def stage(n, chunk, first):
                for d in range(2):
                    at = bass.ds(chunk[d] * C, C)
                    mask = pair_mask.unsqueeze(1).broadcast_to([P, 2, 2, C])
                    if not first:
                        pool.wait_ge(rows_k[d], n)
                    nc.gpsimd.tensor_copy(v_now[d][:], v[:, :, at]).then_inc(staged[d], 1)
                    nc.gpsimd.tensor_tensor(ko_pair[d][:], k_out[d][:, :, at].unsqueeze(2).broadcast_to([P, 2, 2, C]),
                                            mask, ALU.mult).then_inc(staged[d], 1)
                    if not first:
                        pool.wait_ge(outed[d], n)
                    nc.gpsimd.tensor_copy(q_now[d][:], q_in[d][:, :, at]).then_inc(staged[d], 1)

            sequences(pool, stage)

        @block.tensor
        def _(pe):
            def work(n, chunk, first):
                for d in range(2):
                    pe.wait_ge(staged[d], 3 * n + 2)
                    if not first:
                        pe.wait_ge(updated[d], 2 * n)
                    for p in range(2):
                        mm = nc.tensor.transpose(bank(d, V_AT)[:, p * P:(p + 1) * P],
                                                 v_now[d][:, 2 * p:2 * p + 2].rearrange("p a t -> p (a t)"), ident)
                    mm.then_inc(turned_v[d], 1)
                    for p in range(2):
                        mm = nc.tensor.transpose(bank(d, K_AT)[:, p * P:(p + 1) * P],
                                                 ko_pair[d][:, p].rearrange("p a t -> p (a t)"), ident)
                    mm.then_inc(turned_k[d], 1)
                for d in range(2):
                    pe.wait_ge(staged[d], 3 * n + 3)
                    pe.wait_ge(paired[d], 2 * n + 2)
                    if not first:
                        pe.wait_ge(masked[d], n)
                    for p in range(2):
                        mm = nc.tensor.matmul(bank(d, S_AT)[:, p * C:(p + 1) * C],
                                              k_pair[d][:, p].rearrange("p a t -> p (a t)"), q_now[d][:, p], start=True, stop=True)
                    mm.then_inc(scored[d], 1)
                for d in range(2):
                    pe.wait_ge(rows_v[d], n + 1)
                    pe.wait_ge(rows_k[d], n + 1)
                    for p in range(2):
                        mm = nc.tensor.matmul(bank(d, V_AT)[:, p * P:(p + 1) * P],
                                              kt_pair[d][:, p].rearrange("p a t -> p (a t)"), v_rows[d][:, p], start=True, stop=True)
                    mm.then_inc(taken[d], 1)
                for d in range(2):
                    pe.wait_ge(masked[d], n + 1)
                    if first:
                        pe.wait_ge(cleared, 2)
                    else:
                        pe.wait_ge(added[d], n)
                        pe.wait_ge(updated[d], 2 * n)
                        pe.wait_ge(cleared, 2)
                    for h in range(4):
                        o = bank(d, O_AT)[:, h * C:(h + 1) * C]
                        nc.tensor.matmul(o, v_rows[d][:, h // 2], s_pair[d][:, h // 2, h % 2], start=True, stop=False)
                        mm = nc.tensor.matmul(o, state[d][:, h // 2], qs_pair[d][:, h // 2, h % 2], start=False, stop=True)
                    mm.then_inc(outed[d], 1)

            def start(s, c0):
                pe.wait_ge(cleared, 2 * s + 2)

            sequences(pe, work, start)

        @block.scalar
        def _(act):
            def rows(n, chunk, first):
                for d in range(2):
                    act.wait_ge(turned_v[d], n + 1)
                    if not first:
                        act.wait_ge(outed[d], n)
                    nc.scalar.copy(v_rows[d][:], bank(d, V_AT)[:, 0:2 * P].rearrange("p (q e) -> p q e", e=P)).then_inc(rows_v[d], 1)
                    act.wait_ge(turned_k[d], n + 1)
                    nc.scalar.copy(kt_pair[d][:], bank(d, K_AT)[:, 0:2 * P].rearrange("p (q h e) -> p q h e", h=2, e=C)).then_inc(rows_k[d], 1)

            sequences(act, rows)

        @block.vector
        def _(dve):
            dve.wait_ge(zeroed, 2)
            nc.vector.memset(out[:], 0.0).then_inc(out_zeroed, 1)
            dve.wait_ge(out_zeroed, 1)

            def start(s, c0):
                for d in range(2):
                    if s:
                        dve.wait_ge(updated[d], 2 * c0)
                        dve.wait_ge(outed[d], c0)
                    nc.vector.memset(state[d][:], 0.0).then_inc(cleared, 1)
                dve.wait_ge(cleared, 2 * s + 2)

            def work(n, chunk, first):
                for d in range(2):
                    at = bass.ds(chunk[d] * C, C)
                    mask = pair_mask.unsqueeze(1).broadcast_to([P, 2, 2, C])
                    if not first:
                        dve.wait_ge(outed[d], n)
                    nc.vector.tensor_tensor(k_pair[d][:], k_in[d][:, :, at].unsqueeze(2).broadcast_to([P, 2, 2, C]),
                                            mask, ALU.mult).then_inc(paired[d], 1)
                    nc.vector.tensor_tensor(qs_pair[d][:], q_st[d][:, :, at].unsqueeze(2).broadcast_to([P, 2, 2, C]),
                                            mask, ALU.mult).then_inc(paired[d], 1)
                for d in range(2):
                    dve.wait_ge(scored[d], n + 1)
                    if not first:
                        dve.wait_ge(outed[d], n)
                        dve.wait_ge(masked[d], n)
                    nc.vector.memset(mark[:, d:d + 1], 0.0)
                    causal = consts["causal"][:, 2 * d * C:2 * (d + 1) * C].rearrange("p (a t) -> p a t", t=C).bitcast(U32)
                    for p in range(2):
                        mk = nc.vector.copy_predicated(
                            s_pair[d][:, p], causal,
                            bank(d, S_AT)[:, p * C:(p + 1) * C].unsqueeze(1).broadcast_to([P, 2, C]))
                    mk.then_inc(masked[d], 1)
                for d in range(2):
                    dve.wait_ge(outed[d], n + 1)
                    at = bass.ds(chunk[d] * C, C)
                    if not first:
                        dve.wait_ge(added[1 - d], n)
                    nc.vector.tensor_tensor(out[:, :, at], out[:, :, at],
                                            bank(d, O_AT)[:, 0:4 * C].rearrange("p (h t) -> p h t", t=C), ALU.add).then_inc(added[d], 1)
                    dve.wait_ge(taken[d], n + 1)
                    for p in range(2):
                        nc.vector.scalar_tensor_tensor(state[d][:, p], state[d][:, p], decay[d][:, p, bass.ds(chunk[d], 1)],
                                                       bank(d, V_AT)[:, p * P:(p + 1) * P], ALU.mult, ALU.add).then_inc(updated[d], 1)

            sequences(dve, work, start)


def gla_finish_phase(nc, proj_d, vecs, out, consts):
    with ExitStack() as ctx:
        m = Memory(nc, ctx, "glaf")
        g, sq, rstd = m.sb("g", [P, 4, T]), m.sb("sq", [P, 2, T]), m.sb("rstd", [P, 2, T])
        eps = m.sb("eps", [P, 1])
        ps = m.psum()
        loaded, squared, summed, logged, rooted, gated, eps_set = m.sem("loaded"), m.sem("squared"), m.sem("summed"), m.sem("logged"), m.sem("rooted"), m.sem("gated"), m.sem("eps_set")
        silued, done = m.sem("silued"), m.sem("done")
        block = ctx.enter_context(nc.Block())

        @block.sync
        def _(sp):
            sp.dma_start(g[:], proj_d[G_TILE:G_TILE + 4].rearrange("n p t -> p n t")).then_inc(loaded, 16)

        @block.tensor
        def _(pe):
            for h in range(4):
                pe.wait_ge(squared, h + 1)
                if h >= 2:
                    pe.wait_ge(logged, h - 1)
                for c, (t0, tn) in enumerate(TOKEN_CHUNKS):
                    at = (3 * (h % 2) + c) * BANK
                    mm = nc.tensor.matmul(ps[:, at:at + tn], consts["ones"], sq[:, h % 2, t0:t0 + tn], start=True, stop=True)
                mm.then_inc(summed, 1)

        @block.scalar
        def _(act):
            act.wait_ge(loaded, 16)
            nc.scalar.activation(g[:], g[:], ACT.Silu).then_inc(silued, 1)
            act.wait_ge(eps_set, 1)
            for h in range(4):
                if h >= 2:
                    act.wait_ge(summed, h - 1)
                nc.scalar.activation(sq[:, h % 2], out[:, h], ACT.Square).then_inc(squared, 1)
                act.wait_ge(summed, h + 1)
                if h >= 2:
                    act.wait_ge(done, h - 1)
                nc.scalar.activation(rstd[:, h % 2], ps[:, 3 * (h % 2) * BANK:3 * (h % 2) * BANK + T], ACT.Ln,
                                     bias=eps[:], scale=1 / GLA_DV).then_inc(logged, 1)
                act.wait_ge(logged, h + 1)
                nc.scalar.activation(rstd[:, h % 2], rstd[:, h % 2], ACT.Exp, scale=-0.5).then_inc(rooted, 1)

        @block.vector
        def _(dve):
            nc.vector.memset(eps[:], LN_EPS).then_inc(eps_set, 1)
            dve.wait_ge(silued, 1)
            for h in range(4):
                nc.vector.tensor_scalar(g[:, h], g[:, h], vecs[:, GLA_G + h:GLA_G + h + 1], None, ALU.mult).then_inc(gated, 1)
            for h in range(4):
                dve.wait_ge(squared, h + 1)
                dve.wait_ge(gated, 4 + h)
                nc.vector.tensor_tensor(out[:, h], out[:, h], g[:, h], ALU.mult).then_inc(gated, 1)
                dve.wait_ge(gated, 5 + h)
                dve.wait_ge(rooted, h + 1)
                nc.vector.tensor_tensor(out[:, h], out[:, h], rstd[:, h % 2], ALU.mult).then_inc(done, 1)


def rwkv_prepare_phase(nc, a, proj_d, pack_d, vecs, bonus, gate, consts):
    with ExitStack() as ctx:
        m = Memory(nc, ctx, "rwp")
        raw = m.sb("raw", [P, 3, T])
        r, kr, vr = (m.sb(n, [P, T]) for n in ("r", "kr", "vr"))
        decay = m.sb("decay", [P, 2, T])
        aa, kk = m.sb("aa", [P, T]), m.sb("kk", [P, T])
        low = m.sb("low", [P, 3, T])
        lora, keep = m.sb("lora", [P, 4 * P]), m.sb("keep", [P, T])
        pack = m.sb("pack", [P, N_CHUNKS, PACK])
        stay, one_less = m.sb("stay", [P, MU_TILES]), m.sb("one_less", [P, 4])
        ps = m.psum()
        sets = [ps[:, 0:T], ps[:, 3 * BANK:3 * BANK + T]]
        small_in, loaded, lora_in, stored = m.sem("small_in"), m.sem("loaded"), m.sem("lora_in"), m.sem("stored")
        coef, low_scaled, low_ready = m.sem("coef"), m.sem("low_scaled"), m.sem("low_ready")
        scaled, prev_added, next_added = m.sem("scaled"), m.sem("prev_added"), m.sem("next_added")
        logits, sig_done, gate_done, copied = m.sem("logits"), m.sem("sig_done"), m.sem("gate_done"), m.sem("copied")
        scanned, centred, kk_raw, squared, kk_summed, rooted = (
            m.sem(n) for n in ("scanned", "centred", "kk_raw", "squared", "kk_summed", "rooted"))
        k_factor, k_packed, clamped, inverted, kk_packed, b_packed = (
            m.sem(n) for n in ("k_factor", "k_packed", "clamped", "inverted", "kk_packed", "b_packed"))
        rk_done, rk_summed, kept = m.sem("rk_done"), m.sem("rk_summed"), m.sem("kept")
        block = ctx.enter_context(nc.Block())
        view = lambda ap: ap.rearrange("p (c t) -> p c t", t=C)
        part = lambda i: pack[:, :, i * C:(i + 1) * C]
        SEQS = ((0, T_PROMPT), (T_PROMPT, T))

        @block.sync
        def _(sp):
            for j, tile in enumerate((DECAY_TILE, LOW_TILE, GATE_TILE)):
                sp.dma_start(raw[:, j], proj_d[tile]).then_inc(small_in, 16)
            sp.dma_start(keep[:], a["keep"]).then_inc(small_in, 16)
            for t in range(4):
                if t:
                    sp.wait_ge(logits, 4 * t)
                sp.dma_start(lora[:], a["lora"][t]).then_inc(lora_in, 16)
                if t == 0:
                    sp.wait_ge(next_added, 6)
                else:
                    sp.wait_ge(kept, t)
                for j, tile in enumerate((R_TILE, KR_TILE, VR_TILE)):
                    sp.dma_start(raw[:, j], proj_d[tile + t]).then_inc(loaded, 16)
                sp.wait_ge(copied, 2 * (t + 1))
                sp.wait_ge(centred, 4 * (t + 1))
                sp.wait_ge(b_packed, t + 1)
                sp.dma_start(pack_d[:, :, t].rearrange("c p w -> p c w"), pack[:]).then_inc(stored, 16)
            sp.wait_ge(stored, 64)

        @block.tensor
        def _(pe):
            pe.wait_ge(low_ready, 2)
            pe.wait_ge(next_added, 6)
            for t in range(4):
                pe.wait_ge(lora_in, 16 * (t + 1))
                if t:
                    pe.wait_ge(kept, t)
                for j, src in enumerate((0, 0, 1, 2)):
                    if j >= 2:
                        pe.wait_ge(sig_done, 3 * t + j - 1)
                    for t0, tn in TOKEN_CHUNKS:
                        mm = nc.tensor.matmul(sets[j % 2][:, t0:t0 + tn], lora[:, j * P:(j + 1) * P], low[:, src, t0:t0 + tn],
                                              start=True, stop=True)
                    mm.then_inc(logits, 1)
                pe.wait_ge(squared, t + 1)
                pe.wait_ge(sig_done, 3 * t + 3)
                for t0, tn in TOKEN_CHUNKS:
                    mm = nc.tensor.matmul(sets[0][:, t0:t0 + tn], consts["head_ones"], decay[:, 0, t0:t0 + tn], start=True, stop=True)
                mm.then_inc(kk_summed, 1)
                pe.wait_ge(rk_done, t + 1)
                pe.wait_ge(gate_done, t + 1)
                for t0, tn in TOKEN_CHUNKS:
                    mm = nc.tensor.matmul(sets[1][:, t0:t0 + tn], consts["head_ones"], decay[:, 1, t0:t0 + tn], start=True, stop=True)
                mm.then_inc(rk_summed, 1)

        @block.scalar
        def _(act):
            act.wait_ge(small_in, 64)
            act.wait_ge(coef, 3)
            for j in range(3):
                nc.scalar.activation(low[:, j], raw[:, j], ACT.Copy, scale=stay[:, 12 + j:13 + j]).then_inc(low_scaled, 1)
            act.wait_ge(next_added, 6)
            nc.scalar.activation(low[:, 0], low[:, 0], ACT.Tanh).then_inc(low_ready, 1)
            nc.scalar.activation(low[:, 2], low[:, 2], ACT.Sigmoid).then_inc(low_ready, 1)
            for t in range(4):
                act.wait_ge(loaded, 48 * (t + 1))
                if t:
                    act.wait_ge(kept, t)
                for j, dst in enumerate((r, kr, vr)):
                    nc.scalar.activation(dst[:], raw[:, j], ACT.Copy, scale=stay[:, 4 * j + t:4 * j + t + 1]).then_inc(scaled, 1)
                for j in range(3):
                    act.wait_ge(logits, 4 * t + j + 1)
                    dst = aa[:] if j == 2 else decay[:, j]
                    bias = A0 + t if j == 2 else W0 + 4 * j + t
                    nc.scalar.activation(dst, sets[j % 2], ACT.Sigmoid, bias=vecs[:, bias:bias + 1]).then_inc(sig_done, 1)
                act.wait_ge(logits, 4 * t + 4)
                nc.scalar.copy(gate[:, t], sets[1]).then_inc(gate_done, 1)
                act.wait_ge(next_added, 6 * (t + 2))
                if t:
                    act.wait_ge(stored, 16 * t)
                nc.scalar.copy(part(0), view(r[:])).then_inc(copied, 1)
                nc.scalar.copy(part(2), view(vr[:])).then_inc(copied, 1)
                act.wait_ge(kk_raw, t + 1)
                act.wait_ge(scanned, 2 * t + 1)
                nc.scalar.activation(decay[:, 0], kk[:], ACT.Square).then_inc(squared, 1)
                act.wait_ge(kk_summed, t + 1)
                nc.scalar.activation(raw[:, 1], sets[0], ACT.Sqrt).then_inc(rooted, 1)

        @block.vector
        def _(dve):
            nc.vector.tensor_tensor(stay[:], vecs[:, MU_PREV:MU_PREV + MU_TILES], vecs[:, MU_NEXT:MU_NEXT + MU_TILES], ALU.add).then_inc(coef, 1)
            nc.vector.tensor_scalar(one_less[:], vecs[:, K_A:K_A + 4], -1.0, 1.0, ALU.mult, ALU.add).then_inc(coef, 1)
            dve.wait_ge(coef, 2)
            nc.vector.tensor_scalar(stay[:], stay[:], -1.0, 1.0, ALU.mult, ALU.add).then_inc(coef, 1)

            def shift(dst, src, col, count):
                for s0, s1 in SEQS:
                    nc.vector.scalar_tensor_tensor(dst[:, s0 + 1:s1], src[:, s0:s1 - 1], vecs[:, MU_PREV + col:MU_PREV + col + 1],
                                                   dst[:, s0 + 1:s1], ALU.mult, ALU.add).then_inc(prev_added, 1)
                dve.wait_ge(prev_added, 2 * (count + 1))
                for s0, s1 in SEQS:
                    nc.vector.scalar_tensor_tensor(dst[:, s0:s1 - 1], src[:, s0 + 1:s1], vecs[:, MU_NEXT + col:MU_NEXT + col + 1],
                                                   dst[:, s0:s1 - 1], ALU.mult, ALU.add).then_inc(next_added, 1)

            dve.wait_ge(small_in, 64)
            for j in range(3):
                dve.wait_ge(low_scaled, j + 1)
                shift(low[:, j], raw[:, j], 12 + j, j)
            for t in range(4):
                dve.wait_ge(loaded, 48 * (t + 1))
                for j, dst in enumerate((r, kr, vr)):
                    dve.wait_ge(scaled, 3 * t + j + 1)
                    shift(dst[:], raw[:, j], 4 * j + t, 3 * (t + 1) + j)
                dve.wait_ge(next_added, 6 * (t + 2))
                run = raw[:, 0]
                for d in range(2):
                    dve.wait_ge(sig_done, 3 * t + d + 1)
                    if d == 0:
                        nc.vector.tensor_tensor_scan(run, keep[:], decay[:, 0], 0.0, ALU.mult, ALU.add).then_inc(scanned, 1)
                    else:
                        dve.wait_ge(centred, 4 * t + 2)
                        nc.vector.tensor_tensor_scan(run[:, ::-1], keep[:], decay[:, 1, ::-1], 0.0, ALU.mult, ALU.add).then_inc(scanned, 1)
                    dve.wait_ge(scanned, 2 * t + d + 1)
                    if t:
                        dve.wait_ge(stored, 16 * t)
                    end = C - 1 if d == 0 else 0
                    first = G_COL + d * (C + 1)
                    at, edge = (first + 1, first) if d == 0 else (first, first + C)
                    last = view(run)[:, :, end:end + 1]
                    nc.vector.scalar_tensor_tensor(pack[:, :, at:at + C], last.broadcast_to([P, N_CHUNKS, C]), -0.5, view(run),
                                                   ALU.mult, ALU.add).then_inc(centred, 1)
                    nc.vector.tensor_scalar(pack[:, :, edge:edge + 1], last, -0.5, None, ALU.mult).then_inc(centred, 1)
                nc.vector.tensor_scalar(kk[:], kr[:], vecs[:, K_K + t:K_K + t + 1], None, ALU.mult).then_inc(kk_raw, 1)
                dve.wait_ge(sig_done, 3 * t + 3)
                nc.vector.tensor_scalar(raw[:, 2], aa[:], vecs[:, K_A + t:K_A + t + 1], one_less[:, t:t + 1],
                                        ALU.mult, ALU.add).then_inc(k_factor, 1)
                dve.wait_ge(k_factor, t + 1)
                nc.vector.tensor_tensor(part(1), view(kr[:]), view(raw[:, 2]), ALU.mult).then_inc(k_packed, 1)
                dve.wait_ge(k_packed, t + 1)
                dve.wait_ge(scanned, 2 * t + 2)
                nc.vector.scalar_tensor_tensor(view(decay[:, 1]), view(r[:]), vecs[:, R_K + t:R_K + t + 1], part(1),
                                               ALU.mult, ALU.mult).then_inc(rk_done, 1)
                dve.wait_ge(rooted, t + 1)
                nc.vector.tensor_scalar(raw[:, 1], raw[:, 1], KK_EPS, None, ALU.max).then_inc(clamped, 1)
                dve.wait_ge(clamped, t + 1)
                nc.vector.reciprocal(raw[:, 1], raw[:, 1]).then_inc(inverted, 1)
                dve.wait_ge(inverted, t + 1)
                nc.vector.tensor_tensor(part(3), view(kk[:]), view(raw[:, 1]), ALU.mult).then_inc(kk_packed, 1)
                dve.wait_ge(kk_packed, t + 1)
                nc.vector.scalar_tensor_tensor(part(4), part(3), -1.0, view(aa[:]), ALU.mult, ALU.mult).then_inc(b_packed, 1)
                dve.wait_ge(rk_summed, t + 1)
                dve.wait_ge(copied, 2 * (t + 1))
                dve.wait_ge(b_packed, t + 1)
                nc.vector.tensor_tensor(bonus[:, t], sets[1], vr[:], ALU.mult).then_inc(kept, 1)


def rwkv_scan_phase(nc, pack_d, out, consts):
    with ExitStack() as ctx:
        m = Memory(nc, ctx, "rws")
        per_dir = lambda name, shape: [m.sb(f"{name}{d}", shape) for d in range(2)]
        PAIR, STACK = [P, 4, 2, C], [P, 4, C]
        pack = per_dir("pack", [P, 4, PACK])
        decayed, grown = per_dir("decayed", [P, 4, C + 1]), per_dir("grown", [P, 4, C + 1])
        ar = per_dir("ar", PAIR)
        a_pair, b_pair, k_pair, v_pair, grown_pair = (per_dir(n, PAIR) for n in ("a_pair", "b_pair", "k_pair", "v_pair", "grown_pair"))
        b_rows, k_rows, v_rows = (per_dir(n, PAIR) for n in ("b_rows", "k_rows", "v_rows"))
        v_stack = per_dir("v_stack", STACK)
        ab_pair, ak_pair = per_dir("ab_pair", PAIR), per_dir("ak_pair", PAIR)
        rb, rk = per_dir("rb", STACK), per_dir("rk", STACK)
        x, y, xt_pair = per_dir("x", PAIR), per_dir("y", STACK), per_dir("xt_pair", PAIR)
        rhs, u, u_pair = per_dir("rhs", STACK), per_dir("u", STACK), per_dir("u_pair", PAIR)
        h_true, h, h_sum, h_pair = per_dir("h_true", STACK), per_dir("h", STACK), per_dir("h_sum", STACK), per_dir("h_pair", PAIR)
        ps = m.psum()
        bank = lambda d, i: ps[:, (4 * d + i) * BANK:(4 * d + i + 1) * BANK]
        as_pair = lambda ap: ap.rearrange("p (q h t) -> p q h t", h=2, t=C)
        as_stack = lambda ap: ap[:, 0:4 * C].rearrange("p (q t) -> p q t", t=C)
        both = lambda ap: ap.unsqueeze(2).broadcast_to(PAIR)
        tiles = lambda ap: ap.unsqueeze(1).broadcast_to([P, 4] + list(ap.shape[1:]))
        flat = lambda ap: ap.rearrange("p h t -> p (h t)")
        ident, twice_ident = consts["ident"], consts["twice_ident"]
        stack_ident = twice_ident[:, 0:C]

        def mask(name, d, level=0, width=C):
            at = (level * 2 + d) * width
            return consts[name][:, at:at + width]

        each = lambda name: [m.sem(f"{name}{d}") for d in range(2)]
        loaded, exps, grown_2, a_2, v_2, a_r, b_2, k_2 = (each(n) for n in ("loaded", "exps", "grown_2", "a_2", "v_2", "a_r", "b_2", "k_2"))
        with_b, with_k, masked, turned, rows, stacked = (each(n) for n in ("with_b", "with_k", "masked", "turned", "rows", "stacked"))
        ly, y_set, xy, x_set, x_turned, xt_set = (each(n) for n in ("ly", "y_set", "xy", "x_set", "x_turned", "xt_set"))
        rhs_done, rhs_set, u_done, u_set, u_2 = (each(n) for n in ("rhs_done", "rhs_set", "u_done", "u_set", "u_2"))
        h_set, h_2, h_done, h_summed, h_next, y_done, y_added = (
            each(n) for n in ("h_set", "h_2", "h_done", "h_summed", "h_next", "y_done", "y_added"))
        zeroed, out_zeroed, cleared = m.sem("zeroed"), m.sem("out_zeroed"), m.sem("cleared")
        block = ctx.enter_context(nc.Block())
        now = lambda d: slice(1, C + 1) if d == 0 else slice(0, C)
        before = lambda d: slice(0, C) if d == 0 else slice(1, C + 1)
        edge = lambda d: slice(0, 1) if d == 0 else slice(C, C + 1)

        def sequences(engine, step, start=None):
            for s, (c0, cn) in enumerate(SEQ_CHUNKS):
                if start is not None:
                    start(s, c0)
                step(c0, (c0, c0 + cn - 1), c0 == 0)
                with engine.Fori(1, cn) as i:
                    step(i + c0, (i + c0, i * -1 + (c0 + cn - 1)), False)

        @block.sync
        def _(sp):
            def step(n, chunk, first):
                for d in range(2):
                    if not first:
                        sp.wait_ge(b_2[d], n)
                        sp.wait_ge(k_2[d], n)
                        sp.wait_ge(v_2[d], n)
                    sp.dma_start(pack[d][:], pack_d[chunk[d]]).then_inc(loaded[d], 16)

            sequences(sp, step)

        @block.gpsimd
        def _(pool):
            for d in range(2):
                nc.gpsimd.memset(xt_pair[d][:], 0.0).then_inc(zeroed, 1)

            pair = tiles(consts["pair"])

            def step(n, chunk, first):
                for d in range(2):
                    pool.wait_ge(loaded[d], (n + 1) * 16)
                    if not first:
                        pool.wait_ge(turned[d], 3 * n)
                    nc.gpsimd.tensor_tensor(v_pair[d][:], both(pack[d][:, :, 2 * C:3 * C]), pair, ALU.mult).then_inc(v_2[d], 1)
                    pool.wait_ge(exps[d], 2 * n + 2)
                    nc.gpsimd.tensor_tensor(grown_pair[d][:], both(grown[d][:, :, now(d)]), pair, ALU.mult).then_inc(grown_2[d], 1)
                    pool.wait_ge(a_r[d], 2 * n + 2)
                    nc.gpsimd.tensor_tensor(a_pair[d][:], both(ar[d][:, :, 0]), pair, ALU.mult).then_inc(a_2[d], 1)
                for d in range(2):
                    pool.wait_ge(h_set[d], n + 1)
                    nc.gpsimd.tensor_tensor(h_pair[d][:], both(h[d][:]), pair, ALU.mult).then_inc(h_2[d], 1)
                    pool.wait_ge(rows[d], 3 * n + 3)
                    nc.gpsimd.tensor_tensor(v_stack[d][:], v_rows[d][:, :, 0], v_rows[d][:, :, 1], ALU.add).then_inc(stacked[d], 1)
                for d in range(2):
                    pool.wait_ge(u_set[d], n + 1)
                    nc.gpsimd.tensor_tensor(u_pair[d][:], both(u[d][:]), pair, ALU.mult).then_inc(u_2[d], 1)
                for d in range(2):
                    pool.wait_ge(y_done[d], n + 1)

            sequences(pool, step)

        @block.tensor
        def _(pe):
            def turn(d, src, at, done):
                for q in range(4):
                    mm = nc.tensor.transpose(bank(d, at)[:, q * P:(q + 1) * P], flat(src[d][:, q]), ident)
                mm.then_inc(done[d], 1)

            def step(n, chunk, first):
                for d in range(2):
                    pe.wait_ge(b_2[d], n + 1)
                    for q in range(4):
                        mm = nc.tensor.matmul(bank(d, 0)[:, q * P:(q + 1) * P], flat(b_pair[d][:, q]), flat(ar[d][:, q]), start=True, stop=True)
                    mm.then_inc(with_b[d], 1)
                    pe.wait_ge(k_2[d], n + 1)
                    for q in range(4):
                        mm = nc.tensor.matmul(bank(d, 1)[:, q * P:(q + 1) * P], flat(k_pair[d][:, q]), flat(ar[d][:, q]), start=True, stop=True)
                    mm.then_inc(with_k[d], 1)
                    turn(d, b_pair, 2, turned)
                    if not first:
                        pe.wait_ge(y_added[d], n)
                    turn(d, k_pair, 3, turned)
                    pe.wait_ge(v_2[d], n + 1)
                    pe.wait_ge(rows[d], 3 * n + 1)
                    turn(d, v_pair, 2, turned)
                for level in range(LEVELS):
                    for d in range(2):
                        if level == 0:
                            pe.wait_ge(masked[d], 4 * n + 4)
                        else:
                            pe.wait_ge(x_set[d], n * LEVELS + level)
                        for q in range(4):
                            mm = nc.tensor.matmul(bank(d, 0)[:, q * C:(q + 1) * C], flat(ab_pair[d][:, q]),
                                                  x[d][:, q, 0] if level else stack_ident, start=True, stop=True)
                        mm.then_inc(ly[d], 1)
                    if level:
                        for d in range(2):
                            pe.wait_ge(y_set[d], n * LEVELS + level + 1)
                            pe.wait_ge(xt_set[d], (n * LEVELS + level) * 2)
                            for q in range(4):
                                mm = nc.tensor.matmul(bank(d, 1)[:, q * C:(q + 1) * C], flat(xt_pair[d][:, q]), y[d][:, q],
                                                      start=True, stop=True)
                            mm.then_inc(xy[d], 1)
                    for d in range(2):
                        pe.wait_ge(x_set[d], n * LEVELS + level + 1)
                        if level == 0:
                            pe.wait_ge(rows[d], 3 * n + 3)
                        for q in range(4):
                            mm = nc.tensor.transpose(bank(d, 2)[:, q * P:(q + 1) * P],
                                                     flat(x[d][:, q]), ident)
                        mm.then_inc(x_turned[d], 1)
                for d in range(2):
                    pe.wait_ge(h_set[d], n + 1)
                    pe.wait_ge(a_2[d], n + 1)
                    pe.wait_ge(stacked[d], n + 1)
                    for q in range(4):
                        o = bank(d, 3)[:, q * C:(q + 1) * C]
                        nc.tensor.matmul(o, flat(ak_pair[d][:, q]), v_stack[d][:, q], start=True, stop=False)
                        mm = nc.tensor.matmul(o, flat(a_pair[d][:, q]), h[d][:, q], start=False, stop=True)
                    mm.then_inc(rhs_done[d], 1)
                for d in range(2):
                    pe.wait_ge(rhs_set[d], n + 1)
                    pe.wait_ge(xt_set[d], (n + 1) * LEVELS * 2)
                    for q in range(4):
                        mm = nc.tensor.matmul(bank(d, 0)[:, q * C:(q + 1) * C], flat(xt_pair[d][:, q]), rhs[d][:, q], start=True, stop=True)
                    mm.then_inc(u_done[d], 1)
                for d in range(2):
                    pe.wait_ge(u_set[d], n + 1)
                    for q in range(4):
                        o = bank(d, 1)[:, q * C:(q + 1) * C]
                        nc.tensor.matmul(o, flat(b_rows[d][:, q]), u[d][:, q], start=True, stop=False)
                        mm = nc.tensor.matmul(o, flat(k_rows[d][:, q]), v_stack[d][:, q], start=False, stop=True)
                    mm.then_inc(h_done[d], 1)
                for d in range(2):
                    pe.wait_ge(h_2[d], n + 1)
                    pe.wait_ge(u_2[d], n + 1)
                    for q in range(4):
                        o = bank(d, 3)[:, q * C:(q + 1) * C]
                        nc.tensor.matmul(o, flat(h_pair[d][:, q]), ar[d][:, q, 1], start=True, stop=False)
                        nc.tensor.matmul(o, flat(u_pair[d][:, q]), rb[d][:, q], start=False, stop=False)
                        mm = nc.tensor.matmul(o, flat(v_rows[d][:, q]), rk[d][:, q], start=False, stop=True)
                    mm.then_inc(y_done[d], 1)

            sequences(pe, step)

        @block.scalar
        def _(act):
            def halves(dst, src, done):
                for r in range(2):
                    lanes = slice(r * C, (r + 1) * C)
                    nc.scalar.copy(dst[lanes, :, r], as_pair(src)[lanes, :, r]).then_inc(done, 1)

            act.wait_ge(zeroed, 2)

            def step(n, chunk, first):
                for d in range(2):
                    act.wait_ge(loaded[d], (n + 1) * 16)
                    if not first:
                        act.wait_ge(h_next[d], n)
                        act.wait_ge(b_2[d], n)
                    g = pack[d][:, :, G_COL + d * (C + 1):G_COL + (d + 1) * (C + 1)]
                    nc.scalar.activation(decayed[d][:], g, ACT.Exp, scale=-DECAY_UNIT).then_inc(exps[d], 1)
                    nc.scalar.activation(grown[d][:], g, ACT.Exp, scale=DECAY_UNIT).then_inc(exps[d], 1)
                for d in range(2):
                    for j, (dst, at) in enumerate(((b_rows, 2), (k_rows, 3), (v_rows, 2))):
                        act.wait_ge(turned[d], 3 * n + j + 1)
                        if not first:
                            act.wait_ge(y_done[d], n)
                        nc.scalar.copy(dst[d][:], as_pair(bank(d, at))).then_inc(rows[d], 1)
                for level in range(LEVELS):
                    for d in range(2):
                        act.wait_ge(x_turned[d], n * LEVELS + level + 1)
                        halves(xt_pair[d], bank(d, 2), xt_set[d])
                for d in range(2):
                    act.wait_ge(rhs_done[d], n + 1)
                    nc.scalar.copy(rhs[d][:], as_stack(bank(d, 3))).then_inc(rhs_set[d], 1)
                for d in range(2):
                    act.wait_ge(u_done[d], n + 1)
                    nc.scalar.copy(u[d][:], as_stack(bank(d, 0))).then_inc(u_set[d], 1)

            sequences(act, step)

        @block.vector
        def _(dve):
            nc.vector.memset(out[:], 0.0).then_inc(out_zeroed, 1)
            dve.wait_ge(out_zeroed, 1)

            def start(s, c0):
                for d in range(2):
                    if s:
                        dve.wait_ge(h_next[d], c0)
                    nc.vector.memset(h_true[d][:], 0.0).then_inc(cleared, 1)
                dve.wait_ge(cleared, 2 * s + 2)

            def step(n, chunk, first):
                for d in range(2):
                    dve.wait_ge(exps[d], 2 * n + 2)
                    if not first:
                        dve.wait_ge(y_done[d], n)
                        dve.wait_ge(a_2[d], n)
                    nc.vector.tensor_tensor(ar[d][:, :, 0], pack[d][:, :, 3 * C:4 * C], decayed[d][:, :, before(d)], ALU.mult).then_inc(a_r[d], 1)
                    nc.vector.tensor_tensor(ar[d][:, :, 1], pack[d][:, :, 0:C], decayed[d][:, :, now(d)], ALU.mult).then_inc(a_r[d], 1)
                for d in range(2):
                    dve.wait_ge(a_r[d], 2 * n + 2)
                    dve.wait_ge(grown_2[d], n + 1)
                    nc.vector.tensor_tensor(b_pair[d][:], both(pack[d][:, :, 4 * C:5 * C]), grown_pair[d][:], ALU.mult).then_inc(b_2[d], 1)
                    nc.vector.tensor_tensor(k_pair[d][:], both(pack[d][:, :, C:2 * C]), grown_pair[d][:], ALU.mult).then_inc(k_2[d], 1)
                for d in range(2):
                    if not first:
                        dve.wait_ge(h_next[d], n)
                    nc.vector.tensor_tensor(h[d][:], h_true[d][:], grown[d][:, :, edge(d)].broadcast_to(STACK), ALU.mult).then_inc(h_set[d], 1)
                for d in range(2):
                    dve.wait_ge(with_b[d], n + 1)
                    s = as_pair(bank(d, 0))
                    nc.vector.tensor_tensor(ab_pair[d][:], both(s[:, :, 0]), tiles(consts_3d(mask("before_pair", d, width=2 * C))),
                                            ALU.mult).then_inc(masked[d], 1)
                    nc.vector.tensor_tensor(rb[d][:], s[:, :, 1], tiles(mask("upto", d)), ALU.mult).then_inc(masked[d], 1)
                    dve.wait_ge(with_k[d], n + 1)
                    s = as_pair(bank(d, 1))
                    nc.vector.tensor_tensor(ak_pair[d][:], both(s[:, :, 0]), tiles(consts_3d(mask("before_pair", d, width=2 * C))),
                                            ALU.mult).then_inc(masked[d], 1)
                    nc.vector.tensor_tensor(rk[d][:], s[:, :, 1], tiles(mask("upto", d)), ALU.mult).then_inc(masked[d], 1)
                for level in range(LEVELS):
                    for d in range(2):
                        dve.wait_ge(ly[d], n * LEVELS + level + 1)
                        nc.vector.tensor_tensor(y[d][:], as_stack(bank(d, 0)), tiles(mask("level", d, level)), ALU.mult).then_inc(y_set[d], 1)
                    for d in range(2):
                        if level == 0:
                            dve.wait_ge(y_set[d], n * LEVELS + 1)
                            nc.vector.tensor_tensor(x[d][:], both(y[d][:]), tiles(consts_3d(twice_ident)), ALU.add).then_inc(x_set[d], 1)
                        else:
                            dve.wait_ge(xy[d], n * (LEVELS - 1) + level)
                            dve.wait_ge(x_turned[d], n * LEVELS + level)
                            nc.vector.tensor_tensor(x[d][:], x[d][:], both(as_stack(bank(d, 1))), ALU.add).then_inc(x_set[d], 1)
                for d in range(2):
                    dve.wait_ge(h_done[d], n + 1)
                    nc.vector.tensor_tensor(h_sum[d][:], h[d][:], as_stack(bank(d, 1)), ALU.add).then_inc(h_summed[d], 1)
                    dve.wait_ge(h_summed[d], n + 1)
                    nc.vector.tensor_tensor(h_true[d][:], h_sum[d][:], grown[d][:, :, edge(d)].broadcast_to(STACK), ALU.mult).then_inc(h_next[d], 1)
                for d in range(2):
                    dve.wait_ge(y_done[d], n + 1)
                    if not first:
                        dve.wait_ge(y_added[1 - d], n)
                    at = bass.ds(chunk[d] * C, C)
                    nc.vector.tensor_tensor(out[:, :, at], out[:, :, at], as_stack(bank(d, 3)), ALU.add).then_inc(y_added[d], 1)

            sequences(dve, step, start)


def consts_3d(ap):
    return ap.rearrange("p (h t) -> p h t", t=C)


def rwkv_finish_phase(nc, vecs, out, bonus, gate, consts):
    with ExitStack() as ctx:
        m = Memory(nc, ctx, "rwf")
        sq, rstd, eps = m.sb("sq", [P, 2, T]), m.sb("rstd", [P, 2, T]), m.sb("eps", [P, 1])
        ps = m.psum()
        sets = [ps[:, 0:T], ps[:, 3 * BANK:3 * BANK + T]]
        eps_set, summed, centred, squared, sq_summed, logged, rooted = (
            m.sem(n) for n in ("eps_set", "summed", "centred", "squared", "sq_summed", "logged", "rooted"))
        scaled, affine, raised = m.sem("scaled"), m.sem("affine"), m.sem("raised")
        block = ctx.enter_context(nc.Block())

        @block.tensor
        def _(pe):
            for t in range(4):
                if t:
                    pe.wait_ge(centred, t)
                for t0, tn in TOKEN_CHUNKS:
                    mm = nc.tensor.matmul(sets[0][:, t0:t0 + tn], consts["head_ones"], out[:, t, t0:t0 + tn], start=True, stop=True)
                mm.then_inc(summed, 1)
                pe.wait_ge(squared, t + 1)
                if t:
                    pe.wait_ge(logged, t)
                for t0, tn in TOKEN_CHUNKS:
                    mm = nc.tensor.matmul(sets[1][:, t0:t0 + tn], consts["head_ones"], sq[:, t % 2, t0:t0 + tn], start=True, stop=True)
                mm.then_inc(sq_summed, 1)

        @block.scalar
        def _(act):
            act.wait_ge(eps_set, 1)
            for t in range(4):
                act.wait_ge(centred, t + 1)
                nc.scalar.activation(sq[:, t % 2], out[:, t], ACT.Square).then_inc(squared, 1)
                act.wait_ge(sq_summed, t + 1)
                if t >= 2:
                    act.wait_ge(scaled, t - 1)
                nc.scalar.activation(rstd[:, t % 2], sets[1], ACT.Ln, bias=eps[:], scale=1 / C).then_inc(logged, 1)
                act.wait_ge(logged, t + 1)
                nc.scalar.activation(rstd[:, t % 2], rstd[:, t % 2], ACT.Exp, scale=-0.5).then_inc(rooted, 1)

        @block.vector
        def _(dve):
            nc.vector.memset(eps[:], RWKV_GN_EPS).then_inc(eps_set, 1)

            def centre(t):
                dve.wait_ge(summed, t + 1)
                nc.vector.scalar_tensor_tensor(out[:, t], sets[0], -1 / C, out[:, t], ALU.mult, ALU.add).then_inc(centred, 1)

            def norm(t):
                dve.wait_ge(rooted, t + 1)
                nc.vector.tensor_tensor(out[:, t], out[:, t], rstd[:, t % 2], ALU.mult).then_inc(scaled, 1)
                dve.wait_ge(scaled, t + 1)
                nc.vector.tensor_scalar(out[:, t], out[:, t], vecs[:, LNX_G + t:LNX_G + t + 1], vecs[:, LNX_B + t:LNX_B + t + 1],
                                        ALU.mult, ALU.add).then_inc(affine, 1)
                dve.wait_ge(affine, t + 1)
                nc.vector.tensor_tensor(out[:, t], out[:, t], bonus[:, t], ALU.add).then_inc(raised, 1)
                dve.wait_ge(raised, t + 1)
                nc.vector.tensor_tensor(out[:, t], out[:, t], gate[:, t], ALU.mult)

            centre(0)
            for t in range(1, 4):
                centre(t)
                norm(t - 1)
            norm(3)


def split_phase(nc, acc, resid_d, xh, xl):
    with ExitStack() as ctx:
        m = Memory(nc, ctx, "split")
        high, low, back = m.sem("high"), m.sem("low"), m.sem("back")
        block = ctx.enter_context(nc.Block())

        @block.scalar
        def _(act):
            for k in range(KT):
                nc.scalar.copy(xh[:, k, :], acc[:, k, :]).then_inc(high, 1)

        @block.vector
        def _(dve):
            for k in range(KT):
                dve.wait_ge(high, k + 1)
                nc.vector.tensor_tensor(xl[:, k, :], acc[:, k, :], xh[:, k, :], ALU.subtract).then_inc(low, 1)

        @block.sync
        def _(sp):
            for k in range(KT):
                sp.wait_ge(low, k + 1)
                sp.dma_start(acc[:, k, :], resid_d[:, k, :]).then_inc(back, 16)
            sp.wait_ge(back, 16 * KT)


def attention_phase(nc, q, kv_d, xh, xl, ident):
    HEADS, M = 4, 256
    SCALE = 256.0 ** -0.5
    with ExitStack() as ctx:
        m = Memory(nc, ctx, "attn")
        keys = m.sb("keys", [P, KT, 2 * M])
        values = m.sb("values", [P, 4, D])
        q_now = m.sb("q_now", [P, KT, P])
        probs, probs_t = m.sb("probs", [P, HEADS, M]), m.sb("probs_t", [P, 2 * HEADS, P])
        top, neg, total, inverse = (m.sb(n, [P, HEADS]) for n in ("top", "neg", "total", "inverse"))
        ps = m.psum()
        v_raw = [probs[:].rearrange("p h m -> p (h m)")[:, 0:2 * M], probs[:].rearrange("p h m -> p (h m)")[:, 2 * M:4 * M]]
        S_AT, T_AT, O_AT = 0, 2 * BANK, 4 * BANK
        keys_in, v_in = m.sem("keys_in"), [m.sem("v_in0"), m.sem("v_in1")]
        v_turned, v_set = m.sem("v_turned"), m.sem("v_set")
        staged, scored, topped, negated, expd, inverted, normed = (
            m.sem(n) for n in ("staged", "scored", "topped", "negated", "expd", "inverted", "normed"))
        turned, t_set, outed, high, low = (m.sem(n) for n in ("turned", "t_set", "outed", "high", "low"))
        block = ctx.enter_context(nc.Block())
        heads = lambda ap: ap.rearrange("p (h m) -> p h m", h=HEADS)

        def sequences(engine, step):
            for s, (t0, tn) in enumerate(((0, T_PROMPT // P), (T_PROMPT // P, T_SAMPLE // P))):
                step(t0, s, s == 0)
                with engine.Fori(t0 + 1, t0 + tn) as i:
                    step(i, s, False)

        @block.sync
        def _(sp):
            sp.dma_start(keys[:], kv_d[0:KT].rearrange("n p m -> p n m")).then_inc(keys_in, 16)
            for j in range(KT):
                if j >= 2:
                    sp.wait_ge(v_turned, j - 1)
                sp.dma_start(v_raw[j % 2], kv_d[KT + j]).then_inc(v_in[j % 2], 16)

        @block.gpsimd
        def _(pool):
            def step(n, s, first):
                if not first:
                    pool.wait_ge(scored, n)
                nc.gpsimd.tensor_copy(q_now[:], q[:, :, bass.ds(n * P, P)]).then_inc(staged, 1)

            sequences(pool, step)

        @block.tensor
        def _(pe):
            for j in range(KT):
                pe.wait_ge(v_in[j % 2], 16 * (j // 2 + 1))
                if j >= 2:
                    pe.wait_ge(v_set, j - 1)
                for i in range(4):
                    mm = nc.tensor.transpose(ps[:, j % 2 * BANK + i * P:j % 2 * BANK + (i + 1) * P], v_raw[j % 2][:, i * P:(i + 1) * P], ident)
                mm.then_inc(v_turned, 1)
            pe.wait_ge(v_set, KT)
            pe.wait_ge(keys_in, 16)

            def step(n, s, first):
                pe.wait_ge(staged, n + 1)
                if not first:
                    pe.wait_ge(expd, 4 * n)
                for h in range(HEADS):
                    for j in range(2):
                        mm = nc.tensor.matmul(ps[:, S_AT + h * M:S_AT + (h + 1) * M], q_now[:, 2 * h + j],
                                              keys[:, 2 * h + j, s * M:(s + 1) * M], start=(j == 0), stop=(j == 1))
                mm.then_inc(scored, 1)
                pe.wait_ge(normed, n + 1)
                if not first:
                    pe.wait_ge(t_set, n)
                for h in range(HEADS):
                    for j in range(2):
                        at = T_AT + (2 * h + j) * P
                        mm = nc.tensor.transpose(ps[:, at:at + P], probs[:, h, j * P:(j + 1) * P], ident)
                mm.then_inc(turned, 1)
                pe.wait_ge(t_set, n + 1)
                if not first:
                    pe.wait_ge(low, n)
                for o in range(KT):
                    for j in range(2):
                        mm = nc.tensor.matmul(ps[:, O_AT + o * P:O_AT + (o + 1) * P], values[:, 2 * s + j, o * P:(o + 1) * P],
                                              probs_t[:, o // 2 * 2 + j], start=(j == 0), stop=(j == 1))
                mm.then_inc(outed, 1)

            sequences(pe, step)

        @block.scalar
        def _(act):
            for j in range(KT):
                act.wait_ge(v_turned, j + 1)
                nc.scalar.copy(values[:, :, j * P:(j + 1) * P], ps[:, j % 2 * BANK:(j % 2 + 1) * BANK].rearrange("p (i t) -> p i t", i=4)).then_inc(v_set, 1)

            def step(n, s, first):
                act.wait_ge(negated, n + 1)
                if first:
                    act.wait_ge(v_turned, KT)
                else:
                    act.wait_ge(turned, n)
                for h in range(HEADS):
                    nc.scalar.activation(probs[:, h], ps[:, S_AT + h * M:S_AT + (h + 1) * M], ACT.Exp, bias=neg[:, h:h + 1],
                                         scale=SCALE, accum_out=total[:, h:h + 1]).then_inc(expd, 1)
                act.wait_ge(turned, n + 1)
                if not first:
                    act.wait_ge(outed, n)
                nc.scalar.copy(probs_t[:], ps[:, T_AT:T_AT + 2 * BANK].rearrange("p (o t) -> p o t", t=P)).then_inc(t_set, 1)
                act.wait_ge(outed, n + 1)
                nc.scalar.copy(xh[:, :, bass.ds(n * P, P)], ps[:, O_AT:O_AT + 2 * BANK].rearrange("p (o t) -> p o t", t=P)).then_inc(high, 1)

            sequences(act, step)

        @block.vector
        def _(dve):
            def step(n, s, first):
                dve.wait_ge(scored, n + 1)
                nc.vector.tensor_reduce(top[:], heads(ps[:, S_AT:S_AT + 2 * BANK]), mybir.AxisListType.X, ALU.max).then_inc(topped, 1)
                dve.wait_ge(topped, n + 1)
                nc.vector.tensor_scalar(neg[:], top[:], -SCALE, None, ALU.mult).then_inc(negated, 1)
                dve.wait_ge(expd, 4 * n + 4)
                nc.vector.reciprocal(inverse[:], total[:]).then_inc(inverted, 1)
                dve.wait_ge(inverted, n + 1)
                nc.vector.tensor_tensor(probs[:], probs[:], inverse[:].unsqueeze(2).broadcast_to([P, HEADS, M]), ALU.mult).then_inc(normed, 1)
                dve.wait_ge(high, n + 1)
                at = bass.ds(n * P, P)
                nc.vector.tensor_tensor(xl[:, :, at], ps[:, O_AT:O_AT + 2 * BANK].rearrange("p (o t) -> p o t", t=P), xh[:, :, at],
                                        ALU.subtract).then_inc(low, 1)

            sequences(dve, step)


def memory_phases(nc, a, vecs, kv_d):
    with ExitStack() as ctx:
        m = Memory(nc, ctx, "mem")
        mem, mh, ml = m.sb("mem", [P, KT, MEM_T]), m.sb("mh", [P, KT, MEM_T], F32R), m.sb("ml", [P, KT, MEM_T], F32R)
        ones = m.sb("ones", [P, P])
        with ExitStack() as c2:
            loaded = Memory(nc, c2, "memload").sem("loaded")
            block = c2.enter_context(nc.Block())

            @block.sync
            def _(sp):
                sp.dma_start(mem[:], a["mem"]).then_inc(loaded, 16)
                sp.wait_ge(loaded, 16)

            @block.vector
            def _(dve):
                nc.vector.memset(ones[:], 1.0 / D)

        norm_phase(nc, "memln", mem, ones, vecs, VEC["mem_ln_g"], VEC["mem_ln_b"], tokens=MEM_T, xh=mh, xl=ml)
        linear_phase(nc, "kv", a["ca_w_kv"], 2 * KT, mh, ml, ((0, MEM_T),), "store", kv_d)


def mix_phases(nc, a, proj_d, pack_d, vecs, mix_o, mix_y):
    with ExitStack() as mixing:
        const_sb = Memory(nc, mixing, "mix").sb("consts", [P, a["consts"].shape[1]])
        load_constants(nc, a, const_sb)
        consts = {n: const_sb[:, at:at + w] for n, (at, w) in CONST.items()}
        consts["pair"] = consts["pair"].rearrange("p (a t) -> p a t", t=C)
        with ExitStack() as ctx:
            m = Memory(nc, ctx, "gla")
            v = m.sb("v", [P, 4, T])
            q_in, k_in, q_st, k_out = ([m.sb(f"{n}{d}", [P, 2, T]) for d in range(2)] for n in ("q_in", "k_in", "q_st", "k_out"))
            decay = [m.sb(f"decay{d}", [P, 2, N_CHUNKS]) for d in range(2)]
            gla_prepare_phase(nc, a, proj_d, vecs, v, q_in, k_in, q_st, k_out, decay)
            gla_scan_phase(nc, v, q_in, k_in, q_st, k_out, decay, mix_o, consts)
        gla_finish_phase(nc, proj_d, vecs, mix_o, consts)
        with ExitStack() as ctx:
            m = Memory(nc, ctx, "rwkv")
            bonus, gate = m.sb("bonus", [P, 4, T]), m.sb("gate", [P, 4, T])
            rwkv_prepare_phase(nc, a, proj_d, pack_d, vecs, bonus, gate, consts)
            rwkv_scan_phase(nc, pack_d, mix_y, consts)
            rwkv_finish_phase(nc, vecs, mix_y, bonus, gate, consts)


def build(nc, a, out_d):
    proj_d = nc.dram_tensor("proj", (MIX_TILES, P, T), F32, kind="Internal").ap()
    resid_d = nc.dram_tensor("resid", (P, KT, T), F32, kind="Internal").ap()
    pack_d = nc.dram_tensor("pack", (N_CHUNKS, P, 4, PACK), F32, kind="Internal").ap()
    kv_d = nc.dram_tensor("kv", (2 * KT, P, MEM_T), F32, kind="Internal").ap()
    with ExitStack() as ctx:
        m = Memory(nc, ctx, "main")
        vecs = m.sb("vecs", [P, a["vecs"].shape[1]])
        mean_ones = m.sb("mean_ones", [P, P])
        acc = m.sb("acc", [P, KT, T])
        set_ones(nc, mean_ones)
        with ExitStack() as parts:
            mp = Memory(nc, parts, "x1")
            xh, xl = mp.sb("xh", [P, KT, T], F32R), mp.sb("xl", [P, KT, T], F32R)
            load_phase(nc, a["x"], a["vecs"], acc, xh, xl, vecs)
            ffn_phase(nc, "ffn1", a["ffn1_w_in"], a["ffn1_w_out"], xh, xl, acc)
            norm_phase(nc, "ln1", acc, mean_ones, vecs, VEC["ln_ffn1_g"], VEC["ln_ffn1_b"], scale=0.5, xh=xh, xl=xl, after=ALPHA)
            linear_phase(nc, "mixin", a["mix_w_in"], MIX_TILES, xh, xl, TOKEN_CHUNKS, "store", proj_d, spill=(acc[:], resid_d))
        mix_phases(nc, a, proj_d, pack_d, vecs, acc[:, 0:4], acc[:, 4:8])
        memory_phases(nc, a, vecs, kv_d)
        with ExitStack() as parts:
            mp = Memory(nc, parts, "x2")
            xh, xl = mp.sb("xh", [P, KT, T], F32R), mp.sb("xl", [P, KT, T], F32R)
            split_phase(nc, acc, resid_d, xh, xl)
            linear_phase(nc, "mixout", a["mix_w_out"], KT, xh, xl, TOKEN_CHUNKS, "add", acc)
            norm_phase(nc, "ln2", acc, mean_ones, vecs, VEC["ln_mix_g"], VEC["ln_mix_b"], xh=xh, xl=xl, after=ALPHA)
            with ExitStack() as queries:
                mq = Memory(nc, queries, "attq")
                ident = mq.sb("ident", [P, P])
                q = mq.sb("q", [P, KT, T])
                load_ident(nc, a, ident)
                linear_phase(nc, "wq", a["ca_w_q"], KT, xh, xl, TOKEN_CHUNKS, "keep", q)
                attention_phase(nc, q, kv_d, xh, xl, ident[:])
            linear_phase(nc, "wo", a["ca_w_o"], KT, xh, xl, TOKEN_CHUNKS, "add", acc)
            norm_phase(nc, "ln3", acc, mean_ones, vecs, VEC["ln_ca_g"], VEC["ln_ca_b"], xh=xh, xl=xl, after=2 * ALPHA)
            ffn_phase(nc, "ffn2", a["ffn2_w_in"], a["ffn2_w_out"], xh, xl, acc)
            norm_phase(nc, "ln4", acc, mean_ones, vecs, VEC["ln_ffn2_g"], VEC["ln_ffn2_b"], scale=0.5, out_d=out_d)


def load_constants(nc, a, const_sb):
    with ExitStack() as ctx:
        m = Memory(nc, ctx, "const")
        loaded = m.sem("loaded")
        block = ctx.enter_context(nc.Block())

        @block.sync
        def _(sp):
            sp.dma_start(const_sb[:], a["consts"]).then_inc(loaded, 16)
            sp.wait_ge(loaded, 16)


def load_ident(nc, a, ident):
    with ExitStack() as ctx:
        loaded = Memory(nc, ctx, "ident").sem("loaded")
        block = ctx.enter_context(nc.Block())
        at, w = CONST["ident"]

        @block.sync
        def _(sp):
            sp.dma_start(ident[:], a["consts"][:, at:at + w]).then_inc(loaded, 16)
            sp.wait_ge(loaded, 16)


def set_ones(nc, ones):
    with ExitStack() as ctx:
        block = ctx.enter_context(nc.Block())

        @block.vector
        def _(dve):
            nc.vector.memset(ones[:], 1.0 / D)


def constant_table():
    row, tok = np.arange(P)[:, None], np.arange(C)[None, :]
    own = (row // C == np.arange(2)[None, :]).astype(np.float32)
    pair = np.repeat(own, C, 1)
    s = row % C
    upto = [s <= tok, s >= tok]
    before = [s < tok, s > tok]
    levels = []
    for level in range(LEVELS):
        b = 2 ** level
        levels += [(s // b % 2 == 1) & (tok // b == s // b - 1), (s // b % 2 == 0) & (tok // b == s // b + 1)]
    parts = {"ident": np.eye(P), "pair": pair, "ones": np.ones((P, P)), "head_ones": own @ own.T, "twice_ident": np.tile(s == tok, (1, 2)),
             "causal": np.concatenate([pair * np.tile(b, (1, 2)) for b in upto], 1),
             "before_pair": np.concatenate([pair * np.tile(b, (1, 2)) for b in before], 1),
             "upto": np.concatenate(upto, 1), "level": np.concatenate(levels, 1)}
    return {n: v.astype(np.float32) for n, v in parts.items()}


CONST = {}
for _name, _value in constant_table().items():
    CONST[_name] = (sum(w for _, w in CONST.values()), _value.shape[1])


def feature_major(x):
    t, d = x.shape
    return np.ascontiguousarray(x.T.reshape(d // P, P, t).transpose(1, 0, 2))


def column(v):
    return v.reshape(-1, P).T


def output_tiles(w):
    k, n = w.shape
    return w.reshape(k // P, P, n // P, P).transpose(2, 1, 0, 3).reshape(n // P, P, (k // P) * P)


def lay_out(i):
    g = {n: np.asarray(v) for n, v in i.items()}
    out = {"x": feature_major(np.concatenate([g["x_prompt"][0], g["x_sample"][0]], 0)),
           "vecs": np.concatenate([column(g[n][0]) for n in VEC_NAMES], 1)}
    for f in ("ffn1", "ffn2"):
        w = g[f + "_w_in"][0]
        out[f + "_w_in"] = np.concatenate([output_tiles(w[:, :D_FF]), output_tiles(w[:, D_FF:])], 2)
        out[f + "_w_out"] = g[f + "_w_out"][0].reshape(FT, P, D)
    out["mem"] = feature_major(np.concatenate([g["mem_prompt"][0], g["mem_sample"][0]], 0))
    for n in ("mix_w_out", "ca_w_q", "ca_w_kv", "ca_w_o"):
        out[n] = output_tiles(g[n][0])
    def mu_columns(v):
        rkv, wd, ad, gd = v[:1536], v[1536:1664], v[1664:1728], v[1728:]
        return column(np.concatenate([rkv, wd, ad, np.zeros(64, v.dtype), gd]))

    out["vecs"] = np.concatenate(
        [out["vecs"]] + [column(g[n][0]) for n in ("gla_gate_b_fwd", "gla_gate_b_bwd", "gla_norm_g")]
        + [mu_columns(g[n][0]) for n in ("rwkv_mu_prev", "rwkv_mu_next")]
        + [column(g[n][0].reshape(-1)) for n in ("rwkv_w0_fwd", "rwkv_w0_bwd", "rwkv_a0", "rwkv_k_k", "rwkv_k_a", "rwkv_r_k",
                                                 "rwkv_lnx_g", "rwkv_lnx_b")], 1)
    lora = np.zeros((4, P, 4, P), g["rwkv_g_up"].dtype)
    for j, (n, row) in enumerate((("rwkv_w_up_fwd", 0), ("rwkv_w_up_bwd", 64), ("rwkv_a_up", 0), ("rwkv_g_up", 0))):
        w = g[n][0]
        lora[:, row:row + w.shape[0], j] = w.reshape(w.shape[0], 4, P).transpose(1, 0, 2)
    out["lora"] = lora.reshape(4, P, 4 * P)
    w = g["mix_w_in"][0]
    starts = np.cumsum([0, 256, 256, 512, 512, 16, 16, 512, 512, 512, 64, 64, 64, 128])
    q, k, v, gg, gdf, gdb, r, kr, vr, wdf, wdb, ad, gd = (w[:, x:y] for x, y in zip(starts[:-1], starts[1:]))
    pad = np.zeros((D, 32), w.dtype)
    out["mix_w_in"] = output_tiles(np.concatenate([q, k, v, gg, r, kr, vr, wdf, wdb, ad, gdf, gdb, pad, gd], 1))
    up = np.zeros((P, 4 * P), w.dtype)
    up[64:80, :2 * P] = g["gla_gate_up_fwd"][0]
    up[80:96, 2 * P:] = g["gla_gate_up_bwd"][0]
    out["gla_up"] = up
    out["consts"] = np.concatenate(list(constant_table().values()), 1)
    out["keep"] = np.tile((np.arange(T) % C != 0).astype(np.float32), (P, 1))
    return {n: np.ascontiguousarray(v) for n, v in out.items()}


def kernel(**inputs):
    import concourse.bacc as bacc
    from concourse.bass_utils import run_bass_kernel_spmd as run

    nc = bacc.Bacc("TRN2", target_bir_lowering=False, num_devices=1)
    arrays = {n + "_dram": v for n, v in lay_out(inputs).items()}
    args = {n[:-5]: nc.dram_tensor(n, v.shape, F32, kind="ExternalInput").ap() for n, v in arrays.items()}
    out_d = nc.dram_tensor("y_dram", (P, KT, T), F32, kind="ExternalOutput").ap()
    build(nc, args, out_d)
    y = run(nc, [arrays], core_ids=[0]).results[0]["y_dram"]
    y = y.transpose(2, 1, 0).reshape(T, D)
    return y[None, :T_PROMPT], y[None, T_PROMPT:]
```

```python
from contextlib import ExitStack

import numpy as np

import concourse.bass as bass
from concourse import mybir

ALU = mybir.AluOpType
ACT = mybir.ActivationFunctionType
F32 = mybir.dt.float32
F32R = mybir.dt.float32r
U32 = mybir.dt.uint32

P = 128
D = 1024
KT = D // P
T_PROMPT, T_SAMPLE = 256, 1024
T = T_PROMPT + T_SAMPLE
D_FF = 2816
FT = D_FF // P
BANK = 512
TOKEN_CHUNKS = ((0, 512), (512, 512), (1024, 256))
ALPHA = 2.0 ** 0.25
LN_EPS = 1e-5
NT = 256

GLA_DK, GLA_DV, GLA_TAU = 64, 128, 16.0
C = 64
N_CHUNKS = T // C
SEQ_CHUNKS = ((0, T_PROMPT // C), (T_PROMPT // C, T_SAMPLE // C))
Q_TILE, K_TILE, V_TILE, G_TILE = 0, 2, 4, 8
R_TILE, KR_TILE, VR_TILE = 12, 16, 20
DECAY_TILE, LOW_TILE, GATE_TILE = 24, 25, 26
MIX_TILES = 27
RWKV_GN_EPS = 64e-5
KK_EPS = 1e-12
LEVELS = 6
DECAY_UNIT = float(np.exp(-0.5))
R_COL, V_COL, G_COL = 0, C, 2 * C
K_COL = G_COL + 2 * (C + 1)
KK_COL, B_COL, PACK = K_COL + C, K_COL + 2 * C, K_COL + 3 * C
MEM_T = 512

VEC_NAMES = ("ln_ffn1_g", "ln_ffn1_b", "ln_mix_g", "ln_mix_b", "mem_ln_g", "mem_ln_b",
             "ln_ca_g", "ln_ca_b", "ln_ffn2_g", "ln_ffn2_b")
VEC = {n: KT * i for i, n in enumerate(VEC_NAMES)}
GLA_B = KT * len(VEC_NAMES)
GLA_G = GLA_B + 4
MU_TILES = 15
MU_PREV = GLA_G + 4
MU_NEXT = MU_PREV + MU_TILES
W0 = MU_NEXT + MU_TILES
A0, K_K, K_A, R_K, LNX_G, LNX_B = (W0 + 8 + 4 * i for i in range(6))


class Memory:

    def __init__(self, nc, ctx, tag):
        self.nc, self.ctx, self.tag, self.sems = nc, ctx, tag, []
        ctx.callback(self.clear_semaphores)

    def clear_semaphores(self):
        if self.sems:
            with self.nc.Block() as block:
                @block.sync
                def _(sp):
                    for s in self.sems:
                        sp.sem_clear(s)

    def sb(self, name, shape, dt=F32):
        return self.ctx.enter_context(self.nc.sbuf_tensor(f"{self.tag}_{name}", shape, dt))

    def psum(self):
        return self.ctx.enter_context(self.nc.psum_tensor(f"{self.tag}_psum", [P, 8 * BANK], F32))

    def sem(self, name):
        s = self.ctx.enter_context(self.nc.semaphore(f"{self.tag}_{name}"))
        self.sems.append(s)
        return s


def load_phase(nc, x_d, vec_d, x32, xh, xl, vecs):
    with ExitStack() as ctx:
        m = Memory(nc, ctx, "load")
        x_in = [m.sem(f"x_in{k}") for k in range(KT)]
        vec_in, high, low = m.sem("vec_in"), m.sem("high"), m.sem("low")
        block = ctx.enter_context(nc.Block())

        @block.sync
        def _(sp):
            for k in range(KT):
                sp.dma_start(x32[:, k, :], x_d[:, k, :]).then_inc(x_in[k], 16)
            sp.dma_start(vecs[:], vec_d).then_inc(vec_in, 16)
            sp.wait_ge(vec_in, 16)

        @block.scalar
        def _(act):
            for k in range(KT):
                act.wait_ge(x_in[k], 16)
                nc.scalar.copy(xh[:, k, :], x32[:, k, :]).then_inc(high, 1)

        @block.vector
        def _(dve):
            for k in range(KT):
                dve.wait_ge(high, k + 1)
                nc.vector.tensor_tensor(xl[:, k, :], x32[:, k, :], xh[:, k, :], ALU.subtract).then_inc(low, 1)
                dve.wait_ge(low, k + 1)
                nc.vector.tensor_scalar(x32[:, k, :], x32[:, k, :], 2 * ALPHA, None, ALU.mult)


def ffn_phase(nc, tag, w_in_d, w_out_d, xh, xl, acc):
    with ExitStack() as ctx:
        m = Memory(nc, ctx, tag)
        raw_in = m.sb("raw_in", [P, 2 * KT * P])
        raw_out = m.sb("raw_out", [P, D])
        wi_h = m.sb("wi_h", [P, 2, 2 * KT * P], F32R)
        wi_l = m.sb("wi_l", [P, 2, 2 * KT * P], F32R)
        wo_h = m.sb("wo_h", [P, 2, D], F32R)
        wo_l = m.sb("wo_l", [P, 2, D], F32R)
        hid = m.sb("hid", [P, T])
        hid_h = m.sb("hid_h", [P, T], F32R)
        hid_l = m.sb("hid_l", [P, T], F32R)
        ps = m.psum()
        gate_at, up_at, out_at = 0, 3 * BANK, 6 * BANK
        in_loaded, out_loaded = m.sem("in_loaded"), m.sem("out_loaded")
        wi_high, wi_split = m.sem("wi_high"), m.sem("wi_split")
        wo_high, wo_split = m.sem("wo_high"), m.sem("wo_split")
        gate_done, up_done, out_done = m.sem("gate_done"), m.sem("up_done"), m.sem("out_done")
        silu_done, hid_done, hid_high, hid_split = m.sem("silu_done"), m.sem("hid_done"), m.sem("hid_high"), m.sem("hid_split")
        added = m.sem("added")
        OUTS = KT * len(TOKEN_CHUNKS)
        WAIT_GROUPS = 4
        PER_GROUP = OUTS // (2 * KT - WAIT_GROUPS)
        block = ctx.enter_context(nc.Block())

        def pairs(engine, step):
            with engine.Fori(0, (FT - 2) // 2) as i:
                for u in (1, 2):
                    step(2 * i + u, u % 2)
            step(FT - 1, (FT - 1) % 2)

        @block.sync
        def _(sp):
            def load(f, first=False):
                if not first:
                    sp.wait_ge(wi_split, f)
                sp.dma_start(raw_in[:], w_in_d[f]).then_inc(in_loaded, 16)
                if not first:
                    sp.wait_ge(wo_split, f)
                sp.dma_start(raw_out[:], w_out_d[f]).then_inc(out_loaded, 16)

            load(0, first=True)
            with sp.Fori(1, FT) as f:
                load(f)

        @block.tensor
        def _(pe):
            def project(f, slot, n):
                g, k = n // KT, n % KT
                at, cols = (gate_at, up_at)[g], slice(n * P, (n + 1) * P)
                for j, (w, x) in enumerate(((wi_h, xh), (wi_h, xl), (wi_l, xh))):
                    for c, (t0, tn) in enumerate(TOKEN_CHUNKS):
                        mm = nc.tensor.matmul(ps[:, at + c * BANK:at + c * BANK + tn], w[:, slot, cols], x[:, k, t0:t0 + tn],
                                              start=(k == 0 and j == 0), stop=(k == KT - 1 and j == 2))
                if k == KT - 1:
                    mm.then_inc((gate_done, up_done)[g], 1)

            def expand(f, slot, s):
                o, (t0, tn) = s // 3, TOKEN_CHUNKS[s % 3]
                pe.wait_ge(added, OUTS * f + s + 1)
                at = out_at + s % 2 * BANK
                for j, (w, h) in enumerate(((wo_h, hid_h), (wo_h, hid_l), (wo_l, hid_h))):
                    mm = nc.tensor.matmul(ps[:, at:at + tn], w[:, slot, o * P:(o + 1) * P], h[:, t0:t0 + tn],
                                          start=(j == 0), stop=(j == 2))
                mm.then_inc(out_done, 1)

            def step(f, slot):
                pe.wait_ge(wi_split, f + 1)
                for n in range(2 * KT):
                    if n % KT == 0:
                        pe.wait_ge((silu_done, hid_done)[n // KT], f)
                    project(f, slot, n)
                    if n == WAIT_GROUPS:
                        pe.wait_ge(hid_split, f)
                        pe.wait_ge(wo_split, f)
                    if n >= WAIT_GROUPS:
                        for s in range((n - WAIT_GROUPS) * PER_GROUP, (n - WAIT_GROUPS + 1) * PER_GROUP):
                            expand(f - 1, 1 - slot, s)

            pe.wait_ge(wi_split, 1)
            for n in range(2 * KT):
                project(0, 0, n)
            pairs(pe, step)
            pe.wait_ge(hid_split, FT)
            for s in range(OUTS):
                expand(FT - 1, (FT - 1) % 2, s)

        @block.scalar
        def _(act):
            def split_in(f, slot):
                act.wait_ge(in_loaded, 16 * (f + 1))
                nc.scalar.copy(wi_h[:, slot, :], raw_in[:]).then_inc(wi_high, 1)

            def split_out(f, slot):
                act.wait_ge(out_loaded, 16 * (f + 1))
                nc.scalar.copy(wo_h[:, slot, :], raw_out[:]).then_inc(wo_high, 1)

            def activate(f):
                act.wait_ge(gate_done, f + 1)
                nc.scalar.activation(hid[:], ps[:, gate_at:gate_at + T], ACT.Silu).then_inc(silu_done, 1)

            def high_part(f):
                act.wait_ge(hid_done, f + 1)
                nc.scalar.copy(hid_h[:], hid[:]).then_inc(hid_high, 1)

            def step(f, slot, last=False):
                high_part(f - 1)
                if not last:
                    split_in(f + 1, 1 - slot)
                act.wait_ge(hid_split, f)
                split_out(f, slot)
                activate(f)
                act.wait_ge(out_done, OUTS * f)

            split_in(0, 0)
            split_out(0, 0)
            split_in(1, 1)
            activate(0)
            with act.Fori(0, (FT - 2) // 2) as i:
                for u in (1, 2):
                    step(2 * i + u, u % 2)
            step(FT - 1, (FT - 1) % 2, last=True)
            high_part(FT - 1)

        @block.vector
        def _(dve):
            def split_in(f, slot):
                dve.wait_ge(wi_high, f + 1)
                nc.vector.tensor_tensor(wi_l[:, slot, :], raw_in[:], wi_h[:, slot, :], ALU.subtract).then_inc(wi_split, 1)

            def split_out(f, slot):
                dve.wait_ge(wo_high, f + 1)
                nc.vector.tensor_tensor(wo_l[:, slot, :], raw_out[:], wo_h[:, slot, :], ALU.subtract).then_inc(wo_split, 1)

            def accumulate(f):
                for s in range(OUTS):
                    o, (t0, tn) = s // 3, TOKEN_CHUNKS[s % 3]
                    dve.wait_ge(out_done, OUTS * f + s + 1)
                    at = out_at + s % 2 * BANK
                    nc.vector.tensor_tensor(acc[:, o, t0:t0 + tn], acc[:, o, t0:t0 + tn], ps[:, at:at + tn],
                                            ALU.add).then_inc(added, 1)

            def hidden(f):
                dve.wait_ge(up_done, f + 1)
                dve.wait_ge(silu_done, f + 1)
                nc.vector.tensor_tensor(hid[:], hid[:], ps[:, up_at:up_at + T], ALU.mult).then_inc(hid_done, 1)
                dve.wait_ge(hid_high, f + 1)
                nc.vector.tensor_tensor(hid_l[:], hid[:], hid_h[:], ALU.subtract).then_inc(hid_split, 1)

            def step(f, slot, last=False):
                hidden(f - 1)
                if not last:
                    split_in(f + 1, 1 - slot)
                split_out(f, slot)
                accumulate(f - 1)

            dve.sem_inc(added, 2)
            split_in(0, 0)
            split_out(0, 0)
            split_in(1, 1)
            with dve.Fori(0, (FT - 2) // 2) as i:
                for u in (1, 2):
                    step(2 * i + u, u % 2)
            step(FT - 1, (FT - 1) % 2, last=True)
            hidden(FT - 1)
            accumulate(FT - 1)


def linear_phase(nc, tag, w_d, n_tiles, xh, xl, chunks, mode, dest, spill=None, reload=None, scale=1.0):
    tokens = sum(n for _, n in chunks)
    with ExitStack() as ctx:
        m = Memory(nc, ctx, tag)
        raw = m.sb("raw", [P, 2, KT * P])
        w_h = m.sb("w_h", [P, 2, KT * P], F32R)
        w_l = m.sb("w_l", [P, 2, KT * P], F32R)
        stage = m.sb("stage", [P, 2, tokens]) if mode == "store" else None
        ps = m.psum()
        loaded = [m.sem(f"loaded{u}") for u in range(2)]
        high, split, product, emptied = m.sem("high"), m.sem("split"), m.sem("product"), m.sem("emptied")
        stored, spilled, reloaded = [m.sem(f"stored{u}") for u in range(2)], m.sem("spilled"), m.sem("reloaded")
        block = ctx.enter_context(nc.Block())

        def steps(engine, step, last=n_tiles):
            step(0, 0, 0, True)
            step(1, 1, 0, True)
            with engine.Fori(1, last // 2) as i:
                step(2 * i, 0, i, False)
                step(2 * i + 1, 1, i, False)
            if last % 2:
                step(last - 1, 0, last // 2, False)

        @block.sync
        def _(sp):
            def move(n, u, half, first):
                if not first:
                    sp.wait_ge(split, n - 1)
                sp.dma_start(raw[:, u, :], w_d[n]).then_inc(loaded[u], 16)
                if reload is not None and first and u == 1:
                    sp.dma_start(dest[:], reload).then_inc(reloaded, 16)
                if spill is not None and first and u == 1:
                    sp.dma_start(spill[1], spill[0]).then_inc(spilled, 16)

            steps(sp, move)
            if spill is not None:
                sp.wait_ge(spilled, 16)

        @block.tensor
        def _(pe):
            def product_of(n, u, half, first):
                pe.wait_ge(split, n + 1)
                pe.wait_ge(emptied, n + 1)
                for k in range(KT):
                    for j, (w, x) in enumerate(((w_h, xh), (w_h, xl), (w_l, xh))):
                        for c, (t0, tn) in enumerate(chunks):
                            at = (3 * u + c) * BANK
                            mm = nc.tensor.matmul(ps[:, at:at + tn], w[:, u, k * P:(k + 1) * P], x[:, k, t0:t0 + tn],
                                                  start=(k == 0 and j == 0), stop=(k == KT - 1 and j == 2))
                mm.then_inc(product, 1)

            steps(pe, product_of)

        @block.scalar
        def _(act):
            def high_part(n, u, half):
                act.wait_ge(loaded[u], 16 * (half + 1))
                nc.scalar.copy(w_h[:, u, :], raw[:, u, :]).then_inc(high, 1)

            def empty(n, u, half, first):
                act.wait_ge(product, n + 1)
                if mode == "store":
                    if not first:
                        act.wait_ge(stored[u], 16 * half)
                    nc.scalar.copy(stage[:, u, :], ps[:, 3 * u * BANK:3 * u * BANK + tokens]).then_inc(emptied, 1)
                    act.wait_ge(emptied, n + 3)
                    act.dma_start(dest[n], stage[:, u, :]).then_inc(stored[u], 16)
                elif mode == "keep":
                    nc.scalar.copy(dest[:, n, :], ps[:, 3 * u * BANK:3 * u * BANK + tokens]).then_inc(emptied, 1)

            def step(n, u, half, first):
                empty(n, u, half, first)
                high_part(n + 2, u, half + 1)

            high_part(0, 0, 0)
            high_part(1, 1, 0)
            steps(act, step, n_tiles - 2)
            empty(n_tiles - 2, n_tiles % 2, (n_tiles - 2) // 2, False)
            empty(n_tiles - 1, (n_tiles - 1) % 2, (n_tiles - 1) // 2, False)
            if mode == "store":
                act.wait_ge(stored[0], 16 * ((n_tiles + 1) // 2))
                act.wait_ge(stored[1], 16 * (n_tiles // 2))

        @block.vector
        def _(dve):
            dve.sem_inc(emptied, 2)

            def low_part(n, u, half, first=False):
                dve.wait_ge(high, n + 1)
                nc.vector.tensor_tensor(w_l[:, u, :], raw[:, u, :], w_h[:, u, :], ALU.subtract).then_inc(split, 1)

            def add(n, u, half, first):
                dve.wait_ge(product, n + 1)
                nc.vector.scalar_tensor_tensor(dest[:, n, :], dest[:, n, :], scale, ps[:, 3 * u * BANK:3 * u * BANK + tokens],
                                               ALU.mult, ALU.add).then_inc(emptied, 1)

            def step(n, u, half, first):
                add(n, u, half, first)
                low_part(n + 2, u, half + 1)

            if mode == "add":
                low_part(0, 0, 0)
                low_part(1, 1, 0)
                if reload is not None:
                    dve.wait_ge(reloaded, 16)
                steps(dve, step, n_tiles - 2)
                add(n_tiles - 2, n_tiles % 2, (n_tiles - 2) // 2, False)
                add(n_tiles - 1, (n_tiles - 1) % 2, (n_tiles - 1) // 2, False)
            else:
                steps(dve, low_part)


def norm_phase(nc, tag, acc, ones, vecs, gain, bias, tokens=T, scale=1.0, xh=None, xl=None, after=1.0, out_d=None):
    steps = tokens // NT
    with ExitStack() as ctx:
        m = Memory(nc, ctx, tag)
        squares = m.sb("squares", [P, 2, KT, NT])
        rstd = m.sb("rstd", [P, 2, NT])
        eps = m.sb("eps", [P, 1])
        ps = m.psum()
        mean_done, centred, squared, var_done = m.sem("mean_done"), m.sem("centred"), m.sem("squared"), m.sem("var_done")
        rooted, rstd_done, scaled, affine_a, affine_v = m.sem("rooted"), m.sem("rstd_done"), m.sem("scaled"), m.sem("affine_a"), m.sem("affine_v")
        high, low, const_set, stored = m.sem("high"), m.sem("low"), m.sem("const_set"), m.sem("stored")
        HALF = KT // 2
        block = ctx.enter_context(nc.Block())

        def tok(s):
            return slice(s * NT, (s + 1) * NT)

        def mean_ps(s):
            return ps[:, s % 2 * BANK:s % 2 * BANK + NT]

        def var_ps(s):
            return ps[:, (2 + s % 2) * BANK:(2 + s % 2) * BANK + NT]

        @block.tensor
        def _(pe):
            def mean(s):
                if s >= 2:
                    pe.wait_ge(centred, s - 1)
                for k in range(KT):
                    mm = nc.tensor.matmul(mean_ps(s), ones[:], acc[:, k, tok(s)], start=(k == 0), stop=(k == KT - 1))
                mm.then_inc(mean_done, 1)

            mean(0)
            for s in range(steps):
                if s + 1 < steps:
                    mean(s + 1)
                pe.wait_ge(squared, s + 1)
                if s >= 2:
                    pe.wait_ge(rooted, s - 1)
                for k in range(KT):
                    mm = nc.tensor.matmul(var_ps(s), ones[:], squares[:, s % 2, k, :], start=(k == 0), stop=(k == KT - 1))
                mm.then_inc(var_done, 1)

        @block.vector
        def _(dve):
            nc.vector.memset(eps[:], LN_EPS / scale ** 2).then_inc(const_set, 1)

            def centre(s):
                dve.wait_ge(mean_done, s + 1)
                nc.vector.tensor_tensor(acc[:, :, tok(s)], acc[:, :, tok(s)],
                                        mean_ps(s).unsqueeze(1).broadcast_to([P, KT, NT]), ALU.subtract).then_inc(centred, 1)

            def normalise(s):
                dve.wait_ge(rooted, s + 1)
                nc.vector.reciprocal(rstd[:, s % 2, :], rstd[:, s % 2, :]).then_inc(rstd_done, 1)
                dve.wait_ge(rstd_done, s + 1)
                dve.wait_ge(squared, s + 1)
                nc.vector.tensor_tensor(acc[:, :, tok(s)], acc[:, :, tok(s)],
                                        rstd[:, s % 2, :].unsqueeze(1).broadcast_to([P, KT, NT]), ALU.mult).then_inc(scaled, 1)
                dve.wait_ge(scaled, s + 1)
                for k in range(HALF, KT):
                    nc.vector.tensor_scalar(acc[:, k, tok(s)], acc[:, k, tok(s)], vecs[:, gain + k:gain + k + 1],
                                            vecs[:, bias + k:bias + k + 1], ALU.mult, ALU.add).then_inc(affine_v, 1)

            def finish(s):
                dve.wait_ge(high, s + 1)
                if s == steps - 1:
                    nc.vector.tensor_tensor(xl[:, :, tok(s)], acc[:, :, tok(s)], xh[:, :, tok(s)], ALU.subtract).then_inc(low, 1)
                if after != 1.0:
                    dve.wait_ge(low, s + 1)
                    nc.vector.tensor_scalar(acc[:, :, tok(s)], acc[:, :, tok(s)], after, None, ALU.mult)

            centre(0)
            for s in range(steps):
                if s + 1 < steps:
                    centre(s + 1)
                normalise(s)
                if s >= 1 and out_d is None:
                    finish(s - 1)
            if out_d is None:
                finish(steps - 1)

        @block.scalar
        def _(act):
            act.wait_ge(const_set, 1)

            def square(s):
                act.wait_ge(centred, s + 1)
                if s >= 2:
                    act.wait_ge(var_done, s - 1)
                nc.scalar.activation(squares[:, s % 2], acc[:, :, tok(s)], ACT.Square).then_inc(squared, 1)

            square(0)
            for s in range(steps):
                act.wait_ge(var_done, s + 1)
                if s >= 2:
                    act.wait_ge(scaled, s - 1)
                nc.scalar.activation(rstd[:, s % 2, :], var_ps(s), ACT.Sqrt, bias=eps[:]).then_inc(rooted, 1)
                if s + 1 < steps:
                    square(s + 1)
                act.wait_ge(scaled, s + 1)
                for k in range(HALF):
                    nc.scalar.activation(acc[:, k, tok(s)], acc[:, k, tok(s)], ACT.Identity,
                                         bias=vecs[:, bias + k:bias + k + 1],
                                         scale=vecs[:, gain + k:gain + k + 1]).then_inc(affine_a, 1)
                if out_d is None:
                    act.wait_ge(affine_v, HALF * (s + 1))
                    act.wait_ge(affine_a, HALF * (s + 1))
                    nc.scalar.copy(xh[:, :, tok(s)], acc[:, :, tok(s)]).then_inc(high, 1)

        if out_d is None:
            @block.gpsimd
            def _(pool):
                for s in range(steps - 1):
                    pool.wait_ge(high, s + 1)
                    nc.gpsimd.tensor_tensor(xl[:, :, tok(s)], acc[:, :, tok(s)], xh[:, :, tok(s)],
                                            ALU.subtract).then_inc(low, 1)
        else:
            @block.sync
            def _(sp):
                for s in range(steps):
                    sp.wait_ge(affine_a, HALF * (s + 1))
                    sp.wait_ge(affine_v, HALF * (s + 1))
                    sp.dma_start(out_d[:, :, tok(s)], acc[:, :, tok(s)]).then_inc(stored, 16)
                sp.wait_ge(stored, 16 * steps)


def gla_prepare_phase(nc, a, proj_d, vecs, v, q_in, k_in, q_st, k_out, decay):
    with ExitStack() as ctx:
        m = Memory(nc, ctx, "glap")
        q, k = m.sb("q", [P, 2, T]), m.sb("k", [P, 2, T])
        low = m.sb("low", [P, T])
        up = m.sb("up", [P, 4 * P])
        keep = m.sb("keep", [P, T])
        b1, b2, run = m.sb("b1", [P, T]), m.sb("b2", [P, T]), m.sb("run", [P, T])
        e = [m.sb(f"e{i}", [P, T]) for i in range(2)] + [run, b2]
        ps = m.psum()
        loaded, v_loaded, logit = m.sem("loaded"), m.sem("v_loaded"), m.sem("logit")
        split, soft, summed, centred, expd = m.sem("split"), m.sem("soft"), m.sem("summed"), m.sem("centred"), m.sem("expd")
        done_v, done_p, step_v, step_a, scaled = m.sem("done_v"), m.sem("done_p"), m.sem("step_v"), m.sem("step_a"), m.sem("scaled")
        units = [(d, t) for d in range(2) for t in range(2)]
        block = ctx.enter_context(nc.Block())

        @block.sync
        def _(sp):
            loads = [(low, proj_d[LOW_TILE]), (up, a["gla_up"]), (keep, a["keep"])]
            loads += [(q[:, t], proj_d[Q_TILE + t]) for t in range(2)] + [(k[:, t], proj_d[K_TILE + t]) for t in range(2)]
            for dst, src in loads:
                sp.dma_start(dst if isinstance(dst, bass.AP) else dst[:], src).then_inc(loaded, 16)
            for t in range(4):
                sp.dma_start(v[:, t], proj_d[V_TILE + t]).then_inc(v_loaded, 16)
            sp.wait_ge(v_loaded, 64)

        @block.tensor
        def _(pe):
            pe.wait_ge(loaded, 16 * 7)
            for n, (d, t) in enumerate(units):
                if n >= 2:
                    pe.wait_ge(step_a, 2 * n - 3)
                for c, (t0, tn) in enumerate(TOKEN_CHUNKS):
                    at = (3 * (n % 2) + c) * BANK
                    mm = nc.tensor.matmul(ps[:, at:at + tn], up[:, (2 * d + t) * P:(2 * d + t + 1) * P],
                                          low[:, t0:t0 + tn], start=True, stop=True)
                mm.then_inc(logit, 1)

        @block.vector
        def _(dve):
            dve.wait_ge(loaded, 16 * 7)
            nc.vector.tensor_scalar(q[:], q[:], GLA_DK ** -0.5, None, ALU.mult).then_inc(scaled, 1)
            dve.wait_ge(scaled, 1)
            for n, (d, t) in enumerate(units):
                bias = vecs[:, GLA_B + 2 * d + t:GLA_B + 2 * d + t + 1]
                z = ps[:, 3 * (n % 2) * BANK:3 * (n % 2) * BANK + T]
                dve.wait_ge(logit, n + 1)
                if n >= 1:
                    dve.wait_ge(expd, 4 * n)
                    dve.wait_ge(done_p, 2 * n)
                    dve.wait_ge(done_v, 2 * n)
                nc.vector.tensor_scalar(b2[:], z, bias, 0.0, ALU.add, ALU.min).then_inc(split, 1)
                dve.wait_ge(soft, n + 1)
                dve.wait_ge(split, n + 1)
                nc.vector.tensor_tensor(b2[:], b2[:], b1[:], ALU.subtract).then_inc(step_v, 1)
                dve.wait_ge(step_v, 3 * n + 1)
                if d == 0:
                    nc.vector.tensor_tensor_scan(run[:], keep[:], b2[:], 0.0, ALU.mult, ALU.add).then_inc(summed, 1)
                else:
                    nc.vector.tensor_tensor_scan(run[:, ::-1], keep[:], b2[:, ::-1], 0.0, ALU.mult, ALU.add).then_inc(summed, 1)
                dve.wait_ge(summed, n + 1)
                chunks = run[:].rearrange("p (c t) -> p c t", t=C)
                end = C - 1 if d == 0 else 0
                last = chunks[:, :, end:end + 1].broadcast_to([P, N_CHUNKS, C])
                nc.vector.scalar_tensor_tensor(b1[:].rearrange("p (c t) -> p c t", t=C), last, -0.5, chunks,
                                               ALU.mult, ALU.add).then_inc(step_v, 1)
                nc.vector.tensor_tensor(b2[:].rearrange("p (c t) -> p c t", t=C), last, chunks,
                                        ALU.subtract).then_inc(step_v, 1)
                dve.wait_ge(expd, 4 * n + 3)
                nc.vector.tensor_tensor(q_in[d][:, t], q[:, t], e[0][:], ALU.mult).then_inc(done_v, 1)
                nc.vector.tensor_tensor(q_st[d][:, t], q[:, t], e[2][:], ALU.mult).then_inc(done_v, 1)

        @block.gpsimd
        def _(pool):
            pool.wait_ge(loaded, 16 * 7)
            for n, (d, t) in enumerate(units):
                pool.wait_ge(expd, 4 * n + 4)
                nc.gpsimd.tensor_tensor(k_in[d][:, t], k[:, t], e[1][:], ALU.mult).then_inc(done_p, 1)
                nc.gpsimd.tensor_tensor(k_out[d][:, t], k[:, t], e[3][:], ALU.mult).then_inc(done_p, 1)

        @block.scalar
        def _(act):
            for n, (d, t) in enumerate(units):
                end = C - 1 if d == 0 else 0
                act.wait_ge(split, n + 1)
                nc.scalar.activation(b1[:], ps[:, 3 * (n % 2) * BANK:3 * (n % 2) * BANK + T], ACT.Abs,
                                     bias=vecs[:, GLA_B + 2 * d + t:GLA_B + 2 * d + t + 1]).then_inc(step_a, 1)
                act.wait_ge(step_a, 2 * n + 1)
                nc.scalar.activation(b1[:], b1[:], ACT.Exp, scale=-1.0).then_inc(step_a, 1)
                act.wait_ge(step_a, 2 * n + 2)
                nc.scalar.activation(b1[:], b1[:], ACT.Ln, bias=1.0).then_inc(soft, 1)
                act.wait_ge(step_v, 3 * n + 3)
                if n >= 1:
                    act.wait_ge(done_v, 2 * n)
                    act.wait_ge(done_p, 2 * n)
                act.wait_ge(summed, n + 1)
                nc.scalar.activation(decay[d][:, t], run[:].rearrange("p (c t) -> p c t", t=C)[:, :, end],
                                     ACT.Exp, scale=1 / GLA_TAU)
                nc.scalar.activation(e[0][:], b1[:], ACT.Exp, scale=1 / GLA_TAU).then_inc(expd, 1)
                nc.scalar.activation(e[1][:], b1[:], ACT.Exp, scale=-1 / GLA_TAU).then_inc(expd, 1)
                act.wait_ge(expd, 4 * n + 1)
                nc.scalar.activation(e[2][:], run[:], ACT.Exp, scale=1 / GLA_TAU).then_inc(expd, 1)
                nc.scalar.activation(e[3][:], b2[:], ACT.Exp, scale=1 / GLA_TAU).then_inc(expd, 1)


def gla_scan_phase(nc, v, q_in, k_in, q_st, k_out, decay, out, consts):
    with ExitStack() as ctx:
        m = Memory(nc, ctx, "glas")
        per_dir = lambda name, shape: [m.sb(f"{name}{d}", shape) for d in range(2)]
        k_pair, qs_pair, s_pair = per_dir("k_pair", [P, 2, 2, C]), per_dir("qs_pair", [P, 2, 2, C]), per_dir("s_pair", [P, 2, 2, C])
        q_now = per_dir("q_now", [P, 2, C])
        v_now, ko_pair = per_dir("v_now", [P, 4, C]), per_dir("ko_pair", [P, 2, 2, C])
        v_rows, kt_pair = per_dir("v_rows", [P, 2, P]), per_dir("kt_pair", [P, 2, 2, C])
        state = per_dir("state", [P, 2, P])
        mark = m.sb("mark", [P, 2])
        ps = m.psum()
        ident, pair_mask = consts["ident"], consts["pair"]
        bank = lambda d, i: ps[:, (4 * d + i) * BANK:(4 * d + i + 1) * BANK]
        V_AT, K_AT, S_AT, O_AT = range(4)
        each = lambda name: [m.sem(f"{name}{d}") for d in range(2)]
        zeroed, paired, staged, turned_v, turned_k, rows_v, rows_k = m.sem("zeroed"), each("paired"), each("staged"), each("turned_v"), each("turned_k"), each("rows_v"), each("rows_k")
        scored, masked, outed, added, taken, updated = each("scored"), each("masked"), each("outed"), each("added"), each("taken"), each("updated")
        cleared, out_zeroed = m.sem("cleared"), m.sem("out_zeroed")
        block = ctx.enter_context(nc.Block())

        def sequences(engine, step, start=None):
            for s, (c0, cn) in enumerate(SEQ_CHUNKS):
                if start is not None:
                    start(s, c0)
                step(c0, (c0, c0 + cn - 1), c0 == 0)
                with engine.Fori(1, cn) as i:
                    step(i + c0, (i + c0, i * -1 + (c0 + cn - 1)), False)

        @block.gpsimd
        def _(pool):
            for d in range(2):
                nc.gpsimd.memset(s_pair[d][:], 0.0).then_inc(zeroed, 1)

            def stage(n, chunk, first):
                for d in range(2):
                    at = bass.ds(chunk[d] * C, C)
                    mask = pair_mask.unsqueeze(1).broadcast_to([P, 2, 2, C])
                    if not first:
                        pool.wait_ge(rows_k[d], n)
                    nc.gpsimd.tensor_copy(v_now[d][:], v[:, :, at]).then_inc(staged[d], 1)
                    nc.gpsimd.tensor_tensor(ko_pair[d][:], k_out[d][:, :, at].unsqueeze(2).broadcast_to([P, 2, 2, C]),
                                            mask, ALU.mult).then_inc(staged[d], 1)
                    if not first:
                        pool.wait_ge(outed[d], n)
                    nc.gpsimd.tensor_copy(q_now[d][:], q_in[d][:, :, at]).then_inc(staged[d], 1)

            sequences(pool, stage)

        @block.tensor
        def _(pe):
            def work(n, chunk, first):
                for d in range(2):
                    pe.wait_ge(staged[d], 3 * n + 2)
                    if not first:
                        pe.wait_ge(updated[d], 2 * n)
                    for p in range(2):
                        mm = nc.tensor.transpose(bank(d, V_AT)[:, p * P:(p + 1) * P],
                                                 v_now[d][:, 2 * p:2 * p + 2].rearrange("p a t -> p (a t)"), ident)
                    mm.then_inc(turned_v[d], 1)
                    for p in range(2):
                        mm = nc.tensor.transpose(bank(d, K_AT)[:, p * P:(p + 1) * P],
                                                 ko_pair[d][:, p].rearrange("p a t -> p (a t)"), ident)
                    mm.then_inc(turned_k[d], 1)
                for d in range(2):
                    pe.wait_ge(staged[d], 3 * n + 3)
                    pe.wait_ge(paired[d], 2 * n + 2)
                    if not first:
                        pe.wait_ge(masked[d], n)
                    for p in range(2):
                        mm = nc.tensor.matmul(bank(d, S_AT)[:, p * C:(p + 1) * C],
                                              k_pair[d][:, p].rearrange("p a t -> p (a t)"), q_now[d][:, p], start=True, stop=True)
                    mm.then_inc(scored[d], 1)
                for d in range(2):
                    pe.wait_ge(rows_v[d], n + 1)
                    pe.wait_ge(rows_k[d], n + 1)
                    for p in range(2):
                        mm = nc.tensor.matmul(bank(d, V_AT)[:, p * P:(p + 1) * P],
                                              kt_pair[d][:, p].rearrange("p a t -> p (a t)"), v_rows[d][:, p], start=True, stop=True)
                    mm.then_inc(taken[d], 1)
                for d in range(2):
                    pe.wait_ge(masked[d], n + 1)
                    if first:
                        pe.wait_ge(cleared, 2)
                    else:
                        pe.wait_ge(added[d], n)
                        pe.wait_ge(updated[d], 2 * n)
                        pe.wait_ge(cleared, 2)
                    for p in range(2):
                        o = bank(d, O_AT)[:, p * P:(p + 1) * P]
                        nc.tensor.matmul(o, v_rows[d][:, p], s_pair[d][:, p].rearrange("p a t -> p (a t)"), start=True, stop=False)
                        mm = nc.tensor.matmul(o, state[d][:, p], qs_pair[d][:, p].rearrange("p a t -> p (a t)"), start=False, stop=True)
                    mm.then_inc(outed[d], 1)

            def start(s, c0):
                pe.wait_ge(cleared, 2 * s + 2)

            sequences(pe, work, start)

        @block.scalar
        def _(act):
            def rows(n, chunk, first):
                for d in range(2):
                    act.wait_ge(turned_v[d], n + 1)
                    if not first:
                        act.wait_ge(outed[d], n)
                    nc.scalar.copy(v_rows[d][:], bank(d, V_AT)[:, 0:2 * P].rearrange("p (q e) -> p q e", e=P)).then_inc(rows_v[d], 1)
                    act.wait_ge(turned_k[d], n + 1)
                    nc.scalar.copy(kt_pair[d][:], bank(d, K_AT)[:, 0:2 * P].rearrange("p (q h e) -> p q h e", h=2, e=C)).then_inc(rows_k[d], 1)

            sequences(act, rows)

        @block.vector
        def _(dve):
            dve.wait_ge(zeroed, 2)
            nc.vector.memset(out[:], 0.0).then_inc(out_zeroed, 1)
            dve.wait_ge(out_zeroed, 1)

            def start(s, c0):
                for d in range(2):
                    if s:
                        dve.wait_ge(updated[d], 2 * c0)
                        dve.wait_ge(outed[d], c0)
                    nc.vector.memset(state[d][:], 0.0).then_inc(cleared, 1)
                dve.wait_ge(cleared, 2 * s + 2)

            def work(n, chunk, first):
                for d in range(2):
                    at = bass.ds(chunk[d] * C, C)
                    mask = pair_mask.unsqueeze(1).broadcast_to([P, 2, 2, C])
                    if not first:
                        dve.wait_ge(outed[d], n)
                    nc.vector.tensor_tensor(k_pair[d][:], k_in[d][:, :, at].unsqueeze(2).broadcast_to([P, 2, 2, C]),
                                            mask, ALU.mult).then_inc(paired[d], 1)
                    nc.vector.tensor_tensor(qs_pair[d][:], q_st[d][:, :, at].unsqueeze(2).broadcast_to([P, 2, 2, C]),
                                            mask, ALU.mult).then_inc(paired[d], 1)
                for d in range(2):
                    dve.wait_ge(scored[d], n + 1)
                    if not first:
                        dve.wait_ge(outed[d], n)
                        dve.wait_ge(masked[d], n)
                    nc.vector.memset(mark[:, d:d + 1], 0.0)
                    causal = consts["causal"][:, 2 * d * C:2 * (d + 1) * C].rearrange("p (a t) -> p a t", t=C).bitcast(U32)
                    for p in range(2):
                        mk = nc.vector.copy_predicated(
                            s_pair[d][:, p], causal,
                            bank(d, S_AT)[:, p * C:(p + 1) * C].unsqueeze(1).broadcast_to([P, 2, C]))
                    mk.then_inc(masked[d], 1)
                for d in range(2):
                    dve.wait_ge(outed[d], n + 1)
                    at = bass.ds(chunk[d] * C, C)
                    if not first:
                        dve.wait_ge(added[1 - d], n)
                    nc.vector.tensor_tensor(out[:, :, at], out[:, :, at],
                                            bank(d, O_AT)[:, 0:4 * C].rearrange("p (h t) -> p h t", t=C), ALU.add).then_inc(added[d], 1)
                    dve.wait_ge(taken[d], n + 1)
                    for p in range(2):
                        nc.vector.scalar_tensor_tensor(state[d][:, p], state[d][:, p], decay[d][:, p, bass.ds(chunk[d], 1)],
                                                       bank(d, V_AT)[:, p * P:(p + 1) * P], ALU.mult, ALU.add).then_inc(updated[d], 1)

            sequences(dve, work, start)


def gla_finish_phase(nc, proj_d, vecs, out, consts):
    with ExitStack() as ctx:
        m = Memory(nc, ctx, "glaf")
        g, sq, rstd = m.sb("g", [P, 4, T]), m.sb("sq", [P, 2, T]), m.sb("rstd", [P, 2, T])
        eps = m.sb("eps", [P, 1])
        ps = m.psum()
        loaded, squared, summed, logged, rooted, gated, eps_set = m.sem("loaded"), m.sem("squared"), m.sem("summed"), m.sem("logged"), m.sem("rooted"), m.sem("gated"), m.sem("eps_set")
        silued, done = m.sem("silued"), m.sem("done")
        block = ctx.enter_context(nc.Block())

        @block.sync
        def _(sp):
            sp.dma_start(g[:], proj_d[G_TILE:G_TILE + 4].rearrange("n p t -> p n t")).then_inc(loaded, 16)

        @block.tensor
        def _(pe):
            for h in range(4):
                pe.wait_ge(squared, h + 1)
                if h >= 2:
                    pe.wait_ge(logged, h - 1)
                for c, (t0, tn) in enumerate(TOKEN_CHUNKS):
                    at = (3 * (h % 2) + c) * BANK
                    mm = nc.tensor.matmul(ps[:, at:at + tn], consts["ones"], sq[:, h % 2, t0:t0 + tn], start=True, stop=True)
                mm.then_inc(summed, 1)

        @block.scalar
        def _(act):
            act.wait_ge(loaded, 16)
            nc.scalar.activation(g[:], g[:], ACT.Silu).then_inc(silued, 1)
            act.wait_ge(eps_set, 1)
            for h in range(4):
                if h >= 2:
                    act.wait_ge(summed, h - 1)
                nc.scalar.activation(sq[:, h % 2], out[:, h], ACT.Square).then_inc(squared, 1)
                act.wait_ge(summed, h + 1)
                if h >= 2:
                    act.wait_ge(done, h - 1)
                nc.scalar.activation(rstd[:, h % 2], ps[:, 3 * (h % 2) * BANK:3 * (h % 2) * BANK + T], ACT.Ln,
                                     bias=eps[:], scale=1 / GLA_DV).then_inc(logged, 1)
                act.wait_ge(logged, h + 1)
                nc.scalar.activation(rstd[:, h % 2], rstd[:, h % 2], ACT.Exp, scale=-0.5).then_inc(rooted, 1)

        @block.vector
        def _(dve):
            nc.vector.memset(eps[:], LN_EPS).then_inc(eps_set, 1)
            dve.wait_ge(silued, 1)
            for h in range(4):
                nc.vector.tensor_scalar(g[:, h], g[:, h], vecs[:, GLA_G + h:GLA_G + h + 1], None, ALU.mult).then_inc(gated, 1)
            for h in range(4):
                dve.wait_ge(squared, h + 1)
                dve.wait_ge(gated, 4 + h)
                nc.vector.tensor_tensor(out[:, h], out[:, h], g[:, h], ALU.mult).then_inc(gated, 1)
                dve.wait_ge(gated, 5 + h)
                dve.wait_ge(rooted, h + 1)
                nc.vector.tensor_tensor(out[:, h], out[:, h], rstd[:, h % 2], ALU.mult).then_inc(done, 1)


def rwkv_prepare_phase(nc, a, proj_d, pack_d, vecs, bonus_d, gate_d, consts):
    with ExitStack() as ctx:
        m = Memory(nc, ctx, "rwp")
        bonus, gate = m.sb("bonus", [P, T]), m.sb("gate", [P, T])
        raw2 = m.sb("raw", [P, 2, 3, T])
        r, kr, vr = (m.sb(n, [P, T]) for n in ("r", "kr", "vr"))
        decay = m.sb("decay", [P, 2, T])
        aa, kk = m.sb("aa", [P, T]), m.sb("kk", [P, T])
        low = m.sb("low", [P, 3, T])
        lora, keep = m.sb("lora", [P, 4 * P]), m.sb("keep", [P, T])
        pack = m.sb("pack", [P, N_CHUNKS, PACK])
        stay, one_less = m.sb("stay", [P, MU_TILES]), m.sb("one_less", [P, 4])
        ps = m.psum()
        sets = [ps[:, 0:T], ps[:, 3 * BANK:3 * BANK + T]]
        small_in, keep_in, lora_in, loaded = m.sem("small_in"), m.sem("keep_in"), m.sem("lora_in"), [m.sem("loaded0"), m.sem("loaded1")]
        stored_a, stored_b, gate_stored, bonus_stored = (m.sem(n) for n in ("stored_a", "stored_b", "gate_stored", "bonus_stored"))
        coef, low_scaled, low_ready = m.sem("coef"), m.sem("low_scaled"), m.sem("low_ready")
        scaled, prev_added, next_added = m.sem("scaled"), m.sem("prev_added"), m.sem("next_added")
        logits, sig_done, gate_done, copied = m.sem("logits"), m.sem("sig_done"), m.sem("gate_done"), m.sem("copied")
        scanned, centred, kk_raw, squared, kk_summed, logged, rooted = (
            m.sem(n) for n in ("scanned", "centred", "kk_raw", "squared", "kk_summed", "logged", "rooted"))
        k_factor, k_packed, clamped, kk_packed, b_packed = (m.sem(n) for n in ("k_factor", "k_packed", "clamped", "kk_packed", "b_packed"))
        rk_done, rk_summed, kept = m.sem("rk_done"), m.sem("rk_summed"), m.sem("kept")
        block = ctx.enter_context(nc.Block())
        view = lambda ap: ap.rearrange("p (c t) -> p c t", t=C)
        part = lambda col: pack[:, :, col:col + C]
        SEQS = ((0, T_PROMPT), (T_PROMPT, T))

        @block.sync
        def _(sp):
            for j, tile in enumerate((DECAY_TILE, LOW_TILE, GATE_TILE)):
                sp.dma_start(raw2[:, 1, j], proj_d[tile]).then_inc(small_in, 16)
            sp.dma_start(lora[:], a["lora"][0]).then_inc(lora_in, 16)

            def load(t):
                for j, tile in enumerate((R_TILE, KR_TILE, VR_TILE)):
                    sp.dma_start(raw2[:, t % 2, j], proj_d[tile + t]).then_inc(loaded[t % 2], 16)

            load(0)
            sp.dma_start(keep[:], a["keep"]).then_inc(keep_in, 16)
            for t in range(4):
                if t < 3:
                    if t == 0:
                        sp.wait_ge(next_added, 6)
                    else:
                        sp.wait_ge(b_packed, t)
                    load(t + 1)
                sp.wait_ge(gate_done, t + 1)
                sp.dma_start(gate_d[:, t], gate[:]).then_inc(gate_stored, 16)
                if t < 3:
                    sp.wait_ge(logits, 4 * (t + 1))
                    sp.dma_start(lora[:], a["lora"][t + 1]).then_inc(lora_in, 16)
                sp.wait_ge(copied, 2 * (t + 1))
                sp.wait_ge(centred, 4 * (t + 1))
                sp.dma_start(pack_d[:, :, t, 0:K_COL].rearrange("c p w -> p c w"), pack[:, :, 0:K_COL]).then_inc(stored_a, 16)
                sp.wait_ge(b_packed, t + 1)
                sp.dma_start(pack_d[:, :, t, K_COL:PACK].rearrange("c p w -> p c w"), pack[:, :, K_COL:PACK]).then_inc(stored_b, 16)
                sp.wait_ge(kept, t + 1)
                sp.dma_start(bonus_d[:, t], bonus[:]).then_inc(bonus_stored, 16)
            for sem in (stored_a, stored_b, gate_stored, bonus_stored):
                sp.wait_ge(sem, 64)

        @block.tensor
        def _(pe):
            pe.wait_ge(low_ready, 2)
            pe.wait_ge(next_added, 6)
            for t in range(4):
                pe.wait_ge(lora_in, 16 * (t + 1))
                if t:
                    pe.wait_ge(kept, t)
                for j, src in enumerate((0, 0, 1, 2)):
                    if j >= 2:
                        pe.wait_ge(sig_done, 3 * t + j - 1)
                    for t0, tn in TOKEN_CHUNKS:
                        mm = nc.tensor.matmul(sets[j % 2][:, t0:t0 + tn], lora[:, j * P:(j + 1) * P], low[:, src, t0:t0 + tn],
                                              start=True, stop=True)
                    mm.then_inc(logits, 1)
                pe.wait_ge(squared, t + 1)
                pe.wait_ge(sig_done, 3 * t + 3)
                for t0, tn in TOKEN_CHUNKS:
                    mm = nc.tensor.matmul(sets[0][:, t0:t0 + tn], consts["head_ones"], decay[:, 0, t0:t0 + tn], start=True, stop=True)
                mm.then_inc(kk_summed, 1)
                pe.wait_ge(rk_done, t + 1)
                pe.wait_ge(gate_done, t + 1)
                for t0, tn in TOKEN_CHUNKS:
                    mm = nc.tensor.matmul(sets[1][:, t0:t0 + tn], consts["head_ones"], decay[:, 1, t0:t0 + tn], start=True, stop=True)
                mm.then_inc(rk_summed, 1)

        @block.scalar
        def _(act):
            act.wait_ge(small_in, 48)
            act.wait_ge(coef, 3)
            for j in range(3):
                nc.scalar.activation(low[:, j], raw2[:, 1, j], ACT.Copy, scale=stay[:, 12 + j:13 + j]).then_inc(low_scaled, 1)
            act.wait_ge(next_added, 6)
            nc.scalar.activation(low[:, 0], low[:, 0], ACT.Tanh).then_inc(low_ready, 1)
            nc.scalar.activation(low[:, 2], low[:, 2], ACT.Sigmoid).then_inc(low_ready, 1)
            for t in range(4):
                raw = raw2[:, t % 2]
                act.wait_ge(loaded[t % 2], 48 * (t // 2 + 1))
                if t:
                    act.wait_ge(kept, t)
                for j, dst in enumerate((r, kr, vr)):
                    nc.scalar.activation(dst[:], raw[:, j], ACT.Copy, scale=stay[:, 4 * j + t:4 * j + t + 1]).then_inc(scaled, 1)
                for j in range(3):
                    act.wait_ge(logits, 4 * t + j + 1)
                    dst = aa[:] if j == 2 else decay[:, j]
                    bias = A0 + t if j == 2 else W0 + 4 * j + t
                    nc.scalar.activation(dst, sets[j % 2], ACT.Sigmoid, bias=vecs[:, bias:bias + 1]).then_inc(sig_done, 1)
                act.wait_ge(logits, 4 * t + 4)
                if t:
                    act.wait_ge(gate_stored, 16 * t)
                nc.scalar.copy(gate[:], sets[1]).then_inc(gate_done, 1)
                act.wait_ge(next_added, 6 * (t + 2))
                if t:
                    act.wait_ge(stored_a, 16 * t)
                nc.scalar.copy(part(R_COL), view(r[:])).then_inc(copied, 1)
                nc.scalar.copy(part(V_COL), view(vr[:])).then_inc(copied, 1)
                act.wait_ge(kk_raw, t + 1)
                act.wait_ge(scanned, 2 * t + 1)
                nc.scalar.activation(decay[:, 0], kk[:], ACT.Square).then_inc(squared, 1)
                act.wait_ge(clamped, t + 1)
                nc.scalar.activation(raw[:, 1], raw[:, 1], ACT.Ln).then_inc(logged, 1)
                act.wait_ge(logged, t + 1)
                nc.scalar.activation(raw[:, 1], raw[:, 1], ACT.Exp, scale=-0.5).then_inc(rooted, 1)

        @block.vector
        def _(dve):
            nc.vector.tensor_tensor(stay[:], vecs[:, MU_PREV:MU_PREV + MU_TILES], vecs[:, MU_NEXT:MU_NEXT + MU_TILES], ALU.add).then_inc(coef, 1)
            nc.vector.tensor_scalar(one_less[:], vecs[:, K_A:K_A + 4], -1.0, 1.0, ALU.mult, ALU.add).then_inc(coef, 1)
            dve.wait_ge(coef, 2)
            nc.vector.tensor_scalar(stay[:], stay[:], -1.0, 1.0, ALU.mult, ALU.add).then_inc(coef, 1)

            def shift(dst, src, col, count):
                for s0, s1 in SEQS:
                    nc.vector.scalar_tensor_tensor(dst[:, s0 + 1:s1], src[:, s0:s1 - 1], vecs[:, MU_PREV + col:MU_PREV + col + 1],
                                                   dst[:, s0 + 1:s1], ALU.mult, ALU.add).then_inc(prev_added, 1)
                dve.wait_ge(prev_added, 2 * (count + 1))
                for s0, s1 in SEQS:
                    nc.vector.scalar_tensor_tensor(dst[:, s0:s1 - 1], src[:, s0 + 1:s1], vecs[:, MU_NEXT + col:MU_NEXT + col + 1],
                                                   dst[:, s0:s1 - 1], ALU.mult, ALU.add).then_inc(next_added, 1)

            dve.wait_ge(small_in, 48)
            for j in range(3):
                dve.wait_ge(low_scaled, j + 1)
                shift(low[:, j], raw2[:, 1, j], 12 + j, j)
            dve.wait_ge(keep_in, 16)
            for t in range(4):
                raw = raw2[:, t % 2]
                dve.wait_ge(loaded[t % 2], 48 * (t // 2 + 1))
                for j, dst in enumerate((r, kr, vr)):
                    dve.wait_ge(scaled, 3 * t + j + 1)
                    shift(dst[:], raw[:, j], 4 * j + t, 3 * (t + 1) + j)
                dve.wait_ge(next_added, 6 * (t + 2))
                run = raw[:, 0]
                for d in range(2):
                    dve.wait_ge(sig_done, 3 * t + d + 1)
                    if d == 0:
                        nc.vector.tensor_tensor_scan(run, keep[:], decay[:, 0], 0.0, ALU.mult, ALU.add).then_inc(scanned, 1)
                    else:
                        dve.wait_ge(centred, 4 * t + 2)
                        nc.vector.tensor_tensor_scan(run[:, ::-1], keep[:], decay[:, 1, ::-1], 0.0, ALU.mult, ALU.add).then_inc(scanned, 1)
                    dve.wait_ge(scanned, 2 * t + d + 1)
                    if t:
                        dve.wait_ge(stored_a, 16 * t)
                    end = C - 1 if d == 0 else 0
                    first = G_COL + d * (C + 1)
                    at, edge = (first + 1, first) if d == 0 else (first, first + C)
                    last = view(run)[:, :, end:end + 1]
                    nc.vector.scalar_tensor_tensor(pack[:, :, at:at + C], last.broadcast_to([P, N_CHUNKS, C]), -0.5, view(run),
                                                   ALU.mult, ALU.add).then_inc(centred, 1)
                    nc.vector.tensor_scalar(pack[:, :, edge:edge + 1], last, -0.5, None, ALU.mult).then_inc(centred, 1)
                nc.vector.tensor_scalar(kk[:], kr[:], vecs[:, K_K + t:K_K + t + 1], None, ALU.mult).then_inc(kk_raw, 1)
                dve.wait_ge(sig_done, 3 * t + 3)
                nc.vector.tensor_scalar(raw[:, 2], aa[:], vecs[:, K_A + t:K_A + t + 1], one_less[:, t:t + 1],
                                        ALU.mult, ALU.add).then_inc(k_factor, 1)
                dve.wait_ge(k_factor, t + 1)
                if t:
                    dve.wait_ge(stored_b, 16 * t)
                nc.vector.tensor_tensor(part(K_COL), view(kr[:]), view(raw[:, 2]), ALU.mult).then_inc(k_packed, 1)
                dve.wait_ge(kk_summed, t + 1)
                nc.vector.tensor_scalar(raw[:, 1], sets[0], KK_EPS * KK_EPS, None, ALU.max).then_inc(clamped, 1)
                dve.wait_ge(k_packed, t + 1)
                dve.wait_ge(scanned, 2 * t + 2)
                nc.vector.scalar_tensor_tensor(view(decay[:, 1]), view(r[:]), vecs[:, R_K + t:R_K + t + 1], part(K_COL),
                                               ALU.mult, ALU.mult).then_inc(rk_done, 1)
                dve.wait_ge(rooted, t + 1)
                nc.vector.tensor_tensor(part(KK_COL), view(kk[:]), view(raw[:, 1]), ALU.mult).then_inc(kk_packed, 1)
                dve.wait_ge(kk_packed, t + 1)
                nc.vector.scalar_tensor_tensor(part(B_COL), part(KK_COL), -1.0, view(aa[:]), ALU.mult, ALU.mult).then_inc(b_packed, 1)
                dve.wait_ge(rk_summed, t + 1)
                dve.wait_ge(copied, 2 * (t + 1))
                dve.wait_ge(b_packed, t + 1)
                if t:
                    dve.wait_ge(bonus_stored, 16 * t)
                nc.vector.tensor_tensor(bonus[:], sets[1], vr[:], ALU.mult).then_inc(kept, 1)


def rwkv_scan_phase(nc, pack_d, out, consts):
    with ExitStack() as ctx:
        m_ = Memory(nc, ctx, "rws")
        per_dir = lambda name, shape: [m_.sb(f"{name}{d}", shape) for d in range(2)]
        per_slot = lambda name, shape: [[m_.sb(f"{name}{d}{u}", shape) for u in range(2)] for d in range(2)]
        PAIR, STACK = [P, 4, 2, C], [P, 4, C]
        pack, decayed, grown = per_dir("pack", [P, 4, PACK]), per_dir("decayed", [P, 4, C + 1]), per_slot("grown", [P, 4, C + 1])
        ar = per_slot("ar", PAIR)
        a_pair, b_rows, k_rows, v_rows, v_stack = (per_slot(n, s) for n, s in (
            ("a_pair", PAIR), ("b_rows", PAIR), ("k_rows", PAIR), ("v_rows", PAIR), ("v_stack", STACK)))
        b_pair, k_pair, v_pair, grown_pair = (per_dir(n, PAIR) for n in ("b_pair", "k_pair", "v_pair", "grown_pair"))
        ab_pair, ak_pair = per_dir("ab_pair", PAIR), per_slot("ak_pair", PAIR)
        rb, rk = per_slot("rb", STACK), per_slot("rk", STACK)
        x, xt_pair, y = per_dir("x", PAIR), per_slot("xt_pair", PAIR), per_dir("y", STACK)
        rhs, u, u_pair = per_dir("rhs", STACK), per_dir("u", STACK), per_dir("u_pair", PAIR)
        h_true, h, h_sum, h_pair = per_dir("h_true", STACK), per_dir("h", STACK), per_dir("h_sum", STACK), per_dir("h_pair", PAIR)
        ps = m_.psum()
        bank = lambda d, i: ps[:, (4 * d + i) * BANK:(4 * d + i + 1) * BANK]
        BX, KX, TURN, ST = range(4)
        as_pair = lambda ap: ap.rearrange("p (q h t) -> p q h t", h=2, t=C)
        as_stack = lambda ap: ap[:, 0:4 * C].rearrange("p (q t) -> p q t", t=C)
        both = lambda ap: ap.unsqueeze(2).broadcast_to(PAIR)
        tiles = lambda ap: ap.unsqueeze(1).broadcast_to([P, 4] + list(ap.shape[1:]))
        flat = lambda ap: ap.rearrange("p h t -> p (h t)")
        by_head = lambda ap: ap.rearrange("p (h t) -> p h t", t=C)
        ident, twice_ident = consts["ident"], consts["twice_ident"]
        stack_ident = twice_ident[:, 0:C]

        def mask(name, d, level=0, width=C):
            at = (level * 2 + d) * width
            return consts[name][:, at:at + width]

        each = lambda name: [m_.sem(f"{name}{d}") for d in range(2)]
        loaded, exps, grown_2, a_2, v_2, a_r, b_2, k_2 = (each(n) for n in ("loaded", "exps", "grown_2", "a_2", "v_2", "a_r", "b_2", "k_2"))
        with_b, with_k, masked, turned, rows, stacked = (each(n) for n in ("with_b", "with_k", "masked", "turned", "rows", "stacked"))
        ly, y_set, xy, x_set, x_turned, xt_set = (each(n) for n in ("ly", "y_set", "xy", "x_set", "x_turned", "xt_set"))
        rhs_done, rhs_set, u_done, u_set, u_2 = (each(n) for n in ("rhs_done", "rhs_set", "u_done", "u_set", "u_2"))
        h_set, h_2, h_done, h_summed, h_next, y_done, y_added = (
            each(n) for n in ("h_set", "h_2", "h_done", "h_summed", "h_next", "y_done", "y_added"))
        zeroed, out_zeroed = m_.sem("zeroed"), m_.sem("out_zeroed")
        block = ctx.enter_context(nc.Block())
        now = lambda d: slice(1, C + 1) if d == 0 else slice(0, C)
        before = lambda d: slice(0, C) if d == 0 else slice(1, C + 1)
        edge = lambda d: slice(0, 1) if d == 0 else slice(C, C + 1)
        N_PROMPT = SEQ_CHUNKS[0][1]
        DIRS = range(2)

        def chunk_of(n, sample):
            return n, n * -1 + (N_CHUNKS + N_PROMPT - 1 if sample else N_PROMPT - 1)

        def steps(engine, step):
            for n in range(N_PROMPT):
                step(n, n % 2, True, False, n + 1 >= N_PROMPT)
            with engine.Fori(N_PROMPT // 2, N_CHUNKS // 2 - 1) as i:
                for slot in range(2):
                    step(2 * i + slot, slot, True, True, True)
            step(N_CHUNKS - 2, 0, True, True, True)
            step(N_CHUNKS - 1, 1, False, True, True)

        def after(engine, sem, value, m, least):
            if not (isinstance(m, int) and m < least):
                engine.wait_ge(sem, value)

        @block.sync
        def _(sp):
            def load(m, sample):
                for d in DIRS:
                    after(sp, b_2[d], m, m, 1)
                    after(sp, k_2[d], m, m, 1)
                    after(sp, v_2[d], m, m, 1)
                    sp.dma_start(pack[d][:], pack_d[chunk_of(m, sample)[d]]).then_inc(loaded[d], 16)

            load(0, False)
            steps(sp, lambda n, slot, more, sample, next_sample: load(n + 1, next_sample) if more else None)

        @block.gpsimd
        def _(pool):
            pair = tiles(consts["pair"])
            for d in DIRS:
                for u_ in range(2):
                    nc.gpsimd.memset(xt_pair[d][u_][:], 0.0).then_inc(zeroed, 1)

            def spread(m, slot):
                for d in DIRS:
                    pool.wait_ge(exps[d], 2 * m + 2)
                    after(pool, k_2[d], m, m, 1)
                    nc.gpsimd.tensor_tensor(grown_pair[d][:], both(grown[d][slot][:, :, now(d)]), pair, ALU.mult).then_inc(grown_2[d], 1)
                for d in DIRS:
                    pool.wait_ge(loaded[d], (m + 1) * 16)
                    after(pool, turned[d], 3 * m, m, 1)
                    nc.gpsimd.tensor_tensor(v_pair[d][:], both(pack[d][:, :, V_COL:V_COL + C]), pair, ALU.mult).then_inc(v_2[d], 1)

            def spread_late(m, slot):
                for d in DIRS:
                    pool.wait_ge(a_r[d], 2 * m + 2)
                    after(pool, y_done[d], m - 1, m, 2)
                    nc.gpsimd.tensor_tensor(a_pair[d][slot][:], both(ar[d][slot][:, :, 0]), pair, ALU.mult).then_inc(a_2[d], 1)
                for d in DIRS:
                    pool.wait_ge(rows[d], 3 * m + 3)
                    nc.gpsimd.tensor_tensor(v_stack[d][slot][:], v_rows[d][slot][:, :, 0], v_rows[d][slot][:, :, 1], ALU.add).then_inc(stacked[d], 1)

            def step(n, slot, more, sample, next_sample):
                if more:
                    spread(n + 1, 1 - slot)
                for d in DIRS:
                    pool.wait_ge(h_set[d], n + 1)
                    after(pool, y_done[d], n, n, 1)
                    nc.gpsimd.tensor_tensor(h_pair[d][:], both(h[d][:]), pair, ALU.mult).then_inc(h_2[d], 1)
                for d in DIRS:
                    pool.wait_ge(u_set[d], n + 1)
                    nc.gpsimd.tensor_tensor(u_pair[d][:], both(u[d][:]), pair, ALU.mult).then_inc(u_2[d], 1)
                if more:
                    spread_late(n + 1, 1 - slot)

            spread(0, 0)
            spread_late(0, 0)
            steps(pool, step)

        @block.tensor
        def _(pe):
            def each_tile(bank_ap, width, lhs, rhs_of, done):
                for q in range(4):
                    mm = nc.tensor.matmul(bank_ap[:, q * width:(q + 1) * width], flat(lhs[:, q]), rhs_of(q), start=True, stop=True)
                mm.then_inc(done, 1)

            def turn(dst, src, done):
                for q in range(4):
                    mm = nc.tensor.transpose(dst[:, q * P:(q + 1) * P], flat(src[:, q]), ident)
                mm.then_inc(done, 1)

            def prepare(m, slot):
                for d in DIRS:
                    pe.wait_ge(b_2[d], m + 1)
                    each_tile(bank(d, BX), P, b_pair[d], lambda q: flat(ar[d][slot][:, q]), with_b[d])
                    pe.wait_ge(k_2[d], m + 1)
                    each_tile(bank(d, KX), P, k_pair[d], lambda q: flat(ar[d][slot][:, q]), with_k[d])
                    after(pe, xt_set[d], 2 * LEVELS * m, m, 1)
                    turn(bank(d, TURN), b_pair[d], turned[d])
                for d in DIRS:
                    after(pe, h_summed[d], m, m, 1)
                    turn(bank(d, ST), k_pair[d], turned[d])
                for d in DIRS:
                    pe.wait_ge(rows[d], 3 * m + 1)
                    pe.wait_ge(v_2[d], m + 1)
                    turn(bank(d, TURN), v_pair[d], turned[d])
                for d in DIRS:
                    pe.wait_ge(masked[d], 4 * m + 2)
                    each_tile(bank(d, BX), C, ab_pair[d], lambda q: stack_ident, ly[d])

            def invert(m, slot):
                for level in range(1, LEVELS):
                    for d in DIRS:
                        pe.wait_ge(x_set[d], m * LEVELS + level)
                        if level == 1:
                            pe.wait_ge(rows[d], 3 * m + 3)
                        turn(bank(d, TURN), x[d], x_turned[d])
                        each_tile(bank(d, BX), C, ab_pair[d], lambda q: x[d][:, q, 0], ly[d])
                    for d in DIRS:
                        pe.wait_ge(y_set[d], m * LEVELS + level + 1)
                        pe.wait_ge(xt_set[d], (m * LEVELS + level) * 2)
                        if level == 1:
                            pe.wait_ge(masked[d], 4 * m + 4)
                        each_tile(bank(d, KX), C, xt_pair[d][slot], lambda q: y[d][:, q], xy[d])
                for d in DIRS:
                    pe.wait_ge(x_set[d], (m + 1) * LEVELS)
                    turn(bank(d, TURN), x[d], x_turned[d])

            def state_first(n, slot):
                for d in DIRS:
                    pe.wait_ge(h_set[d], n + 1)
                    pe.wait_ge(a_2[d], n + 1)
                    pe.wait_ge(stacked[d], n + 1)
                    after(pe, y_added[d], n, n, 1)
                    for q in range(4):
                        o = bank(d, ST)[:, q * C:(q + 1) * C]
                        nc.tensor.matmul(o, flat(ak_pair[d][slot][:, q]), v_stack[d][slot][:, q], start=True, stop=False)
                        mm = nc.tensor.matmul(o, flat(a_pair[d][slot][:, q]), h[d][:, q], start=False, stop=True)
                    mm.then_inc(rhs_done[d], 1)
                for d in DIRS:
                    pe.wait_ge(rhs_set[d], n + 1)
                    pe.wait_ge(xt_set[d], (n + 1) * LEVELS * 2)
                    each_tile(bank(d, ST), C, xt_pair[d][slot], lambda q: rhs[d][:, q], u_done[d])
                for d in DIRS:
                    pe.wait_ge(u_set[d], n + 1)
                    for q in range(4):
                        o = bank(d, ST)[:, q * C:(q + 1) * C]
                        nc.tensor.matmul(o, flat(b_rows[d][slot][:, q]), u[d][:, q], start=True, stop=False)
                        mm = nc.tensor.matmul(o, flat(k_rows[d][slot][:, q]), v_stack[d][slot][:, q], start=False, stop=True)
                    mm.then_inc(h_done[d], 1)

            def state_out(n, slot, more):
                for d in DIRS:
                    if more:
                        pe.wait_ge(rows[d], 3 * (n + 1) + 2)
                    pe.wait_ge(h_2[d], n + 1)
                    pe.wait_ge(u_2[d], n + 1)
                    pe.wait_ge(h_summed[d], n + 1)
                    for q in range(4):
                        o = bank(d, ST)[:, q * C:(q + 1) * C]
                        nc.tensor.matmul(o, flat(h_pair[d][:, q]), ar[d][slot][:, q, 1], start=True, stop=False)
                        nc.tensor.matmul(o, flat(u_pair[d][:, q]), rb[d][slot][:, q], start=False, stop=False)
                        mm = nc.tensor.matmul(o, flat(v_rows[d][slot][:, q]), rk[d][slot][:, q], start=False, stop=True)
                    mm.then_inc(y_done[d], 1)

            def step(n, slot, more, sample, next_sample):
                state_first(n, slot)
                if more:
                    prepare(n + 1, 1 - slot)
                state_out(n, slot, more)
                if more:
                    invert(n + 1, 1 - slot)

            prepare(0, 0)
            invert(0, 0)
            steps(pe, step)

        @block.scalar
        def _(act):
            def halves(dst, src, done):
                for r in range(2):
                    lanes = slice(r * C, (r + 1) * C)
                    nc.scalar.copy(dst[lanes, :, r], as_pair(src)[lanes, :, r]).then_inc(done, 1)

            def exponentials(m, slot):
                for d in DIRS:
                    act.wait_ge(loaded[d], (m + 1) * 16)
                    after(act, b_2[d], m, m, 1)
                    after(act, h_next[d], m, m, 2)
                    g = pack[d][:, :, G_COL + d * (C + 1):G_COL + (d + 1) * (C + 1)]
                    nc.scalar.activation(grown[d][slot][:], g, ACT.Exp, scale=DECAY_UNIT).then_inc(exps[d], 1)
                    nc.scalar.activation(decayed[d][:], g, ACT.Exp, scale=-DECAY_UNIT).then_inc(exps[d], 1)

            def invert(m, slot):
                for j, dst in enumerate((b_rows, k_rows, v_rows)):
                    for d in DIRS:
                        act.wait_ge(turned[d], 3 * m + j + 1)
                        after(act, y_done[d], m - 1, m, 2)
                        nc.scalar.copy(dst[d][slot][:], as_pair(bank(d, ST if dst is k_rows else TURN))).then_inc(rows[d], 1)
                for level in range(LEVELS):
                    for d in DIRS:
                        act.wait_ge(x_turned[d], m * LEVELS + level + 1)
                        halves(xt_pair[d][slot], bank(d, TURN), xt_set[d])

            def step(n, slot, more, sample, next_sample):
                if more:
                    exponentials(n + 1, 1 - slot)
                for d in DIRS:
                    act.wait_ge(rhs_done[d], n + 1)
                    nc.scalar.copy(rhs[d][:], as_stack(bank(d, ST))).then_inc(rhs_set[d], 1)
                for d in DIRS:
                    act.wait_ge(u_done[d], n + 1)
                    nc.scalar.copy(u[d][:], as_stack(bank(d, ST))).then_inc(u_set[d], 1)
                if more:
                    invert(n + 1, 1 - slot)

            act.wait_ge(zeroed, 4)
            exponentials(0, 0)
            invert(0, 0)
            steps(act, step)

        @block.vector
        def _(dve):
            nc.vector.memset(out[:], 0.0).then_inc(out_zeroed, 1)
            dve.wait_ge(out_zeroed, 1)
            for d in DIRS:
                nc.vector.memset(h_true[d][:], 0.0).then_inc(h_next[d], 1)

            def products(m, slot):
                for d in DIRS:
                    dve.wait_ge(exps[d], 2 * m + 2)
                    after(dve, y_done[d], m - 1, m, 2)
                    nc.vector.tensor_tensor(ar[d][slot][:, :, 0], pack[d][:, :, KK_COL:KK_COL + C], decayed[d][:, :, before(d)], ALU.mult).then_inc(a_r[d], 1)
                    nc.vector.tensor_tensor(ar[d][slot][:, :, 1], pack[d][:, :, R_COL:R_COL + C], decayed[d][:, :, now(d)], ALU.mult).then_inc(a_r[d], 1)
                for d in DIRS:
                    dve.wait_ge(a_r[d], 2 * m + 2)
                    dve.wait_ge(grown_2[d], m + 1)
                    after(dve, turned[d], 3 * m, m, 1)
                    nc.vector.tensor_tensor(b_pair[d][:], both(pack[d][:, :, B_COL:B_COL + C]), grown_pair[d][:], ALU.mult).then_inc(b_2[d], 1)
                    nc.vector.tensor_tensor(k_pair[d][:], both(pack[d][:, :, K_COL:K_COL + C]), grown_pair[d][:], ALU.mult).then_inc(k_2[d], 1)

            def before_pair(d, ap):
                return both(ap[:, :, 0]), tiles(by_head(mask("before_pair", d, width=2 * C)))

            def masks_b(m, slot):
                for d in DIRS:
                    dve.wait_ge(with_b[d], m + 1)
                    s = as_pair(bank(d, BX))
                    after(dve, x_turned[d], LEVELS * m, m, 1)
                    nc.vector.tensor_tensor(ab_pair[d][:], *before_pair(d, s), ALU.mult).then_inc(masked[d], 1)
                    nc.vector.tensor_tensor(rb[d][slot][:], s[:, :, 1], tiles(mask("upto", d)), ALU.mult).then_inc(masked[d], 1)

            def masks_k(m, slot):
                for d in DIRS:
                    dve.wait_ge(with_k[d], m + 1)
                    s = as_pair(bank(d, KX))
                    nc.vector.tensor_tensor(ak_pair[d][slot][:], *before_pair(d, s), ALU.mult).then_inc(masked[d], 1)
                    nc.vector.tensor_tensor(rk[d][slot][:], s[:, :, 1], tiles(mask("upto", d)), ALU.mult).then_inc(masked[d], 1)

            def invert_first(m):
                for d in DIRS:
                    dve.wait_ge(ly[d], m * LEVELS + 1)
                    nc.vector.tensor_tensor(y[d][:], as_stack(bank(d, BX)), tiles(mask("level", d)), ALU.mult).then_inc(y_set[d], 1)
                for d in DIRS:
                    dve.wait_ge(y_set[d], m * LEVELS + 1)
                    nc.vector.tensor_tensor(x[d][:], both(y[d][:]), tiles(by_head(twice_ident)), ALU.add).then_inc(x_set[d], 1)

            def invert(m, level):
                for d in DIRS:
                    dve.wait_ge(ly[d], m * LEVELS + level + 1)
                    nc.vector.tensor_tensor(y[d][:], as_stack(bank(d, BX)), tiles(mask("level", d, level)), ALU.mult).then_inc(y_set[d], 1)
                for d in DIRS:
                    dve.wait_ge(xy[d], m * (LEVELS - 1) + level)
                    dve.wait_ge(x_turned[d], m * LEVELS + level)
                    nc.vector.tensor_tensor(x[d][:], x[d][:], both(as_stack(bank(d, KX))), ALU.add).then_inc(x_set[d], 1)

            def step(n, slot, more, sample, next_sample):
                for d in DIRS:
                    dve.wait_ge(h_next[d], n + 1)
                    after(dve, y_done[d], n, n, 1)
                    nc.vector.tensor_tensor(h[d][:], h_true[d][:], grown[d][slot][:, :, edge(d)].broadcast_to(STACK), ALU.mult).then_inc(h_set[d], 1)
                if more:
                    products(n + 1, 1 - slot)
                for d in DIRS:
                    dve.wait_ge(h_done[d], n + 1)
                    nc.vector.tensor_tensor(h_sum[d][:], h[d][:], as_stack(bank(d, ST)), ALU.add).then_inc(h_summed[d], 1)
                    if not sample and next_sample:
                        nc.vector.memset(h_true[d][:], 0.0).then_inc(h_next[d], 1)
                    else:
                        dve.wait_ge(h_summed[d], n + 1)
                        nc.vector.tensor_tensor(h_true[d][:], h_sum[d][:], grown[d][slot][:, :, edge(d)].broadcast_to(STACK),
                                                ALU.mult).then_inc(h_next[d], 1)
                if more:
                    masks_b(n + 1, 1 - slot)
                    invert_first(n + 1)
                    masks_k(n + 1, 1 - slot)
                for d in DIRS:
                    dve.wait_ge(y_done[d], n + 1)
                    after(dve, y_added[1 - d], n, n, 1)
                    at = bass.ds(chunk_of(n, sample)[d] * C, C)
                    nc.vector.tensor_tensor(out[:, :, at], out[:, :, at], as_stack(bank(d, ST)), ALU.add).then_inc(y_added[d], 1)
                if more:
                    for level in range(1, LEVELS):
                        invert(n + 1, level)

            products(0, 0)
            masks_b(0, 0)
            invert_first(0)
            masks_k(0, 0)
            for level in range(1, LEVELS):
                invert(0, level)
            steps(dve, step)


def rwkv_finish_phase(nc, vecs, out, bonus_d, gate_d, consts):
    with ExitStack() as ctx:
        m = Memory(nc, ctx, "rwf")
        sq, rstd, eps = m.sb("sq", [P, 2, T]), m.sb("rstd", [P, 2, T]), m.sb("eps", [P, 1])
        bonus, gate, loaded = m.sb("bonus", [P, 4, T]), m.sb("gate", [P, 4, T]), m.sem("loaded")
        ps = m.psum()
        sets = [ps[:, 0:T], ps[:, 3 * BANK:3 * BANK + T]]
        eps_set, summed, centred, squared, sq_summed, logged, rooted = (
            m.sem(n) for n in ("eps_set", "summed", "centred", "squared", "sq_summed", "logged", "rooted"))
        scaled, affine, raised = m.sem("scaled"), m.sem("affine"), m.sem("raised")
        block = ctx.enter_context(nc.Block())

        @block.sync
        def _(sp):
            sp.dma_start(bonus[:], bonus_d).then_inc(loaded, 16)
            sp.dma_start(gate[:], gate_d).then_inc(loaded, 16)

        @block.tensor
        def _(pe):
            for t in range(4):
                if t:
                    pe.wait_ge(centred, t)
                for t0, tn in TOKEN_CHUNKS:
                    mm = nc.tensor.matmul(sets[0][:, t0:t0 + tn], consts["head_ones"], out[:, t, t0:t0 + tn], start=True, stop=True)
                mm.then_inc(summed, 1)
                pe.wait_ge(squared, t + 1)
                if t:
                    pe.wait_ge(logged, t)
                for t0, tn in TOKEN_CHUNKS:
                    mm = nc.tensor.matmul(sets[1][:, t0:t0 + tn], consts["head_ones"], sq[:, t % 2, t0:t0 + tn], start=True, stop=True)
                mm.then_inc(sq_summed, 1)

        @block.scalar
        def _(act):
            act.wait_ge(eps_set, 1)
            for t in range(4):
                act.wait_ge(centred, t + 1)
                nc.scalar.activation(sq[:, t % 2], out[:, t], ACT.Square).then_inc(squared, 1)
                act.wait_ge(sq_summed, t + 1)
                if t >= 2:
                    act.wait_ge(scaled, t - 1)
                nc.scalar.activation(rstd[:, t % 2], sets[1], ACT.Ln, bias=eps[:], scale=1 / C).then_inc(logged, 1)
                act.wait_ge(logged, t + 1)
                nc.scalar.activation(rstd[:, t % 2], rstd[:, t % 2], ACT.Exp, scale=-0.5).then_inc(rooted, 1)

        @block.vector
        def _(dve):
            nc.vector.memset(eps[:], RWKV_GN_EPS).then_inc(eps_set, 1)

            def centre(t):
                dve.wait_ge(summed, t + 1)
                nc.vector.scalar_tensor_tensor(out[:, t], sets[0], -1 / C, out[:, t], ALU.mult, ALU.add).then_inc(centred, 1)

            def norm(t):
                dve.wait_ge(rooted, t + 1)
                nc.vector.tensor_tensor(out[:, t], out[:, t], rstd[:, t % 2], ALU.mult).then_inc(scaled, 1)
                dve.wait_ge(scaled, t + 1)
                nc.vector.tensor_scalar(out[:, t], out[:, t], vecs[:, LNX_G + t:LNX_G + t + 1], vecs[:, LNX_B + t:LNX_B + t + 1],
                                        ALU.mult, ALU.add).then_inc(affine, 1)
                dve.wait_ge(affine, t + 1)
                nc.vector.tensor_tensor(out[:, t], out[:, t], bonus[:, t], ALU.add).then_inc(raised, 1)
                dve.wait_ge(raised, t + 1)
                nc.vector.tensor_tensor(out[:, t], out[:, t], gate[:, t], ALU.mult)

            centre(0)
            dve.wait_ge(loaded, 32)
            for t in range(1, 4):
                centre(t)
                norm(t - 1)
            norm(3)


def split_phase(nc, acc, xh, xl):
    with ExitStack() as ctx:
        m = Memory(nc, ctx, "split")
        high = m.sem("high")
        block = ctx.enter_context(nc.Block())

        @block.scalar
        def _(act):
            for k in range(KT):
                nc.scalar.copy(xh[:, k, :], acc[:, k, :]).then_inc(high, 1)

        @block.vector
        def _(dve):
            for k in range(KT):
                dve.wait_ge(high, k + 1)
                nc.vector.tensor_tensor(xl[:, k, :], acc[:, k, :], xh[:, k, :], ALU.subtract)


def attention_phase(nc, q, kv_d, xh, xl, ident):
    HEADS, M = 4, 256
    SCALE = 256.0 ** -0.5
    with ExitStack() as ctx:
        m = Memory(nc, ctx, "attn")
        keys = m.sb("keys", [P, KT, 2 * M])
        values = m.sb("values", [P, 4, D])
        q_now = m.sb("q_now", [P, KT, P])
        probs, probs_t = m.sb("probs", [P, HEADS, M]), m.sb("probs_t", [P, 2 * HEADS, P])
        top, neg, total, inverse = (m.sb(n, [P, HEADS]) for n in ("top", "neg", "total", "inverse"))
        ps = m.psum()
        v_raw = [probs[:].rearrange("p h m -> p (h m)")[:, 0:2 * M], probs[:].rearrange("p h m -> p (h m)")[:, 2 * M:4 * M]]
        S_AT, T_AT, O_AT = 0, 2 * BANK, 4 * BANK
        keys_in, v_in = m.sem("keys_in"), [m.sem("v_in0"), m.sem("v_in1")]
        v_turned, v_set = m.sem("v_turned"), m.sem("v_set")
        staged, scored, topped, negated, expd, inverted, normed = (
            m.sem(n) for n in ("staged", "scored", "topped", "negated", "expd", "inverted", "normed"))
        turned, t_set, outed, high, low = (m.sem(n) for n in ("turned", "t_set", "outed", "high", "low"))
        block = ctx.enter_context(nc.Block())
        heads = lambda ap: ap.rearrange("p (h m) -> p h m", h=HEADS)

        N, N0 = T // P, T_PROMPT // P

        def tiles(engine, begin, end):
            begin(0, 0, True)
            for n in range(N0):
                begin(n + 1, int(n + 1 >= N0), False)
                end(n, 0, n == 0)
            with engine.Fori(N0, N - 1) as n:
                begin(n + 1, 1, False)
                end(n, 1, False)
            end(N - 1, 1, False)

        @block.sync
        def _(sp):
            sp.dma_start(keys[:], kv_d[0:KT].rearrange("n p m -> p n m")).then_inc(keys_in, 16)
            for j in range(KT):
                if j >= 2:
                    sp.wait_ge(v_turned, j - 1)
                sp.dma_start(v_raw[j % 2], kv_d[KT + j]).then_inc(v_in[j % 2], 16)

        @block.gpsimd
        def _(pool):
            def stage(n, s, first):
                if not first:
                    pool.wait_ge(scored, n)
                nc.gpsimd.tensor_copy(q_now[:], q[:, :, bass.ds(n * P, P)]).then_inc(staged, 1)

            tiles(pool, stage, lambda n, s, first: None)

        @block.tensor
        def _(pe):
            for j in range(KT):
                pe.wait_ge(v_in[j % 2], 16 * (j // 2 + 1))
                if j >= 2:
                    pe.wait_ge(v_set, j - 1)
                for i in range(4):
                    mm = nc.tensor.transpose(ps[:, j % 2 * BANK + i * P:j % 2 * BANK + (i + 1) * P], v_raw[j % 2][:, i * P:(i + 1) * P], ident)
                mm.then_inc(v_turned, 1)
            pe.wait_ge(v_set, KT)
            pe.wait_ge(keys_in, 16)

            def score(n, s, first):
                pe.wait_ge(staged, n + 1)
                if not first:
                    pe.wait_ge(expd, 4 * n)
                for h in range(HEADS):
                    for j in range(2):
                        mm = nc.tensor.matmul(ps[:, S_AT + h * M:S_AT + (h + 1) * M], q_now[:, 2 * h + j],
                                              keys[:, 2 * h + j, s * M:(s + 1) * M], start=(j == 0), stop=(j == 1))
                mm.then_inc(scored, 1)

            def answer(n, s, first):
                pe.wait_ge(normed, n + 1)
                if not first:
                    pe.wait_ge(t_set, n)
                for h in range(HEADS):
                    for j in range(2):
                        at = T_AT + (2 * h + j) * P
                        mm = nc.tensor.transpose(ps[:, at:at + P], probs[:, h, j * P:(j + 1) * P], ident)
                mm.then_inc(turned, 1)
                pe.wait_ge(t_set, n + 1)
                if not first:
                    pe.wait_ge(low, n)
                for o in range(KT):
                    for j in range(2):
                        mm = nc.tensor.matmul(ps[:, O_AT + o * P:O_AT + (o + 1) * P], values[:, 2 * s + j, o * P:(o + 1) * P],
                                              probs_t[:, o // 2 * 2 + j], start=(j == 0), stop=(j == 1))
                mm.then_inc(outed, 1)

            tiles(pe, score, answer)

        @block.scalar
        def _(act):
            for j in range(KT):
                act.wait_ge(v_turned, j + 1)
                nc.scalar.copy(values[:, :, j * P:(j + 1) * P], ps[:, j % 2 * BANK:(j % 2 + 1) * BANK].rearrange("p (i t) -> p i t", i=4)).then_inc(v_set, 1)

            def exponentials(n, s, first):
                act.wait_ge(negated, n + 1)
                if first:
                    act.wait_ge(v_turned, KT)
                for h in range(HEADS):
                    nc.scalar.activation(probs[:, h], ps[:, S_AT + h * M:S_AT + (h + 1) * M], ACT.Exp, bias=neg[:, h:h + 1],
                                         scale=SCALE, accum_out=total[:, h:h + 1]).then_inc(expd, 1)

            def turned_out(n, s, first):
                act.wait_ge(turned, n + 1)
                if not first:
                    act.wait_ge(outed, n)
                nc.scalar.copy(probs_t[:], ps[:, T_AT:T_AT + 2 * BANK].rearrange("p (o t) -> p o t", t=P)).then_inc(t_set, 1)

            def high_part(n, s, first):
                act.wait_ge(outed, n + 1)
                nc.scalar.copy(xh[:, :, bass.ds(n * P, P)], ps[:, O_AT:O_AT + 2 * BANK].rearrange("p (o t) -> p o t", t=P)).then_inc(high, 1)

            def begin(n, s, first):
                if not first:
                    turned_out(n - 1, s, isinstance(n, int) and n == 1)
                exponentials(n, s, first)

            def end(n, s, first):
                if isinstance(n, int) and n == N - 1:
                    turned_out(n, s, False)
                high_part(n, s, first)

            tiles(act, begin, end)

        @block.vector
        def _(dve):
            def softmax(n, s, first):
                dve.wait_ge(scored, n + 1)
                nc.vector.tensor_reduce(top[:], heads(ps[:, S_AT:S_AT + 2 * BANK]), mybir.AxisListType.X, ALU.max).then_inc(topped, 1)
                dve.wait_ge(topped, n + 1)
                nc.vector.tensor_scalar(neg[:], top[:], -SCALE, None, ALU.mult).then_inc(negated, 1)
                dve.wait_ge(expd, 4 * n + 4)
                nc.vector.reciprocal(inverse[:], total[:]).then_inc(inverted, 1)
                dve.wait_ge(inverted, n + 1)
                nc.vector.tensor_tensor(probs[:], probs[:], inverse[:].unsqueeze(2).broadcast_to([P, HEADS, M]), ALU.mult).then_inc(normed, 1)

            def low_part(n, s, first):
                dve.wait_ge(high, n + 1)
                at = bass.ds(n * P, P)
                nc.vector.tensor_tensor(xl[:, :, at], ps[:, O_AT:O_AT + 2 * BANK].rearrange("p (o t) -> p o t", t=P), xh[:, :, at],
                                        ALU.subtract).then_inc(low, 1)

            tiles(dve, softmax, low_part)


def memory_phases(nc, a, vecs, kv_d):
    with ExitStack() as ctx:
        m = Memory(nc, ctx, "mem")
        mem, mh, ml = m.sb("mem", [P, KT, MEM_T]), m.sb("mh", [P, KT, MEM_T], F32R), m.sb("ml", [P, KT, MEM_T], F32R)
        ones = m.sb("ones", [P, P])
        with ExitStack() as c2:
            loaded = Memory(nc, c2, "memload").sem("loaded")
            block = c2.enter_context(nc.Block())

            @block.sync
            def _(sp):
                sp.dma_start(mem[:], a["mem"]).then_inc(loaded, 16)
                sp.wait_ge(loaded, 16)

            @block.vector
            def _(dve):
                nc.vector.memset(ones[:], 1.0 / D)

        norm_phase(nc, "memln", mem, ones, vecs, VEC["mem_ln_g"], VEC["mem_ln_b"], tokens=MEM_T, xh=mh, xl=ml)
        linear_phase(nc, "kv", a["ca_w_kv"], 2 * KT, mh, ml, ((0, MEM_T),), "store", kv_d)


def mix_phases(nc, a, proj_d, pack_d, side_d, vecs, mix_o, mix_y):
    with ExitStack() as mixing:
        const_sb = Memory(nc, mixing, "mix").sb("consts", [P, a["consts"].shape[1]])
        load_constants(nc, a, const_sb)
        consts = {n: const_sb[:, at:at + w] for n, (at, w) in CONST.items()}
        consts["pair"] = consts["pair"].rearrange("p (a t) -> p a t", t=C)
        with ExitStack() as ctx:
            m = Memory(nc, ctx, "gla")
            v = m.sb("v", [P, 4, T])
            q_in, k_in, q_st, k_out = ([m.sb(f"{n}{d}", [P, 2, T]) for d in range(2)] for n in ("q_in", "k_in", "q_st", "k_out"))
            decay = [m.sb(f"decay{d}", [P, 2, N_CHUNKS]) for d in range(2)]
            gla_prepare_phase(nc, a, proj_d, vecs, v, q_in, k_in, q_st, k_out, decay)
            gla_scan_phase(nc, v, q_in, k_in, q_st, k_out, decay, mix_o, consts)
        gla_finish_phase(nc, proj_d, vecs, mix_o, consts)
        rwkv_prepare_phase(nc, a, proj_d, pack_d, vecs, side_d[0], side_d[1], consts)
        rwkv_scan_phase(nc, pack_d, mix_y, consts)
        rwkv_finish_phase(nc, vecs, mix_y, side_d[0], side_d[1], consts)


def build(nc, a, out_d):
    proj_d = nc.dram_tensor("proj", (MIX_TILES, P, T), F32, kind="Internal").ap()
    resid_d = nc.dram_tensor("resid", (P, KT, T), F32, kind="Internal").ap()
    pack_d = nc.dram_tensor("pack", (N_CHUNKS, P, 4, PACK), F32, kind="Internal").ap()
    side_d = nc.dram_tensor("side", (2, P, 4, T), F32, kind="Internal").ap()
    kv_d = nc.dram_tensor("kv", (2 * KT, P, MEM_T), F32, kind="Internal").ap()
    with ExitStack() as ctx:
        m = Memory(nc, ctx, "main")
        vecs = m.sb("vecs", [P, a["vecs"].shape[1]])
        mean_ones = m.sb("mean_ones", [P, P])
        acc = m.sb("acc", [P, KT, T])
        set_ones(nc, mean_ones)
        with ExitStack() as parts:
            mp = Memory(nc, parts, "x1")
            xh, xl = mp.sb("xh", [P, KT, T], F32R), mp.sb("xl", [P, KT, T], F32R)
            load_phase(nc, a["x"], a["vecs"], acc, xh, xl, vecs)
            ffn_phase(nc, "ffn1", a["ffn1_w_in"], a["ffn1_w_out"], xh, xl, acc)
            norm_phase(nc, "ln1", acc, mean_ones, vecs, VEC["ln_ffn1_g"], VEC["ln_ffn1_b"], scale=0.5, xh=xh, xl=xl)
            linear_phase(nc, "mixin", a["mix_w_in"], MIX_TILES, xh, xl, TOKEN_CHUNKS, "store", proj_d, spill=(acc[:], resid_d))
        mix_phases(nc, a, proj_d, pack_d, side_d, vecs, acc[:, 0:4], acc[:, 4:8])
        memory_phases(nc, a, vecs, kv_d)
        with ExitStack() as parts:
            mp = Memory(nc, parts, "x2")
            xh, xl = mp.sb("xh", [P, KT, T], F32R), mp.sb("xl", [P, KT, T], F32R)
            split_phase(nc, acc, xh, xl)
            linear_phase(nc, "mixout", a["mix_w_out"], KT, xh, xl, TOKEN_CHUNKS, "add", acc, reload=resid_d, scale=ALPHA)
            norm_phase(nc, "ln2", acc, mean_ones, vecs, VEC["ln_mix_g"], VEC["ln_mix_b"], xh=xh, xl=xl)
            with ExitStack() as queries:
                mq = Memory(nc, queries, "attq")
                ident = mq.sb("ident", [P, P])
                q = mq.sb("q", [P, KT, T])
                load_ident(nc, a, ident)
                linear_phase(nc, "wq", a["ca_w_q"], KT, xh, xl, TOKEN_CHUNKS, "keep", q)
                attention_phase(nc, q, kv_d, xh, xl, ident[:])
            linear_phase(nc, "wo", a["ca_w_o"], KT, xh, xl, TOKEN_CHUNKS, "add", acc, scale=ALPHA)
            norm_phase(nc, "ln3", acc, mean_ones, vecs, VEC["ln_ca_g"], VEC["ln_ca_b"], xh=xh, xl=xl, after=2 * ALPHA)
            ffn_phase(nc, "ffn2", a["ffn2_w_in"], a["ffn2_w_out"], xh, xl, acc)
            norm_phase(nc, "ln4", acc, mean_ones, vecs, VEC["ln_ffn2_g"], VEC["ln_ffn2_b"], scale=0.5, out_d=out_d)


def load_constants(nc, a, const_sb):
    with ExitStack() as ctx:
        m = Memory(nc, ctx, "const")
        loaded = m.sem("loaded")
        block = ctx.enter_context(nc.Block())

        @block.sync
        def _(sp):
            sp.dma_start(const_sb[:], a["consts"]).then_inc(loaded, 16)
            sp.wait_ge(loaded, 16)


def load_ident(nc, a, ident):
    with ExitStack() as ctx:
        loaded = Memory(nc, ctx, "ident").sem("loaded")
        block = ctx.enter_context(nc.Block())
        at, w = CONST["ident"]

        @block.sync
        def _(sp):
            sp.dma_start(ident[:], a["consts"][:, at:at + w]).then_inc(loaded, 16)
            sp.wait_ge(loaded, 16)


def set_ones(nc, ones):
    with ExitStack() as ctx:
        block = ctx.enter_context(nc.Block())

        @block.vector
        def _(dve):
            nc.vector.memset(ones[:], 1.0 / D)


def constant_table():
    row, tok = np.arange(P)[:, None], np.arange(C)[None, :]
    own = (row // C == np.arange(2)[None, :]).astype(np.float32)
    pair = np.repeat(own, C, 1)
    s = row % C
    upto = [s <= tok, s >= tok]
    before = [s < tok, s > tok]
    levels = []
    for level in range(LEVELS):
        b = 2 ** level
        levels += [(s // b % 2 == 1) & (tok // b == s // b - 1), (s // b % 2 == 0) & (tok // b == s // b + 1)]
    parts = {"ident": np.eye(P), "pair": pair, "ones": np.ones((P, P)), "head_ones": own @ own.T, "twice_ident": np.tile(s == tok, (1, 2)),
             "causal": np.concatenate([pair * np.tile(b, (1, 2)) for b in upto], 1),
             "before_pair": np.concatenate([pair * np.tile(b, (1, 2)) for b in before], 1),
             "upto": np.concatenate(upto, 1), "level": np.concatenate(levels, 1)}
    return {n: v.astype(np.float32) for n, v in parts.items()}


CONST = {}
for _name, _value in constant_table().items():
    CONST[_name] = (sum(w for _, w in CONST.values()), _value.shape[1])


def feature_major(x):
    t, d = x.shape
    return np.ascontiguousarray(x.T.reshape(d // P, P, t).transpose(1, 0, 2))


def column(v):
    return v.reshape(-1, P).T


def output_tiles(w):
    k, n = w.shape
    return w.reshape(k // P, P, n // P, P).transpose(2, 1, 0, 3).reshape(n // P, P, (k // P) * P)


def lay_out(i):
    g = {n: np.asarray(v) for n, v in i.items()}
    out = {"x": feature_major(np.concatenate([g["x_prompt"][0], g["x_sample"][0]], 0)),
           "vecs": np.concatenate([column(g[n][0]) for n in VEC_NAMES], 1)}
    for f in ("ffn1", "ffn2"):
        w = g[f + "_w_in"][0]
        out[f + "_w_in"] = np.concatenate([output_tiles(w[:, :D_FF]), output_tiles(w[:, D_FF:])], 2)
        out[f + "_w_out"] = g[f + "_w_out"][0].reshape(FT, P, D)
    out["mem"] = feature_major(np.concatenate([g["mem_prompt"][0], g["mem_sample"][0]], 0))
    for n in ("mix_w_out", "ca_w_q", "ca_w_kv", "ca_w_o"):
        out[n] = output_tiles(g[n][0])
    def mu_columns(v):
        rkv, wd, ad, gd = v[:1536], v[1536:1664], v[1664:1728], v[1728:]
        return column(np.concatenate([rkv, wd, ad, np.zeros(64, v.dtype), gd]))

    out["vecs"] = np.concatenate(
        [out["vecs"]] + [column(g[n][0]) for n in ("gla_gate_b_fwd", "gla_gate_b_bwd", "gla_norm_g")]
        + [mu_columns(g[n][0]) for n in ("rwkv_mu_prev", "rwkv_mu_next")]
        + [column(g[n][0].reshape(-1)) for n in ("rwkv_w0_fwd", "rwkv_w0_bwd", "rwkv_a0", "rwkv_k_k", "rwkv_k_a", "rwkv_r_k",
                                                 "rwkv_lnx_g", "rwkv_lnx_b")], 1)
    lora = np.zeros((4, P, 4, P), g["rwkv_g_up"].dtype)
    for j, (n, row) in enumerate((("rwkv_w_up_fwd", 0), ("rwkv_w_up_bwd", 64), ("rwkv_a_up", 0), ("rwkv_g_up", 0))):
        w = g[n][0]
        lora[:, row:row + w.shape[0], j] = w.reshape(w.shape[0], 4, P).transpose(1, 0, 2)
    out["lora"] = lora.reshape(4, P, 4 * P)
    w = g["mix_w_in"][0]
    starts = np.cumsum([0, 256, 256, 512, 512, 16, 16, 512, 512, 512, 64, 64, 64, 128])
    q, k, v, gg, gdf, gdb, r, kr, vr, wdf, wdb, ad, gd = (w[:, x:y] for x, y in zip(starts[:-1], starts[1:]))
    pad = np.zeros((D, 32), w.dtype)
    out["mix_w_in"] = output_tiles(np.concatenate([q, k, v, gg, r, kr, vr, wdf, wdb, ad, gdf, gdb, pad, gd], 1))
    up = np.zeros((P, 4 * P), w.dtype)
    up[64:80, :2 * P] = g["gla_gate_up_fwd"][0]
    up[80:96, 2 * P:] = g["gla_gate_up_bwd"][0]
    out["gla_up"] = up
    out["consts"] = np.concatenate(list(constant_table().values()), 1)
    out["keep"] = np.tile((np.arange(T) % C != 0).astype(np.float32), (P, 1))
    return {n: np.ascontiguousarray(v) for n, v in out.items()}


def kernel(**inputs):
    import concourse.bacc as bacc
    from concourse.bass_utils import run_bass_kernel_spmd as run

    nc = bacc.Bacc("TRN2", target_bir_lowering=False, num_devices=1)
    arrays = {n + "_dram": v for n, v in lay_out(inputs).items()}
    args = {n[:-5]: nc.dram_tensor(n, v.shape, F32, kind="ExternalInput").ap() for n, v in arrays.items()}
    out_d = nc.dram_tensor("y_dram", (P, KT, T), F32, kind="ExternalOutput").ap()
    build(nc, args, out_d)
    y = run(nc, [arrays], core_ids=[0]).results[0]["y_dram"]
    y = y.transpose(2, 1, 0).reshape(T, D)
    return y[None, :T_PROMPT], y[None, T_PROMPT:]
```

```python
from contextlib import ExitStack

import numpy as np

import concourse.bass as bass
from concourse import mybir

ALU = mybir.AluOpType
ACT = mybir.ActivationFunctionType
F32 = mybir.dt.float32
F32R = mybir.dt.float32r
U32 = mybir.dt.uint32

P = 128
D = 1024
KT = D // P
T_PROMPT, T_SAMPLE = 256, 1024
T = T_PROMPT + T_SAMPLE
D_FF = 2816
FT = D_FF // P
BANK = 512
TOKEN_CHUNKS = ((0, 512), (512, 512), (1024, 256))
ALPHA = 2.0 ** 0.25
LN_EPS = 1e-5
NT = 256

GLA_DK, GLA_DV, GLA_TAU = 64, 128, 16.0
C = 64
N_CHUNKS = T // C
SEQ_CHUNKS = ((0, T_PROMPT // C), (T_PROMPT // C, T_SAMPLE // C))
Q_TILE, K_TILE, V_TILE, G_TILE = 0, 2, 4, 8
R_TILE, KR_TILE, VR_TILE = 12, 16, 20
DECAY_TILE, LOW_TILE, GATE_TILE = 24, 25, 26
MIX_TILES = 27
RWKV_GN_EPS = 64e-5
KK_EPS = 1e-12
LEVELS = 6
DECAY_UNIT = float(np.exp(-0.5))
R_COL, V_COL, G_COL = 0, C, 2 * C
K_COL = G_COL + 2 * (C + 1)
KK_COL, B_COL, PACK = K_COL + C, K_COL + 2 * C, K_COL + 3 * C
MEM_T = 512

VEC_NAMES = ("ln_ffn1_g", "ln_ffn1_b", "ln_mix_g", "ln_mix_b", "mem_ln_g", "mem_ln_b",
             "ln_ca_g", "ln_ca_b", "ln_ffn2_g", "ln_ffn2_b")
VEC = {n: KT * i for i, n in enumerate(VEC_NAMES)}
GLA_B = KT * len(VEC_NAMES)
GLA_G = GLA_B + 4
MU_TILES = 15
MU_PREV = GLA_G + 4
MU_NEXT = MU_PREV + MU_TILES
W0 = MU_NEXT + MU_TILES
A0, K_K, K_A, R_K, LNX_G, LNX_B = (W0 + 8 + 4 * i for i in range(6))


class Memory:

    def __init__(self, nc, ctx, tag):
        self.nc, self.ctx, self.tag, self.sems = nc, ctx, tag, []
        ctx.callback(self.clear_semaphores)

    def clear_semaphores(self):
        if self.sems:
            with self.nc.Block() as block:
                @block.sync
                def _(sp):
                    for s in self.sems:
                        sp.sem_clear(s)

    def sb(self, name, shape, dt=F32):
        return self.ctx.enter_context(self.nc.sbuf_tensor(f"{self.tag}_{name}", shape, dt))

    def psum(self):
        return self.ctx.enter_context(self.nc.psum_tensor(f"{self.tag}_psum", [P, 8 * BANK], F32))

    def sem(self, name):
        s = self.ctx.enter_context(self.nc.semaphore(f"{self.tag}_{name}"))
        self.sems.append(s)
        return s


class LinearWeights:

    def __init__(self, nc, ctx, tag, w_d):
        m = Memory(nc, ctx, tag + "_w")
        self.tiles, self.raw = w_d, m.sb("raw", [P, 2, KT * P])
        self.loaded = [m.sem(f"loaded{u}") for u in range(2)]

    def start(self, engine):
        for u in range(2):
            engine.dma_start(self.raw[:, u, :], self.tiles[u]).then_inc(self.loaded[u], 16)


class FfnWeights:

    def __init__(self, nc, ctx, tag, w_in_d, w_out_d):
        m = Memory(nc, ctx, tag + "_w")
        self.w_in, self.w_out = w_in_d, w_out_d
        self.raw_in, self.raw_out = m.sb("raw_in", [P, 2 * KT * P]), m.sb("raw_out", [P, D])
        self.in_loaded, self.out_loaded = m.sem("in_loaded"), m.sem("out_loaded")

    def start(self, engine):
        engine.dma_start(self.raw_in[:], self.w_in[0]).then_inc(self.in_loaded, 16)
        engine.dma_start(self.raw_out[:], self.w_out[0]).then_inc(self.out_loaded, 16)


def load_phase(nc, x_d, vec_d, x32, xh, xl, vecs, weights):
    with ExitStack() as ctx:
        m = Memory(nc, ctx, "load")
        x_in = [m.sem(f"x_in{k}") for k in range(KT)]
        vec_in, high, low = m.sem("vec_in"), m.sem("high"), m.sem("low")
        block = ctx.enter_context(nc.Block())

        @block.sync
        def _(sp):
            for k in range(KT):
                sp.dma_start(x32[:, k, :], x_d[:, k, :]).then_inc(x_in[k], 16)
            sp.dma_start(vecs[:], vec_d).then_inc(vec_in, 16)
            weights.start(sp)
            sp.wait_ge(vec_in, 16)

        @block.scalar
        def _(act):
            for k in range(KT):
                act.wait_ge(x_in[k], 16)
                nc.scalar.copy(xh[:, k, :], x32[:, k, :]).then_inc(high, 1)

        @block.vector
        def _(dve):
            for k in range(KT):
                dve.wait_ge(high, k + 1)
                nc.vector.tensor_tensor(xl[:, k, :], x32[:, k, :], xh[:, k, :], ALU.subtract).then_inc(low, 1)
                dve.wait_ge(low, k + 1)
                nc.vector.tensor_scalar(x32[:, k, :], x32[:, k, :], 2 * ALPHA, None, ALU.mult)


def ffn_phase(nc, tag, weights, xh, xl, acc):
    with ExitStack() as ctx:
        m = Memory(nc, ctx, tag)
        raw_in, raw_out, in_loaded, out_loaded = weights.raw_in, weights.raw_out, weights.in_loaded, weights.out_loaded
        wi_h = m.sb("wi_h", [P, 2, 2 * KT * P], F32R)
        wi_l = m.sb("wi_l", [P, 2, 2 * KT * P], F32R)
        wo_h = m.sb("wo_h", [P, 2, D], F32R)
        wo_l = m.sb("wo_l", [P, 2, D], F32R)
        hid = m.sb("hid", [P, T])
        hid_h = m.sb("hid_h", [P, T], F32R)
        hid_l = m.sb("hid_l", [P, T], F32R)
        ps = m.psum()
        gate_at, up_at, out_at = 0, 3 * BANK, 6 * BANK
        wi_high, wi_split = m.sem("wi_high"), m.sem("wi_split")
        wo_high, wo_split = m.sem("wo_high"), m.sem("wo_split")
        gate_done, up_done, out_done = m.sem("gate_done"), m.sem("up_done"), m.sem("out_done")
        silu_done, hid_done, hid_high, hid_split = m.sem("silu_done"), m.sem("hid_done"), m.sem("hid_high"), m.sem("hid_split")
        added = m.sem("added")
        OUTS = KT * len(TOKEN_CHUNKS)
        WAIT_GROUPS = 4
        PER_GROUP = OUTS // (2 * KT - WAIT_GROUPS)
        block = ctx.enter_context(nc.Block())

        def pairs(engine, step):
            with engine.Fori(0, (FT - 2) // 2) as i:
                for u in (1, 2):
                    step(2 * i + u, u % 2)
            step(FT - 1, (FT - 1) % 2)

        @block.sync
        def _(sp):
            with sp.Fori(1, FT) as f:
                sp.wait_ge(wi_split, f)
                sp.dma_start(raw_in[:], weights.w_in[f]).then_inc(in_loaded, 16)
                sp.wait_ge(wo_split, f)
                sp.dma_start(raw_out[:], weights.w_out[f]).then_inc(out_loaded, 16)

        @block.tensor
        def _(pe):
            def project(f, slot, n):
                g, k = n // KT, n % KT
                at, cols = (gate_at, up_at)[g], slice(n * P, (n + 1) * P)
                for j, (w, x) in enumerate(((wi_h, xh), (wi_h, xl), (wi_l, xh))):
                    for c, (t0, tn) in enumerate(TOKEN_CHUNKS):
                        mm = nc.tensor.matmul(ps[:, at + c * BANK:at + c * BANK + tn], w[:, slot, cols], x[:, k, t0:t0 + tn],
                                              start=(k == 0 and j == 0), stop=(k == KT - 1 and j == 2))
                if k == KT - 1:
                    mm.then_inc((gate_done, up_done)[g], 1)

            def expand(f, slot, s):
                o, (t0, tn) = s // 3, TOKEN_CHUNKS[s % 3]
                pe.wait_ge(added, OUTS * f + s + 1)
                at = out_at + s % 2 * BANK
                for j, (w, h) in enumerate(((wo_h, hid_h), (wo_h, hid_l), (wo_l, hid_h))):
                    mm = nc.tensor.matmul(ps[:, at:at + tn], w[:, slot, o * P:(o + 1) * P], h[:, t0:t0 + tn],
                                          start=(j == 0), stop=(j == 2))
                mm.then_inc(out_done, 1)

            def step(f, slot):
                pe.wait_ge(wi_split, f + 1)
                for n in range(2 * KT):
                    if n % KT == 0:
                        pe.wait_ge((silu_done, hid_done)[n // KT], f)
                    project(f, slot, n)
                    if n == WAIT_GROUPS:
                        pe.wait_ge(hid_split, f)
                        pe.wait_ge(wo_split, f)
                    if n >= WAIT_GROUPS:
                        for s in range((n - WAIT_GROUPS) * PER_GROUP, (n - WAIT_GROUPS + 1) * PER_GROUP):
                            expand(f - 1, 1 - slot, s)

            pe.wait_ge(wi_split, 1)
            for n in range(2 * KT):
                project(0, 0, n)
            pairs(pe, step)
            pe.wait_ge(hid_split, FT)
            for s in range(OUTS):
                expand(FT - 1, (FT - 1) % 2, s)

        @block.scalar
        def _(act):
            def split_in(f, slot):
                act.wait_ge(in_loaded, 16 * (f + 1))
                nc.scalar.copy(wi_h[:, slot, :], raw_in[:]).then_inc(wi_high, 1)

            def split_out(f, slot):
                act.wait_ge(out_loaded, 16 * (f + 1))
                nc.scalar.copy(wo_h[:, slot, :], raw_out[:]).then_inc(wo_high, 1)

            def activate(f):
                act.wait_ge(gate_done, f + 1)
                nc.scalar.activation(hid[:], ps[:, gate_at:gate_at + T], ACT.Silu).then_inc(silu_done, 1)

            def high_part(f):
                act.wait_ge(hid_done, f + 1)
                nc.scalar.copy(hid_h[:], hid[:]).then_inc(hid_high, 1)

            def step(f, slot, last=False):
                high_part(f - 1)
                if not last:
                    split_in(f + 1, 1 - slot)
                act.wait_ge(hid_split, f)
                split_out(f, slot)
                activate(f)
                act.wait_ge(out_done, OUTS * f)

            split_in(0, 0)
            split_out(0, 0)
            split_in(1, 1)
            activate(0)
            with act.Fori(0, (FT - 2) // 2) as i:
                for u in (1, 2):
                    step(2 * i + u, u % 2)
            step(FT - 1, (FT - 1) % 2, last=True)
            high_part(FT - 1)

        @block.vector
        def _(dve):
            def split_in(f, slot):
                dve.wait_ge(wi_high, f + 1)
                nc.vector.tensor_tensor(wi_l[:, slot, :], raw_in[:], wi_h[:, slot, :], ALU.subtract).then_inc(wi_split, 1)

            def split_out(f, slot):
                dve.wait_ge(wo_high, f + 1)
                nc.vector.tensor_tensor(wo_l[:, slot, :], raw_out[:], wo_h[:, slot, :], ALU.subtract).then_inc(wo_split, 1)

            def accumulate(f):
                for s in range(OUTS):
                    o, (t0, tn) = s // 3, TOKEN_CHUNKS[s % 3]
                    dve.wait_ge(out_done, OUTS * f + s + 1)
                    at = out_at + s % 2 * BANK
                    nc.vector.tensor_tensor(acc[:, o, t0:t0 + tn], acc[:, o, t0:t0 + tn], ps[:, at:at + tn],
                                            ALU.add).then_inc(added, 1)

            def hidden(f):
                dve.wait_ge(up_done, f + 1)
                dve.wait_ge(silu_done, f + 1)
                nc.vector.tensor_tensor(hid[:], hid[:], ps[:, up_at:up_at + T], ALU.mult).then_inc(hid_done, 1)
                dve.wait_ge(hid_high, f + 1)
                nc.vector.tensor_tensor(hid_l[:], hid[:], hid_h[:], ALU.subtract).then_inc(hid_split, 1)

            def step(f, slot, last=False):
                hidden(f - 1)
                if not last:
                    split_in(f + 1, 1 - slot)
                split_out(f, slot)
                accumulate(f - 1)

            dve.sem_inc(added, 2)
            split_in(0, 0)
            split_out(0, 0)
            split_in(1, 1)
            with dve.Fori(0, (FT - 2) // 2) as i:
                for u in (1, 2):
                    step(2 * i + u, u % 2)
            step(FT - 1, (FT - 1) % 2, last=True)
            hidden(FT - 1)
            accumulate(FT - 1)


def linear_phase(nc, tag, weights, n_tiles, xh, xl, chunks, mode, dest, spill=None, reload=None, scale=1.0,
                 started=True):
    tokens = sum(n for _, n in chunks)
    with ExitStack() as ctx:
        m = Memory(nc, ctx, tag)
        raw, loaded, w_d = weights.raw, weights.loaded, weights.tiles
        w_h = m.sb("w_h", [P, 2, KT * P], F32R)
        w_l = m.sb("w_l", [P, 2, KT * P], F32R)
        stage = m.sb("stage", [P, 2, tokens]) if mode == "store" else None
        ps = m.psum()
        high, split, product, emptied = m.sem("high"), m.sem("split"), m.sem("product"), m.sem("emptied")
        stored, spilled, reloaded = [m.sem(f"stored{u}") for u in range(2)], m.sem("spilled"), m.sem("reloaded")
        block = ctx.enter_context(nc.Block())

        def steps(engine, step, last=n_tiles):
            step(0, 0, 0, True)
            step(1, 1, 0, True)
            with engine.Fori(1, last // 2) as i:
                step(2 * i, 0, i, False)
                step(2 * i + 1, 1, i, False)
            if last % 2:
                step(last - 1, 0, last // 2, False)

        @block.sync
        def _(sp):
            if not started:
                weights.start(sp)

            def move(n, u, half, first):
                if not first:
                    sp.wait_ge(split, n - 1)
                    sp.dma_start(raw[:, u, :], w_d[n]).then_inc(loaded[u], 16)
                if reload is not None and first and u == 1:
                    sp.dma_start(dest[:], reload).then_inc(reloaded, 16)
                if spill is not None and first and u == 1:
                    sp.dma_start(spill[1], spill[0]).then_inc(spilled, 16)

            steps(sp, move)
            if spill is not None:
                sp.wait_ge(spilled, 16)

        @block.tensor
        def _(pe):
            def product_of(n, u, half, first):
                pe.wait_ge(split, n + 1)
                pe.wait_ge(emptied, n + 1)
                for k in range(KT):
                    for j, (w, x) in enumerate(((w_h, xh), (w_h, xl), (w_l, xh))):
                        for c, (t0, tn) in enumerate(chunks):
                            at = (3 * u + c) * BANK
                            mm = nc.tensor.matmul(ps[:, at:at + tn], w[:, u, k * P:(k + 1) * P], x[:, k, t0:t0 + tn],
                                                  start=(k == 0 and j == 0), stop=(k == KT - 1 and j == 2))
                mm.then_inc(product, 1)

            steps(pe, product_of)

        @block.scalar
        def _(act):
            def high_part(n, u, half):
                act.wait_ge(loaded[u], 16 * (half + 1))
                nc.scalar.copy(w_h[:, u, :], raw[:, u, :]).then_inc(high, 1)

            def empty(n, u, half, first):
                act.wait_ge(product, n + 1)
                if mode == "store":
                    if not first:
                        act.wait_ge(stored[u], 16 * half)
                    nc.scalar.copy(stage[:, u, :], ps[:, 3 * u * BANK:3 * u * BANK + tokens]).then_inc(emptied, 1)
                    act.wait_ge(emptied, n + 3)
                    act.dma_start(dest[n], stage[:, u, :]).then_inc(stored[u], 16)
                elif mode == "keep":
                    nc.scalar.copy(dest[:, n, :], ps[:, 3 * u * BANK:3 * u * BANK + tokens]).then_inc(emptied, 1)

            def step(n, u, half, first):
                empty(n, u, half, first)
                high_part(n + 2, u, half + 1)

            high_part(0, 0, 0)
            high_part(1, 1, 0)
            steps(act, step, n_tiles - 2)
            empty(n_tiles - 2, n_tiles % 2, (n_tiles - 2) // 2, False)
            empty(n_tiles - 1, (n_tiles - 1) % 2, (n_tiles - 1) // 2, False)
            if mode == "store":
                act.wait_ge(stored[0], 16 * ((n_tiles + 1) // 2))
                act.wait_ge(stored[1], 16 * (n_tiles // 2))

        @block.vector
        def _(dve):
            dve.sem_inc(emptied, 2)

            def low_part(n, u, half, first=False):
                dve.wait_ge(high, n + 1)
                nc.vector.tensor_tensor(w_l[:, u, :], raw[:, u, :], w_h[:, u, :], ALU.subtract).then_inc(split, 1)

            def add(n, u, half, first):
                dve.wait_ge(product, n + 1)
                nc.vector.scalar_tensor_tensor(dest[:, n, :], dest[:, n, :], scale, ps[:, 3 * u * BANK:3 * u * BANK + tokens],
                                               ALU.mult, ALU.add).then_inc(emptied, 1)

            def step(n, u, half, first):
                add(n, u, half, first)
                low_part(n + 2, u, half + 1)

            if mode == "add":
                low_part(0, 0, 0)
                low_part(1, 1, 0)
                if reload is not None:
                    dve.wait_ge(reloaded, 16)
                steps(dve, step, n_tiles - 2)
                add(n_tiles - 2, n_tiles % 2, (n_tiles - 2) // 2, False)
                add(n_tiles - 1, (n_tiles - 1) % 2, (n_tiles - 1) // 2, False)
            else:
                steps(dve, low_part)


def norm_phase(nc, tag, acc, ones, vecs, gain, bias, tokens=T, scale=1.0, xh=None, xl=None, after=1.0, out_d=None, weights=None):
    steps = tokens // NT
    with ExitStack() as ctx:
        m = Memory(nc, ctx, tag)
        squares = m.sb("squares", [P, 2, KT, NT])
        rstd = m.sb("rstd", [P, 2, NT])
        eps = m.sb("eps", [P, 1])
        ps = m.psum()
        mean_done, centred, squared, var_done = m.sem("mean_done"), m.sem("centred"), m.sem("squared"), m.sem("var_done")
        rooted, rstd_done, scaled, affine_a, affine_v = m.sem("rooted"), m.sem("rstd_done"), m.sem("scaled"), m.sem("affine_a"), m.sem("affine_v")
        high, low, const_set, stored = m.sem("high"), m.sem("low"), m.sem("const_set"), m.sem("stored")
        HALF = KT // 2
        block = ctx.enter_context(nc.Block())

        def tok(s):
            return slice(s * NT, (s + 1) * NT)

        def mean_ps(s):
            return ps[:, s % 2 * BANK:s % 2 * BANK + NT]

        def var_ps(s):
            return ps[:, (2 + s % 2) * BANK:(2 + s % 2) * BANK + NT]

        @block.tensor
        def _(pe):
            def mean(s):
                if s >= 2:
                    pe.wait_ge(centred, s - 1)
                for k in range(KT):
                    mm = nc.tensor.matmul(mean_ps(s), ones[:], acc[:, k, tok(s)], start=(k == 0), stop=(k == KT - 1))
                mm.then_inc(mean_done, 1)

            mean(0)
            for s in range(steps):
                if s + 1 < steps:
                    mean(s + 1)
                pe.wait_ge(squared, s + 1)
                if s >= 2:
                    pe.wait_ge(rooted, s - 1)
                for k in range(KT):
                    mm = nc.tensor.matmul(var_ps(s), ones[:], squares[:, s % 2, k, :], start=(k == 0), stop=(k == KT - 1))
                mm.then_inc(var_done, 1)

        @block.vector
        def _(dve):
            nc.vector.memset(eps[:], LN_EPS / scale ** 2).then_inc(const_set, 1)

            def centre(s):
                dve.wait_ge(mean_done, s + 1)
                nc.vector.tensor_tensor(acc[:, :, tok(s)], acc[:, :, tok(s)],
                                        mean_ps(s).unsqueeze(1).broadcast_to([P, KT, NT]), ALU.subtract).then_inc(centred, 1)

            def normalise(s):
                dve.wait_ge(rooted, s + 1)
                nc.vector.reciprocal(rstd[:, s % 2, :], rstd[:, s % 2, :]).then_inc(rstd_done, 1)
                dve.wait_ge(rstd_done, s + 1)
                dve.wait_ge(squared, s + 1)
                nc.vector.tensor_tensor(acc[:, :, tok(s)], acc[:, :, tok(s)],
                                        rstd[:, s % 2, :].unsqueeze(1).broadcast_to([P, KT, NT]), ALU.mult).then_inc(scaled, 1)
                dve.wait_ge(scaled, s + 1)
                for k in range(HALF, KT):
                    nc.vector.tensor_scalar(acc[:, k, tok(s)], acc[:, k, tok(s)], vecs[:, gain + k:gain + k + 1],
                                            vecs[:, bias + k:bias + k + 1], ALU.mult, ALU.add).then_inc(affine_v, 1)

            def finish(s):
                dve.wait_ge(high, s + 1)
                if s == steps - 1:
                    nc.vector.tensor_tensor(xl[:, :, tok(s)], acc[:, :, tok(s)], xh[:, :, tok(s)], ALU.subtract).then_inc(low, 1)
                if after != 1.0:
                    dve.wait_ge(low, s + 1)
                    nc.vector.tensor_scalar(acc[:, :, tok(s)], acc[:, :, tok(s)], after, None, ALU.mult)

            centre(0)
            for s in range(steps):
                if s + 1 < steps:
                    centre(s + 1)
                normalise(s)
                if s >= 1 and out_d is None:
                    finish(s - 1)
            if out_d is None:
                finish(steps - 1)

        @block.scalar
        def _(act):
            act.wait_ge(const_set, 1)

            def square(s):
                act.wait_ge(centred, s + 1)
                if s >= 2:
                    act.wait_ge(var_done, s - 1)
                nc.scalar.activation(squares[:, s % 2], acc[:, :, tok(s)], ACT.Square).then_inc(squared, 1)

            square(0)
            for s in range(steps):
                act.wait_ge(var_done, s + 1)
                if s >= 2:
                    act.wait_ge(scaled, s - 1)
                nc.scalar.activation(rstd[:, s % 2, :], var_ps(s), ACT.Sqrt, bias=eps[:]).then_inc(rooted, 1)
                if s + 1 < steps:
                    square(s + 1)
                act.wait_ge(scaled, s + 1)
                for k in range(HALF):
                    nc.scalar.activation(acc[:, k, tok(s)], acc[:, k, tok(s)], ACT.Identity,
                                         bias=vecs[:, bias + k:bias + k + 1],
                                         scale=vecs[:, gain + k:gain + k + 1]).then_inc(affine_a, 1)
                if out_d is None:
                    act.wait_ge(affine_v, HALF * (s + 1))
                    act.wait_ge(affine_a, HALF * (s + 1))
                    nc.scalar.copy(xh[:, :, tok(s)], acc[:, :, tok(s)]).then_inc(high, 1)

        if out_d is None:
            @block.sync
            def _(sp):
                weights.start(sp)

            @block.gpsimd
            def _(pool):
                for s in range(steps - 1):
                    pool.wait_ge(high, s + 1)
                    nc.gpsimd.tensor_tensor(xl[:, :, tok(s)], acc[:, :, tok(s)], xh[:, :, tok(s)],
                                            ALU.subtract).then_inc(low, 1)
        else:
            @block.sync
            def _(sp):
                for s in range(steps):
                    sp.wait_ge(affine_a, HALF * (s + 1))
                    sp.wait_ge(affine_v, HALF * (s + 1))
                    sp.dma_start(out_d[:, :, tok(s)], acc[:, :, tok(s)]).then_inc(stored, 16)
                sp.wait_ge(stored, 16 * steps)


def gla_prepare_phase(nc, a, proj_d, vecs, v, q_in, k_in, q_st, k_out, decay, spare, consts_sb):
    with ExitStack() as ctx:
        m = Memory(nc, ctx, "glap")
        q, k = m.sb("q", [P, 2, T]), m.sb("k", [P, 2, T])
        low = m.sb("low", [P, T])
        up = m.sb("up", [P, 4 * P])
        keep = m.sb("keep", [P, T])
        slots = [[m.sb("b1", [P, T])[:], m.sb("b2", [P, T])[:]] + spare[0:3], spare[3:8]]

        def scratch(n):
            b1, b2, run, e0, e1 = slots[n % 2]
            return b1, b2, run, (e0, e1, run, b2)

        ps = m.psum()
        gates_in, loaded, v_loaded, logit = m.sem("gates_in"), m.sem("loaded"), m.sem("v_loaded"), m.sem("logit")
        split, soft, summed, centred, expd = m.sem("split"), m.sem("soft"), m.sem("summed"), m.sem("centred"), m.sem("expd")
        done_v, done_p, step_v, step_a, scaled = m.sem("done_v"), m.sem("done_p"), m.sem("step_v"), m.sem("step_a"), m.sem("scaled")
        consts_in = m.sem("consts_in")
        units = [(d, t) for d in range(2) for t in range(2)]
        block = ctx.enter_context(nc.Block())

        @block.sync
        def _(sp):
            for dst, src in ((low, proj_d[LOW_TILE]), (up, a["gla_up"]), (keep, a["keep"])):
                sp.dma_start(dst[:], src).then_inc(gates_in, 16)
            for dst, tile in ((q, Q_TILE), (k, K_TILE)):
                for t in range(2):
                    sp.dma_start(dst[:, t], proj_d[tile + t]).then_inc(loaded, 16)
            for t in range(4):
                sp.dma_start(v[:, t], proj_d[V_TILE + t]).then_inc(v_loaded, 16)
            sp.dma_start(consts_sb[:], a["consts"]).then_inc(consts_in, 16)
            sp.wait_ge(v_loaded, 64)
            sp.wait_ge(consts_in, 16)

        @block.tensor
        def _(pe):
            pe.wait_ge(gates_in, 48)
            for n, (d, t) in enumerate(units):
                if n >= 2:
                    pe.wait_ge(step_a, 2 * n - 3)
                for c, (t0, tn) in enumerate(TOKEN_CHUNKS):
                    at = (3 * (n % 2) + c) * BANK
                    mm = nc.tensor.matmul(ps[:, at:at + tn], up[:, (2 * d + t) * P:(2 * d + t + 1) * P],
                                          low[:, t0:t0 + tn], start=True, stop=True)
                mm.then_inc(logit, 1)

        @block.vector
        def _(dve):
            dve.wait_ge(gates_in, 48)

            def split_logit(n):
                d, t = units[n]
                b1, b2, run, e = scratch(n)
                bias = vecs[:, GLA_B + 2 * d + t:GLA_B + 2 * d + t + 1]
                z = ps[:, 3 * (n % 2) * BANK:3 * (n % 2) * BANK + T]
                dve.wait_ge(logit, n + 1)
                if n >= 2:
                    dve.wait_ge(expd, 4 * (n - 1))
                    dve.wait_ge(done_p, 2 * (n - 1))
                    dve.wait_ge(done_v, 2 * (n - 1))
                nc.vector.tensor_scalar(b2, z, bias, 0.0, ALU.add, ALU.min).then_inc(split, 1)

            def sums(n):
                d, t = units[n]
                b1, b2, run, e = scratch(n)
                dve.wait_ge(soft, n + 1)
                dve.wait_ge(split, n + 1)
                nc.vector.tensor_tensor(b2, b2, b1, ALU.subtract).then_inc(step_v, 1)
                dve.wait_ge(step_v, 3 * n + 1)
                if d == 0:
                    nc.vector.tensor_tensor_scan(run, keep[:], b2, 0.0, ALU.mult, ALU.add).then_inc(summed, 1)
                else:
                    nc.vector.tensor_tensor_scan(run[:, ::-1], keep[:], b2[:, ::-1], 0.0, ALU.mult, ALU.add).then_inc(summed, 1)
                dve.wait_ge(summed, n + 1)
                chunks = run.rearrange("p (c t) -> p c t", t=C)
                end = C - 1 if d == 0 else 0
                last = chunks[:, :, end:end + 1].broadcast_to([P, N_CHUNKS, C])
                nc.vector.scalar_tensor_tensor(b1.rearrange("p (c t) -> p c t", t=C), last, -0.5, chunks,
                                               ALU.mult, ALU.add).then_inc(step_v, 1)
                nc.vector.tensor_tensor(b2.rearrange("p (c t) -> p c t", t=C), last, chunks,
                                        ALU.subtract).then_inc(step_v, 1)

            def queries(n):
                d, t = units[n]
                b1, b2, run, e = scratch(n)
                dve.wait_ge(expd, 4 * n + 3)
                nc.vector.tensor_tensor(q_in[d][:, t], q[:, t], e[0], ALU.mult).then_inc(done_v, 1)
                nc.vector.tensor_tensor(q_st[d][:, t], q[:, t], e[2], ALU.mult).then_inc(done_v, 1)

            split_logit(0)
            split_logit(1)
            sums(0)
            dve.wait_ge(loaded, 64)
            nc.vector.tensor_scalar(q[:], q[:], GLA_DK ** -0.5, None, ALU.mult).then_inc(scaled, 1)
            dve.wait_ge(scaled, 1)
            for n in range(4):
                if n < 3:
                    sums(n + 1)
                queries(n)
                if n < 2:
                    split_logit(n + 2)

        @block.gpsimd
        def _(pool):
            pool.wait_ge(loaded, 64)
            for n, (d, t) in enumerate(units):
                e = scratch(n)[3]
                pool.wait_ge(expd, 4 * n + 4)
                nc.gpsimd.tensor_tensor(k_in[d][:, t], k[:, t], e[1], ALU.mult).then_inc(done_p, 1)
                nc.gpsimd.tensor_tensor(k_out[d][:, t], k[:, t], e[3], ALU.mult).then_inc(done_p, 1)

        @block.scalar
        def _(act):
            def softplus(n):
                d, t = units[n]
                b1 = scratch(n)[0]
                act.wait_ge(split, n + 1)
                nc.scalar.activation(b1, ps[:, 3 * (n % 2) * BANK:3 * (n % 2) * BANK + T], ACT.Abs,
                                     bias=vecs[:, GLA_B + 2 * d + t:GLA_B + 2 * d + t + 1]).then_inc(step_a, 1)
                act.wait_ge(step_a, 2 * n + 1)
                nc.scalar.activation(b1, b1, ACT.Exp, scale=-1.0).then_inc(step_a, 1)
                act.wait_ge(step_a, 2 * n + 2)
                nc.scalar.activation(b1, b1, ACT.Ln, bias=1.0).then_inc(soft, 1)

            def exponentials(n):
                d, t = units[n]
                b1, b2, run, e = scratch(n)
                end = C - 1 if d == 0 else 0
                act.wait_ge(step_v, 3 * n + 3)
                if n >= 2:
                    act.wait_ge(done_v, 2 * (n - 1))
                    act.wait_ge(done_p, 2 * (n - 1))
                act.wait_ge(summed, n + 1)
                nc.scalar.activation(decay[d][:, t], run.rearrange("p (c t) -> p c t", t=C)[:, :, end],
                                     ACT.Exp, scale=1 / GLA_TAU)
                nc.scalar.activation(e[0], b1, ACT.Exp, scale=1 / GLA_TAU).then_inc(expd, 1)
                nc.scalar.activation(e[1], b1, ACT.Exp, scale=-1 / GLA_TAU).then_inc(expd, 1)
                act.wait_ge(expd, 4 * n + 1)
                nc.scalar.activation(e[2], run, ACT.Exp, scale=1 / GLA_TAU).then_inc(expd, 1)
                nc.scalar.activation(e[3], b2, ACT.Exp, scale=1 / GLA_TAU).then_inc(expd, 1)

            softplus(0)
            softplus(1)
            for n in range(4):
                exponentials(n)
                if n < 2:
                    softplus(n + 2)


def gla_scan_phase(nc, v, q_in, k_in, q_st, k_out, decay, out, consts):
    with ExitStack() as ctx:
        m = Memory(nc, ctx, "glas")
        per_dir = lambda name, shape: [m.sb(f"{name}{d}", shape) for d in range(2)]
        k_pair, qs_pair, s_pair = per_dir("k_pair", [P, 2, 2, C]), per_dir("qs_pair", [P, 2, 2, C]), per_dir("s_pair", [P, 2, 2, C])
        q_now = per_dir("q_now", [P, 2, C])
        v_now, ko_pair = per_dir("v_now", [P, 4, C]), per_dir("ko_pair", [P, 2, 2, C])
        v_rows, kt_pair = per_dir("v_rows", [P, 2, P]), per_dir("kt_pair", [P, 2, 2, C])
        state = per_dir("state", [P, 2, P])
        mark = m.sb("mark", [P, 2])
        ps = m.psum()
        ident, pair_mask = consts["ident"], consts["pair"]
        bank = lambda d, i: ps[:, (4 * d + i) * BANK:(4 * d + i + 1) * BANK]
        TURN, KV, S_AT, O_AT = range(4)
        each = lambda name: [m.sem(f"{name}{d}") for d in range(2)]
        zeroed, k_zeroed, keyed, paired, staged, turned, rows_v, rows_k = m.sem("zeroed"), m.sem("k_zeroed"), each("keyed"), each("paired"), each("staged"), each("turned"), each("rows_v"), each("rows_k")
        scored, masked, outed, added, taken, updated = each("scored"), each("masked"), each("outed"), each("added"), each("taken"), each("updated")
        cleared, out_zeroed = m.sem("cleared"), m.sem("out_zeroed")
        block = ctx.enter_context(nc.Block())

        def sequences(engine, step, start=None):
            for s, (c0, cn) in enumerate(SEQ_CHUNKS):
                if start is not None:
                    start(s, c0)
                step(c0, (c0, c0 + cn - 1), c0 == 0)
                with engine.Fori(1, cn) as i:
                    step(i + c0, (i + c0, i * -1 + (c0 + cn - 1)), False)

        @block.gpsimd
        def _(pool):
            for d in range(2):
                nc.gpsimd.memset(s_pair[d][:], 0.0).then_inc(zeroed, 1)
                nc.gpsimd.memset(k_pair[d][:], 0.0).then_inc(k_zeroed, 1)

            def stage(n, chunk, first):
                mask = pair_mask.unsqueeze(1).broadcast_to([P, 2, 2, C])
                for d in range(2):
                    at = bass.ds(chunk[d] * C, C)
                    if not first:
                        pool.wait_ge(rows_k[d], n)
                    nc.gpsimd.tensor_copy(v_now[d][:], v[:, :, at]).then_inc(staged[d], 1)
                    nc.gpsimd.tensor_tensor(ko_pair[d][:], k_out[d][:, :, at].unsqueeze(2).broadcast_to([P, 2, 2, C]),
                                            mask, ALU.mult).then_inc(staged[d], 1)
                for d in range(2):
                    at = bass.ds(chunk[d] * C, C)
                    if not first:
                        pool.wait_ge(scored[d], n)
                    nc.gpsimd.tensor_copy(q_now[d][:], q_in[d][:, :, at]).then_inc(staged[d], 1)

            sequences(pool, stage)

        @block.tensor
        def _(pe):
            def work(n, chunk, first):
                for d in range(2):
                    pe.wait_ge(staged[d], 3 * n + 2)
                    if not first:
                        pe.wait_ge(rows_v[d], n)
                        pe.wait_ge(rows_k[d], n)
                    for p in range(2):
                        nc.tensor.transpose(bank(d, TURN)[:, p * P:(p + 1) * P],
                                                 v_now[d][:, 2 * p:2 * p + 2].rearrange("p a t -> p (a t)"), ident)
                    for p in range(2):
                        mm = nc.tensor.transpose(bank(d, TURN)[:, (2 + p) * P:(3 + p) * P],
                                                 ko_pair[d][:, p].rearrange("p a t -> p (a t)"), ident)
                    mm.then_inc(turned[d], 1)
                for d in range(2):
                    pe.wait_ge(staged[d], 3 * n + 3)
                    pe.wait_ge(keyed[d], 2 * n + 2)
                    if not first:
                        pe.wait_ge(masked[d], n)
                    for p in range(2):
                        mm = nc.tensor.matmul(bank(d, S_AT)[:, p * C:(p + 1) * C],
                                              k_pair[d][:, p].rearrange("p a t -> p (a t)"), q_now[d][:, p], start=True, stop=True)
                    mm.then_inc(scored[d], 1)
                for d in range(2):
                    pe.wait_ge(rows_v[d], n + 1)
                    pe.wait_ge(rows_k[d], n + 1)
                    if not first:
                        pe.wait_ge(updated[d], 2 * n)
                    for p in range(2):
                        mm = nc.tensor.matmul(bank(d, KV)[:, p * P:(p + 1) * P],
                                              kt_pair[d][:, p].rearrange("p a t -> p (a t)"), v_rows[d][:, p], start=True, stop=True)
                    mm.then_inc(taken[d], 1)
                for d in range(2):
                    pe.wait_ge(masked[d], n + 1)
                    pe.wait_ge(paired[d], n + 1)
                    if first:
                        pe.wait_ge(cleared, 2)
                    else:
                        pe.wait_ge(added[d], n)
                        pe.wait_ge(updated[d], 2 * n)
                        pe.wait_ge(cleared, 2)
                    for p in range(2):
                        o = bank(d, O_AT)[:, p * P:(p + 1) * P]
                        nc.tensor.matmul(o, v_rows[d][:, p], s_pair[d][:, p].rearrange("p a t -> p (a t)"), start=True, stop=False)
                        mm = nc.tensor.matmul(o, state[d][:, p], qs_pair[d][:, p].rearrange("p a t -> p (a t)"), start=False, stop=True)
                    mm.then_inc(outed[d], 1)

            def start(s, c0):
                pe.wait_ge(cleared, 2 * s + 2)

            sequences(pe, work, start)

        @block.scalar
        def _(act):
            act.wait_ge(k_zeroed, 2)

            def rows(n, chunk, first):
                for d in range(2):
                    if not first:
                        act.wait_ge(scored[d], n)
                    for h in range(2):
                        lanes = slice(h * C, (h + 1) * C)
                        nc.scalar.copy(k_pair[d][lanes, :, h], k_in[d][lanes, :, bass.ds(chunk[d] * C, C)]).then_inc(keyed[d], 1)
                for d in range(2):
                    act.wait_ge(turned[d], n + 1)
                    if not first:
                        act.wait_ge(outed[d], n)
                    nc.scalar.copy(v_rows[d][:], bank(d, TURN)[:, 0:2 * P].rearrange("p (q e) -> p q e", e=P)).then_inc(rows_v[d], 1)
                    nc.scalar.copy(kt_pair[d][:], bank(d, TURN)[:, 2 * P:4 * P].rearrange("p (q h e) -> p q h e", h=2, e=C)).then_inc(rows_k[d], 1)

            sequences(act, rows)

        @block.vector
        def _(dve):
            dve.wait_ge(zeroed, 2)
            nc.vector.memset(out[:], 0.0).then_inc(out_zeroed, 1)
            dve.wait_ge(out_zeroed, 1)

            def start(s, c0):
                for d in range(2):
                    if s:
                        dve.wait_ge(updated[d], 2 * c0)
                        dve.wait_ge(outed[d], c0)
                    nc.vector.memset(state[d][:], 0.0).then_inc(cleared, 1)
                dve.wait_ge(cleared, 2 * s + 2)

            def work(n, chunk, first):
                for d in range(2):
                    at = bass.ds(chunk[d] * C, C)
                    mask = pair_mask.unsqueeze(1).broadcast_to([P, 2, 2, C])
                    if not first:
                        dve.wait_ge(outed[d], n)
                    nc.vector.tensor_tensor(qs_pair[d][:], q_st[d][:, :, at].unsqueeze(2).broadcast_to([P, 2, 2, C]),
                                            mask, ALU.mult).then_inc(paired[d], 1)
                for d in range(2):
                    dve.wait_ge(scored[d], n + 1)
                    if not first:
                        dve.wait_ge(outed[d], n)
                        dve.wait_ge(masked[d], n)
                    nc.vector.memset(mark[:, d:d + 1], 0.0)
                    causal = consts["causal"][:, 2 * d * C:2 * (d + 1) * C].rearrange("p (a t) -> p a t", t=C).bitcast(U32)
                    for p in range(2):
                        mk = nc.vector.copy_predicated(
                            s_pair[d][:, p], causal,
                            bank(d, S_AT)[:, p * C:(p + 1) * C].unsqueeze(1).broadcast_to([P, 2, C]))
                    mk.then_inc(masked[d], 1)
                for d in range(2):
                    dve.wait_ge(outed[d], n + 1)
                    at = bass.ds(chunk[d] * C, C)
                    if not first:
                        dve.wait_ge(added[1 - d], n)
                    nc.vector.tensor_tensor(out[:, :, at], out[:, :, at],
                                            bank(d, O_AT)[:, 0:4 * C].rearrange("p (h t) -> p h t", t=C), ALU.add).then_inc(added[d], 1)
                    dve.wait_ge(taken[d], n + 1)
                    for p in range(2):
                        nc.vector.scalar_tensor_tensor(state[d][:, p], state[d][:, p], decay[d][:, p, bass.ds(chunk[d], 1)],
                                                       bank(d, KV)[:, p * P:(p + 1) * P], ALU.mult, ALU.add).then_inc(updated[d], 1)

            sequences(dve, work, start)


def gla_finish_phase(nc, proj_d, vecs, out, consts):
    with ExitStack() as ctx:
        m = Memory(nc, ctx, "glaf")
        g, sq, rstd = m.sb("g", [P, 4, T]), m.sb("sq", [P, 4, T]), m.sb("rstd", [P, 4, T])
        eps = m.sb("eps", [P, 1])
        ps = m.psum()
        loaded, squared, summed, logged, rooted, gated, eps_set = m.sem("loaded"), m.sem("squared"), m.sem("summed"), m.sem("logged"), m.sem("rooted"), m.sem("gated"), m.sem("eps_set")
        silued = m.sem("silued")
        block = ctx.enter_context(nc.Block())

        @block.sync
        def _(sp):
            sp.dma_start(g[:], proj_d[G_TILE:G_TILE + 4].rearrange("n p t -> p n t")).then_inc(loaded, 16)

        @block.tensor
        def _(pe):
            for h in range(4):
                pe.wait_ge(squared, h + 1)
                if h >= 2:
                    pe.wait_ge(logged, h - 1)
                for c, (t0, tn) in enumerate(TOKEN_CHUNKS):
                    at = (3 * (h % 2) + c) * BANK
                    mm = nc.tensor.matmul(ps[:, at:at + tn], consts["ones"], sq[:, h, t0:t0 + tn], start=True, stop=True)
                mm.then_inc(summed, 1)

        @block.scalar
        def _(act):
            for h in range(4):
                nc.scalar.activation(sq[:, h], out[:, h], ACT.Square).then_inc(squared, 1)
            act.wait_ge(loaded, 16)
            nc.scalar.activation(g[:], g[:], ACT.Silu).then_inc(silued, 1)
            act.wait_ge(eps_set, 1)
            for h in range(4):
                act.wait_ge(summed, h + 1)
                nc.scalar.activation(rstd[:, h], ps[:, 3 * (h % 2) * BANK:3 * (h % 2) * BANK + T], ACT.Ln,
                                     bias=eps[:], scale=1 / GLA_DV).then_inc(logged, 1)
            for h in range(4):
                act.wait_ge(logged, h + 1)
                nc.scalar.activation(rstd[:, h], rstd[:, h], ACT.Exp, scale=-0.5).then_inc(rooted, 1)

        @block.vector
        def _(dve):
            nc.vector.memset(eps[:], LN_EPS).then_inc(eps_set, 1)
            dve.wait_ge(silued, 1)
            for h in range(4):
                nc.vector.tensor_scalar(g[:, h], g[:, h], vecs[:, GLA_G + h:GLA_G + h + 1], None, ALU.mult).then_inc(gated, 1)
            for h in range(4):
                dve.wait_ge(squared, h + 1)
                dve.wait_ge(gated, 4 + h)
                nc.vector.tensor_tensor(out[:, h], out[:, h], g[:, h], ALU.mult).then_inc(gated, 1)
            for h in range(4):
                dve.wait_ge(gated, 5 + h)
                dve.wait_ge(rooted, h + 1)
                nc.vector.tensor_tensor(out[:, h], out[:, h], rstd[:, h], ALU.mult)


def rwkv_prepare_phase(nc, a, proj_d, pack_d, vecs, bonus_d, gate_d, consts):
    with ExitStack() as ctx:
        m = Memory(nc, ctx, "rwp")
        bonus, gate = m.sb("bonus", [P, T]), m.sb("gate", [P, T])
        raw2 = m.sb("raw", [P, 2, 3, T])
        r, kr, vr = (m.sb(n, [P, T]) for n in ("r", "kr", "vr"))
        decay = m.sb("decay", [P, 2, T])
        aa, kk = m.sb("aa", [P, T]), m.sb("kk", [P, T])
        low = m.sb("low", [P, 3, T])
        lora, keep = m.sb("lora", [P, 4 * P]), m.sb("keep", [P, T])
        pack = m.sb("pack", [P, N_CHUNKS, PACK])
        stay, one_less = m.sb("stay", [P, MU_TILES]), m.sb("one_less", [P, 4])
        ps = m.psum()
        sets = [ps[:, 0:T], ps[:, 3 * BANK:3 * BANK + T]]
        small_in, keep_in, lora_in, loaded = m.sem("small_in"), m.sem("keep_in"), m.sem("lora_in"), [m.sem("loaded0"), m.sem("loaded1")]
        stored_a, stored_b, gate_stored, bonus_stored = (m.sem(n) for n in ("stored_a", "stored_b", "gate_stored", "bonus_stored"))
        coef, low_scaled, low_ready = m.sem("coef"), m.sem("low_scaled"), m.sem("low_ready")
        scaled, prev_added, next_added = m.sem("scaled"), m.sem("prev_added"), m.sem("next_added")
        logits, sig_done, gate_done, copied = m.sem("logits"), m.sem("sig_done"), m.sem("gate_done"), m.sem("copied")
        scanned, centred, kk_raw, squared, kk_summed, logged, rooted = (
            m.sem(n) for n in ("scanned", "centred", "kk_raw", "squared", "kk_summed", "logged", "rooted"))
        k_factor, k_packed, clamped, kk_packed, b_packed = (m.sem(n) for n in ("k_factor", "k_packed", "clamped", "kk_packed", "b_packed"))
        rk_done, rk_summed, kept = m.sem("rk_done"), m.sem("rk_summed"), m.sem("kept")
        block = ctx.enter_context(nc.Block())
        view = lambda ap: ap.rearrange("p (c t) -> p c t", t=C)
        part = lambda col: pack[:, :, col:col + C]
        SEQS = ((0, T_PROMPT), (T_PROMPT, T))

        @block.sync
        def _(sp):
            for j, tile in enumerate((DECAY_TILE, LOW_TILE, GATE_TILE)):
                sp.dma_start(raw2[:, 1, j], proj_d[tile]).then_inc(small_in, 16)
            sp.dma_start(lora[:], a["lora"][0]).then_inc(lora_in, 16)

            def load(t):
                for j, tile in enumerate((R_TILE, KR_TILE, VR_TILE)):
                    sp.dma_start(raw2[:, t % 2, j], proj_d[tile + t]).then_inc(loaded[t % 2], 16)

            load(0)
            sp.dma_start(keep[:], a["keep"]).then_inc(keep_in, 16)
            for t in range(4):
                if t < 3:
                    if t == 0:
                        sp.wait_ge(next_added, 6)
                    else:
                        sp.wait_ge(b_packed, t)
                    load(t + 1)
                sp.wait_ge(gate_done, t + 1)
                sp.dma_start(gate_d[:, t], gate[:]).then_inc(gate_stored, 16)
                if t < 3:
                    sp.wait_ge(logits, 4 * (t + 1))
                    sp.dma_start(lora[:], a["lora"][t + 1]).then_inc(lora_in, 16)
                sp.wait_ge(copied, 2 * (t + 1))
                sp.wait_ge(centred, 4 * (t + 1))
                sp.dma_start(pack_d[:, :, t, 0:K_COL].rearrange("c p w -> p c w"), pack[:, :, 0:K_COL]).then_inc(stored_a, 16)
                sp.wait_ge(b_packed, t + 1)
                sp.dma_start(pack_d[:, :, t, K_COL:PACK].rearrange("c p w -> p c w"), pack[:, :, K_COL:PACK]).then_inc(stored_b, 16)
                sp.wait_ge(kept, t + 1)
                sp.dma_start(bonus_d[:, t], bonus[:]).then_inc(bonus_stored, 16)
            for sem in (stored_a, stored_b, gate_stored, bonus_stored):
                sp.wait_ge(sem, 64)

        @block.tensor
        def _(pe):
            pe.wait_ge(low_ready, 2)
            pe.wait_ge(next_added, 6)
            for t in range(4):
                pe.wait_ge(lora_in, 16 * (t + 1))
                if t:
                    pe.wait_ge(kept, t)
                for j, src in enumerate((0, 0, 1, 2)):
                    if j >= 2:
                        pe.wait_ge(sig_done, 3 * t + j - 1)
                    for t0, tn in TOKEN_CHUNKS:
                        mm = nc.tensor.matmul(sets[j % 2][:, t0:t0 + tn], lora[:, j * P:(j + 1) * P], low[:, src, t0:t0 + tn],
                                              start=True, stop=True)
                    mm.then_inc(logits, 1)
                pe.wait_ge(squared, t + 1)
                pe.wait_ge(sig_done, 3 * t + 3)
                for t0, tn in TOKEN_CHUNKS:
                    mm = nc.tensor.matmul(sets[0][:, t0:t0 + tn], consts["head_ones"], decay[:, 0, t0:t0 + tn], start=True, stop=True)
                mm.then_inc(kk_summed, 1)
                pe.wait_ge(rk_done, t + 1)
                pe.wait_ge(gate_done, t + 1)
                for t0, tn in TOKEN_CHUNKS:
                    mm = nc.tensor.matmul(sets[1][:, t0:t0 + tn], consts["head_ones"], decay[:, 1, t0:t0 + tn], start=True, stop=True)
                mm.then_inc(rk_summed, 1)

        @block.scalar
        def _(act):
            act.wait_ge(small_in, 48)
            act.wait_ge(coef, 3)
            for j in range(3):
                nc.scalar.activation(low[:, j], raw2[:, 1, j], ACT.Copy, scale=stay[:, 12 + j:13 + j]).then_inc(low_scaled, 1)
            act.wait_ge(next_added, 6)
            nc.scalar.activation(low[:, 0], low[:, 0], ACT.Tanh).then_inc(low_ready, 1)
            nc.scalar.activation(low[:, 2], low[:, 2], ACT.Sigmoid).then_inc(low_ready, 1)
            for t in range(4):
                raw = raw2[:, t % 2]
                act.wait_ge(loaded[t % 2], 48 * (t // 2 + 1))
                if t:
                    act.wait_ge(kept, t)
                for j, dst in enumerate((r, kr, vr)):
                    nc.scalar.activation(dst[:], raw[:, j], ACT.Copy, scale=stay[:, 4 * j + t:4 * j + t + 1]).then_inc(scaled, 1)
                for j in range(3):
                    act.wait_ge(logits, 4 * t + j + 1)
                    dst = aa[:] if j == 2 else decay[:, j]
                    bias = A0 + t if j == 2 else W0 + 4 * j + t
                    nc.scalar.activation(dst, sets[j % 2], ACT.Sigmoid, bias=vecs[:, bias:bias + 1]).then_inc(sig_done, 1)
                act.wait_ge(logits, 4 * t + 4)
                if t:
                    act.wait_ge(gate_stored, 16 * t)
                nc.scalar.copy(gate[:], sets[1]).then_inc(gate_done, 1)
                act.wait_ge(next_added, 6 * (t + 2))
                if t:
                    act.wait_ge(stored_a, 16 * t)
                nc.scalar.copy(part(R_COL), view(r[:])).then_inc(copied, 1)
                nc.scalar.copy(part(V_COL), view(vr[:])).then_inc(copied, 1)
                act.wait_ge(kk_raw, t + 1)
                act.wait_ge(scanned, 2 * t + 1)
                nc.scalar.activation(decay[:, 0], kk[:], ACT.Square).then_inc(squared, 1)
                act.wait_ge(clamped, t + 1)
                nc.scalar.activation(raw[:, 1], raw[:, 1], ACT.Ln).then_inc(logged, 1)
                act.wait_ge(logged, t + 1)
                nc.scalar.activation(raw[:, 1], raw[:, 1], ACT.Exp, scale=-0.5).then_inc(rooted, 1)

        @block.vector
        def _(dve):
            nc.vector.tensor_tensor(stay[:], vecs[:, MU_PREV:MU_PREV + MU_TILES], vecs[:, MU_NEXT:MU_NEXT + MU_TILES], ALU.add).then_inc(coef, 1)
            nc.vector.tensor_scalar(one_less[:], vecs[:, K_A:K_A + 4], -1.0, 1.0, ALU.mult, ALU.add).then_inc(coef, 1)
            dve.wait_ge(coef, 2)
            nc.vector.tensor_scalar(stay[:], stay[:], -1.0, 1.0, ALU.mult, ALU.add).then_inc(coef, 1)

            def shift(dst, src, col, count):
                for s0, s1 in SEQS:
                    nc.vector.scalar_tensor_tensor(dst[:, s0 + 1:s1], src[:, s0:s1 - 1], vecs[:, MU_PREV + col:MU_PREV + col + 1],
                                                   dst[:, s0 + 1:s1], ALU.mult, ALU.add).then_inc(prev_added, 1)
                dve.wait_ge(prev_added, 2 * (count + 1))
                for s0, s1 in SEQS:
                    nc.vector.scalar_tensor_tensor(dst[:, s0:s1 - 1], src[:, s0 + 1:s1], vecs[:, MU_NEXT + col:MU_NEXT + col + 1],
                                                   dst[:, s0:s1 - 1], ALU.mult, ALU.add).then_inc(next_added, 1)

            dve.wait_ge(small_in, 48)
            for j in range(3):
                dve.wait_ge(low_scaled, j + 1)
                shift(low[:, j], raw2[:, 1, j], 12 + j, j)
            dve.wait_ge(keep_in, 16)
            for t in range(4):
                raw = raw2[:, t % 2]
                dve.wait_ge(loaded[t % 2], 48 * (t // 2 + 1))
                for j, dst in enumerate((r, kr, vr)):
                    dve.wait_ge(scaled, 3 * t + j + 1)
                    shift(dst[:], raw[:, j], 4 * j + t, 3 * (t + 1) + j)
                dve.wait_ge(next_added, 6 * (t + 2))
                run = raw[:, 0]
                for d in range(2):
                    dve.wait_ge(sig_done, 3 * t + d + 1)
                    if d == 0:
                        nc.vector.tensor_tensor_scan(run, keep[:], decay[:, 0], 0.0, ALU.mult, ALU.add).then_inc(scanned, 1)
                    else:
                        dve.wait_ge(centred, 4 * t + 2)
                        nc.vector.tensor_tensor_scan(run[:, ::-1], keep[:], decay[:, 1, ::-1], 0.0, ALU.mult, ALU.add).then_inc(scanned, 1)
                    dve.wait_ge(scanned, 2 * t + d + 1)
                    if t:
                        dve.wait_ge(stored_a, 16 * t)
                    end = C - 1 if d == 0 else 0
                    first = G_COL + d * (C + 1)
                    at, edge = (first + 1, first) if d == 0 else (first, first + C)
                    last = view(run)[:, :, end:end + 1]
                    nc.vector.scalar_tensor_tensor(pack[:, :, at:at + C], last.broadcast_to([P, N_CHUNKS, C]), -0.5, view(run),
                                                   ALU.mult, ALU.add).then_inc(centred, 1)
                    nc.vector.tensor_scalar(pack[:, :, edge:edge + 1], last, -0.5, None, ALU.mult).then_inc(centred, 1)
                nc.vector.tensor_scalar(kk[:], kr[:], vecs[:, K_K + t:K_K + t + 1], None, ALU.mult).then_inc(kk_raw, 1)
                dve.wait_ge(sig_done, 3 * t + 3)
                nc.vector.tensor_scalar(raw[:, 2], aa[:], vecs[:, K_A + t:K_A + t + 1], one_less[:, t:t + 1],
                                        ALU.mult, ALU.add).then_inc(k_factor, 1)
                dve.wait_ge(k_factor, t + 1)
                if t:
                    dve.wait_ge(stored_b, 16 * t)
                nc.vector.tensor_tensor(part(K_COL), view(kr[:]), view(raw[:, 2]), ALU.mult).then_inc(k_packed, 1)
                dve.wait_ge(kk_summed, t + 1)
                nc.vector.tensor_scalar(raw[:, 1], sets[0], KK_EPS * KK_EPS, None, ALU.max).then_inc(clamped, 1)
                dve.wait_ge(k_packed, t + 1)
                dve.wait_ge(scanned, 2 * t + 2)
                nc.vector.scalar_tensor_tensor(view(decay[:, 1]), view(r[:]), vecs[:, R_K + t:R_K + t + 1], part(K_COL),
                                               ALU.mult, ALU.mult).then_inc(rk_done, 1)
                dve.wait_ge(rooted, t + 1)
                nc.vector.tensor_tensor(part(KK_COL), view(kk[:]), view(raw[:, 1]), ALU.mult).then_inc(kk_packed, 1)
                dve.wait_ge(kk_packed, t + 1)
                nc.vector.scalar_tensor_tensor(part(B_COL), part(KK_COL), -1.0, view(aa[:]), ALU.mult, ALU.mult).then_inc(b_packed, 1)
                dve.wait_ge(rk_summed, t + 1)
                dve.wait_ge(copied, 2 * (t + 1))
                dve.wait_ge(b_packed, t + 1)
                if t:
                    dve.wait_ge(bonus_stored, 16 * t)
                nc.vector.tensor_tensor(bonus[:], sets[1], vr[:], ALU.mult).then_inc(kept, 1)


def rwkv_scan_phase(nc, pack_d, out, consts):
    with ExitStack() as ctx:
        m_ = Memory(nc, ctx, "rws")
        per_dir = lambda name, shape: [m_.sb(f"{name}{d}", shape) for d in range(2)]
        per_slot = lambda name, shape: [[m_.sb(f"{name}{d}{u}", shape) for u in range(2)] for d in range(2)]
        PAIR, STACK = [P, 4, 2, C], [P, 4, C]
        pack, decayed, grown = per_dir("pack", [P, 4, PACK]), per_dir("decayed", [P, 4, C + 1]), per_slot("grown", [P, 4, C + 1])
        ar = per_slot("ar", PAIR)
        a_pair, b_rows, k_rows, v_rows, v_stack = (per_slot(n, s) for n, s in (
            ("a_pair", PAIR), ("b_rows", PAIR), ("k_rows", PAIR), ("v_rows", PAIR), ("v_stack", STACK)))
        b_pair, k_pair, v_pair, grown_pair = (per_dir(n, PAIR) for n in ("b_pair", "k_pair", "v_pair", "grown_pair"))
        ab_pair, ak_pair = per_dir("ab_pair", PAIR), per_slot("ak_pair", PAIR)
        rb, rk = per_slot("rb", STACK), per_slot("rk", STACK)
        x, xt_pair, y = per_dir("x", PAIR), per_slot("xt_pair", PAIR), per_dir("y", STACK)
        rhs, u, u_pair = per_dir("rhs", STACK), per_dir("u", STACK), per_dir("u_pair", PAIR)
        h_true, h, h_sum, h_pair = per_dir("h_true", STACK), per_dir("h", STACK), per_dir("h_sum", STACK), per_dir("h_pair", PAIR)
        ps = m_.psum()
        bank = lambda d, i: ps[:, (4 * d + i) * BANK:(4 * d + i + 1) * BANK]
        BX, KX, TURN, ST = range(4)
        as_pair = lambda ap: ap.rearrange("p (q h t) -> p q h t", h=2, t=C)
        as_stack = lambda ap: ap[:, 0:4 * C].rearrange("p (q t) -> p q t", t=C)
        both = lambda ap: ap.unsqueeze(2).broadcast_to(PAIR)
        tiles = lambda ap: ap.unsqueeze(1).broadcast_to([P, 4] + list(ap.shape[1:]))
        flat = lambda ap: ap.rearrange("p h t -> p (h t)")
        by_head = lambda ap: ap.rearrange("p (h t) -> p h t", t=C)
        ident, twice_ident = consts["ident"], consts["twice_ident"]
        stack_ident = twice_ident[:, 0:C]

        def mask(name, d, level=0, width=C):
            at = (level * 2 + d) * width
            return consts[name][:, at:at + width]

        each = lambda name: [m_.sem(f"{name}{d}") for d in range(2)]
        loaded, exps, grown_2, a_2, v_2, a_r, b_2, k_2 = (each(n) for n in ("loaded", "exps", "grown_2", "a_2", "v_2", "a_r", "b_2", "k_2"))
        with_b, with_k, masked, turned, rows, stacked = (each(n) for n in ("with_b", "with_k", "masked", "turned", "rows", "stacked"))
        ly, y_set, xy, x_set, x_turned, xt_set = (each(n) for n in ("ly", "y_set", "xy", "x_set", "x_turned", "xt_set"))
        rhs_done, rhs_set, u_done, u_set, u_2 = (each(n) for n in ("rhs_done", "rhs_set", "u_done", "u_set", "u_2"))
        h_set, h_2, h_done, h_summed, h_next, y_done, y_added = (
            each(n) for n in ("h_set", "h_2", "h_done", "h_summed", "h_next", "y_done", "y_added"))
        zeroed, out_zeroed = m_.sem("zeroed"), m_.sem("out_zeroed")
        block = ctx.enter_context(nc.Block())
        now = lambda d: slice(1, C + 1) if d == 0 else slice(0, C)
        before = lambda d: slice(0, C) if d == 0 else slice(1, C + 1)
        edge = lambda d: slice(0, 1) if d == 0 else slice(C, C + 1)
        N_PROMPT = SEQ_CHUNKS[0][1]
        DIRS = range(2)

        def chunk_of(n, sample):
            return n, n * -1 + (N_CHUNKS + N_PROMPT - 1 if sample else N_PROMPT - 1)

        def steps(engine, step):
            for n in range(N_PROMPT):
                step(n, n % 2, True, False, n + 1 >= N_PROMPT)
            with engine.Fori(N_PROMPT // 2, N_CHUNKS // 2 - 1) as i:
                for slot in range(2):
                    step(2 * i + slot, slot, True, True, True)
            step(N_CHUNKS - 2, 0, True, True, True)
            step(N_CHUNKS - 1, 1, False, True, True)

        def after(engine, sem, value, m, least):
            if not (isinstance(m, int) and m < least):
                engine.wait_ge(sem, value)

        @block.sync
        def _(sp):
            def load(m, sample):
                for d in DIRS:
                    after(sp, b_2[d], m, m, 1)
                    after(sp, k_2[d], m, m, 1)
                    after(sp, v_2[d], m, m, 1)
                    sp.dma_start(pack[d][:], pack_d[chunk_of(m, sample)[d]]).then_inc(loaded[d], 16)

            load(0, False)
            steps(sp, lambda n, slot, more, sample, next_sample: load(n + 1, next_sample) if more else None)

        @block.gpsimd
        def _(pool):
            pair = tiles(consts["pair"])
            for d in DIRS:
                for u_ in range(2):
                    nc.gpsimd.memset(xt_pair[d][u_][:], 0.0).then_inc(zeroed, 1)

            def spread(m, slot):
                for d in DIRS:
                    pool.wait_ge(exps[d], 2 * m + 2)
                    after(pool, k_2[d], m, m, 1)
                    nc.gpsimd.tensor_tensor(grown_pair[d][:], both(grown[d][slot][:, :, now(d)]), pair, ALU.mult).then_inc(grown_2[d], 1)
                for d in DIRS:
                    pool.wait_ge(loaded[d], (m + 1) * 16)
                    after(pool, turned[d], 3 * m, m, 1)
                    nc.gpsimd.tensor_tensor(v_pair[d][:], both(pack[d][:, :, V_COL:V_COL + C]), pair, ALU.mult).then_inc(v_2[d], 1)

            def spread_late(m, slot):
                for d in DIRS:
                    pool.wait_ge(a_r[d], 2 * m + 2)
                    after(pool, y_done[d], m - 1, m, 2)
                    nc.gpsimd.tensor_tensor(a_pair[d][slot][:], both(ar[d][slot][:, :, 0]), pair, ALU.mult).then_inc(a_2[d], 1)
                for d in DIRS:
                    pool.wait_ge(rows[d], 3 * m + 3)
                    nc.gpsimd.tensor_tensor(v_stack[d][slot][:], v_rows[d][slot][:, :, 0], v_rows[d][slot][:, :, 1], ALU.add).then_inc(stacked[d], 1)

            def step(n, slot, more, sample, next_sample):
                if more:
                    spread(n + 1, 1 - slot)
                for d in DIRS:
                    pool.wait_ge(h_set[d], n + 1)
                    after(pool, y_done[d], n, n, 1)
                    nc.gpsimd.tensor_tensor(h_pair[d][:], both(h[d][:]), pair, ALU.mult).then_inc(h_2[d], 1)
                for d in DIRS:
                    pool.wait_ge(u_set[d], n + 1)
                    nc.gpsimd.tensor_tensor(u_pair[d][:], both(u[d][:]), pair, ALU.mult).then_inc(u_2[d], 1)
                if more:
                    spread_late(n + 1, 1 - slot)

            spread(0, 0)
            spread_late(0, 0)
            steps(pool, step)

        @block.tensor
        def _(pe):
            def each_tile(bank_ap, width, lhs, rhs_of, done):
                for q in range(4):
                    mm = nc.tensor.matmul(bank_ap[:, q * width:(q + 1) * width], flat(lhs[:, q]), rhs_of(q), start=True, stop=True)
                mm.then_inc(done, 1)

            def turn(dst, src, done):
                for q in range(4):
                    mm = nc.tensor.transpose(dst[:, q * P:(q + 1) * P], flat(src[:, q]), ident)
                mm.then_inc(done, 1)

            def prepare(m, slot):
                for d in DIRS:
                    pe.wait_ge(b_2[d], m + 1)
                    each_tile(bank(d, BX), P, b_pair[d], lambda q: flat(ar[d][slot][:, q]), with_b[d])
                    pe.wait_ge(k_2[d], m + 1)
                    each_tile(bank(d, KX), P, k_pair[d], lambda q: flat(ar[d][slot][:, q]), with_k[d])
                    after(pe, xt_set[d], 2 * LEVELS * m, m, 1)
                    turn(bank(d, TURN), b_pair[d], turned[d])
                for d in DIRS:
                    after(pe, h_summed[d], m, m, 1)
                    turn(bank(d, ST), k_pair[d], turned[d])
                for d in DIRS:
                    pe.wait_ge(rows[d], 3 * m + 1)
                    pe.wait_ge(v_2[d], m + 1)
                    turn(bank(d, TURN), v_pair[d], turned[d])
                for d in DIRS:
                    pe.wait_ge(masked[d], 4 * m + 2)
                    each_tile(bank(d, BX), C, ab_pair[d], lambda q: stack_ident, ly[d])

            def invert(m, slot):
                for level in range(1, LEVELS):
                    for d in DIRS:
                        pe.wait_ge(x_set[d], m * LEVELS + level)
                        if level == 1:
                            pe.wait_ge(rows[d], 3 * m + 3)
                        turn(bank(d, TURN), x[d], x_turned[d])
                        each_tile(bank(d, BX), C, ab_pair[d], lambda q: x[d][:, q, 0], ly[d])
                    for d in DIRS:
                        pe.wait_ge(y_set[d], m * LEVELS + level + 1)
                        pe.wait_ge(xt_set[d], (m * LEVELS + level) * 2)
                        if level == 1:
                            pe.wait_ge(masked[d], 4 * m + 4)
                        each_tile(bank(d, KX), C, xt_pair[d][slot], lambda q: y[d][:, q], xy[d])
                for d in DIRS:
                    pe.wait_ge(x_set[d], (m + 1) * LEVELS)
                    turn(bank(d, TURN), x[d], x_turned[d])

            def state_first(n, slot):
                for d in DIRS:
                    pe.wait_ge(h_set[d], n + 1)
                    pe.wait_ge(a_2[d], n + 1)
                    pe.wait_ge(stacked[d], n + 1)
                    after(pe, y_added[d], n, n, 1)
                    for q in range(4):
                        o = bank(d, ST)[:, q * C:(q + 1) * C]
                        nc.tensor.matmul(o, flat(ak_pair[d][slot][:, q]), v_stack[d][slot][:, q], start=True, stop=False)
                        mm = nc.tensor.matmul(o, flat(a_pair[d][slot][:, q]), h[d][:, q], start=False, stop=True)
                    mm.then_inc(rhs_done[d], 1)
                for d in DIRS:
                    pe.wait_ge(rhs_set[d], n + 1)
                    pe.wait_ge(xt_set[d], (n + 1) * LEVELS * 2)
                    each_tile(bank(d, ST), C, xt_pair[d][slot], lambda q: rhs[d][:, q], u_done[d])
                for d in DIRS:
                    pe.wait_ge(u_set[d], n + 1)
                    for q in range(4):
                        o = bank(d, ST)[:, q * C:(q + 1) * C]
                        nc.tensor.matmul(o, flat(b_rows[d][slot][:, q]), u[d][:, q], start=True, stop=False)
                        mm = nc.tensor.matmul(o, flat(k_rows[d][slot][:, q]), v_stack[d][slot][:, q], start=False, stop=True)
                    mm.then_inc(h_done[d], 1)

            def state_out(n, slot, more):
                for d in DIRS:
                    if more:
                        pe.wait_ge(rows[d], 3 * (n + 1) + 2)
                    pe.wait_ge(h_2[d], n + 1)
                    pe.wait_ge(u_2[d], n + 1)
                    pe.wait_ge(h_summed[d], n + 1)
                    for q in range(4):
                        o = bank(d, ST)[:, q * C:(q + 1) * C]
                        nc.tensor.matmul(o, flat(h_pair[d][:, q]), ar[d][slot][:, q, 1], start=True, stop=False)
                        nc.tensor.matmul(o, flat(u_pair[d][:, q]), rb[d][slot][:, q], start=False, stop=False)
                        mm = nc.tensor.matmul(o, flat(v_rows[d][slot][:, q]), rk[d][slot][:, q], start=False, stop=True)
                    mm.then_inc(y_done[d], 1)

            def step(n, slot, more, sample, next_sample):
                state_first(n, slot)
                if more:
                    prepare(n + 1, 1 - slot)
                state_out(n, slot, more)
                if more:
                    invert(n + 1, 1 - slot)

            prepare(0, 0)
            invert(0, 0)
            steps(pe, step)

        @block.scalar
        def _(act):
            def halves(dst, src, done):
                for r in range(2):
                    lanes = slice(r * C, (r + 1) * C)
                    nc.scalar.copy(dst[lanes, :, r], as_pair(src)[lanes, :, r]).then_inc(done, 1)

            def exponentials(m, slot):
                for d in DIRS:
                    act.wait_ge(loaded[d], (m + 1) * 16)
                    after(act, b_2[d], m, m, 1)
                    after(act, h_next[d], m, m, 2)
                    g = pack[d][:, :, G_COL + d * (C + 1):G_COL + (d + 1) * (C + 1)]
                    nc.scalar.activation(grown[d][slot][:], g, ACT.Exp, scale=DECAY_UNIT).then_inc(exps[d], 1)
                    nc.scalar.activation(decayed[d][:], g, ACT.Exp, scale=-DECAY_UNIT).then_inc(exps[d], 1)

            def invert(m, slot):
                for j, dst in enumerate((b_rows, k_rows, v_rows)):
                    for d in DIRS:
                        act.wait_ge(turned[d], 3 * m + j + 1)
                        after(act, y_done[d], m - 1, m, 2)
                        nc.scalar.copy(dst[d][slot][:], as_pair(bank(d, ST if dst is k_rows else TURN))).then_inc(rows[d], 1)
                for level in range(LEVELS):
                    for d in DIRS:
                        act.wait_ge(x_turned[d], m * LEVELS + level + 1)
                        halves(xt_pair[d][slot], bank(d, TURN), xt_set[d])

            def step(n, slot, more, sample, next_sample):
                if more:
                    exponentials(n + 1, 1 - slot)
                for d in DIRS:
                    act.wait_ge(rhs_done[d], n + 1)
                    nc.scalar.copy(rhs[d][:], as_stack(bank(d, ST))).then_inc(rhs_set[d], 1)
                for d in DIRS:
                    act.wait_ge(u_done[d], n + 1)
                    nc.scalar.copy(u[d][:], as_stack(bank(d, ST))).then_inc(u_set[d], 1)
                if more:
                    invert(n + 1, 1 - slot)

            act.wait_ge(zeroed, 4)
            exponentials(0, 0)
            invert(0, 0)
            steps(act, step)

        @block.vector
        def _(dve):
            nc.vector.memset(out[:], 0.0).then_inc(out_zeroed, 1)
            dve.wait_ge(out_zeroed, 1)
            for d in DIRS:
                nc.vector.memset(h_true[d][:], 0.0).then_inc(h_next[d], 1)

            def products(m, slot):
                for d in DIRS:
                    dve.wait_ge(exps[d], 2 * m + 2)
                    after(dve, y_done[d], m - 1, m, 2)
                    nc.vector.tensor_tensor(ar[d][slot][:, :, 0], pack[d][:, :, KK_COL:KK_COL + C], decayed[d][:, :, before(d)], ALU.mult).then_inc(a_r[d], 1)
                    nc.vector.tensor_tensor(ar[d][slot][:, :, 1], pack[d][:, :, R_COL:R_COL + C], decayed[d][:, :, now(d)], ALU.mult).then_inc(a_r[d], 1)
                for d in DIRS:
                    dve.wait_ge(a_r[d], 2 * m + 2)
                    dve.wait_ge(grown_2[d], m + 1)
                    after(dve, turned[d], 3 * m, m, 1)
                    nc.vector.tensor_tensor(b_pair[d][:], both(pack[d][:, :, B_COL:B_COL + C]), grown_pair[d][:], ALU.mult).then_inc(b_2[d], 1)
                    nc.vector.tensor_tensor(k_pair[d][:], both(pack[d][:, :, K_COL:K_COL + C]), grown_pair[d][:], ALU.mult).then_inc(k_2[d], 1)

            def before_pair(d, ap):
                return both(ap[:, :, 0]), tiles(by_head(mask("before_pair", d, width=2 * C)))

            def masks_b(m, slot):
                for d in DIRS:
                    dve.wait_ge(with_b[d], m + 1)
                    s = as_pair(bank(d, BX))
                    after(dve, x_turned[d], LEVELS * m, m, 1)
                    nc.vector.tensor_tensor(ab_pair[d][:], *before_pair(d, s), ALU.mult).then_inc(masked[d], 1)
                    nc.vector.tensor_tensor(rb[d][slot][:], s[:, :, 1], tiles(mask("upto", d)), ALU.mult).then_inc(masked[d], 1)

            def masks_k(m, slot):
                for d in DIRS:
                    dve.wait_ge(with_k[d], m + 1)
                    s = as_pair(bank(d, KX))
                    nc.vector.tensor_tensor(ak_pair[d][slot][:], *before_pair(d, s), ALU.mult).then_inc(masked[d], 1)
                    nc.vector.tensor_tensor(rk[d][slot][:], s[:, :, 1], tiles(mask("upto", d)), ALU.mult).then_inc(masked[d], 1)

            def invert_first(m):
                for d in DIRS:
                    dve.wait_ge(ly[d], m * LEVELS + 1)
                    nc.vector.tensor_tensor(y[d][:], as_stack(bank(d, BX)), tiles(mask("level", d)), ALU.mult).then_inc(y_set[d], 1)
                for d in DIRS:
                    dve.wait_ge(y_set[d], m * LEVELS + 1)
                    nc.vector.tensor_tensor(x[d][:], both(y[d][:]), tiles(by_head(twice_ident)), ALU.add).then_inc(x_set[d], 1)

            def invert(m, level):
                for d in DIRS:
                    dve.wait_ge(ly[d], m * LEVELS + level + 1)
                    nc.vector.tensor_tensor(y[d][:], as_stack(bank(d, BX)), tiles(mask("level", d, level)), ALU.mult).then_inc(y_set[d], 1)
                for d in DIRS:
                    dve.wait_ge(xy[d], m * (LEVELS - 1) + level)
                    dve.wait_ge(x_turned[d], m * LEVELS + level)
                    nc.vector.tensor_tensor(x[d][:], x[d][:], both(as_stack(bank(d, KX))), ALU.add).then_inc(x_set[d], 1)

            def step(n, slot, more, sample, next_sample):
                for d in DIRS:
                    dve.wait_ge(h_next[d], n + 1)
                    after(dve, y_done[d], n, n, 1)
                    nc.vector.tensor_tensor(h[d][:], h_true[d][:], grown[d][slot][:, :, edge(d)].broadcast_to(STACK), ALU.mult).then_inc(h_set[d], 1)
                if more:
                    products(n + 1, 1 - slot)
                for d in DIRS:
                    dve.wait_ge(h_done[d], n + 1)
                    nc.vector.tensor_tensor(h_sum[d][:], h[d][:], as_stack(bank(d, ST)), ALU.add).then_inc(h_summed[d], 1)
                    if not sample and next_sample:
                        nc.vector.memset(h_true[d][:], 0.0).then_inc(h_next[d], 1)
                    else:
                        dve.wait_ge(h_summed[d], n + 1)
                        nc.vector.tensor_tensor(h_true[d][:], h_sum[d][:], grown[d][slot][:, :, edge(d)].broadcast_to(STACK),
                                                ALU.mult).then_inc(h_next[d], 1)
                if more:
                    masks_b(n + 1, 1 - slot)
                    invert_first(n + 1)
                    masks_k(n + 1, 1 - slot)
                for d in DIRS:
                    dve.wait_ge(y_done[d], n + 1)
                    after(dve, y_added[1 - d], n, n, 1)
                    at = bass.ds(chunk_of(n, sample)[d] * C, C)
                    nc.vector.tensor_tensor(out[:, :, at], out[:, :, at], as_stack(bank(d, ST)), ALU.add).then_inc(y_added[d], 1)
                if more:
                    for level in range(1, LEVELS):
                        invert(n + 1, level)

            products(0, 0)
            masks_b(0, 0)
            invert_first(0)
            masks_k(0, 0)
            for level in range(1, LEVELS):
                invert(0, level)
            steps(dve, step)


def rwkv_finish_phase(nc, vecs, out, bonus_d, gate_d, consts, mem, mem_d, mem_in):
    with ExitStack() as ctx:
        m = Memory(nc, ctx, "rwf")
        sq, rstd, eps = m.sb("sq", [P, 4, T]), m.sb("rstd", [P, 4, T]), m.sb("eps", [P, 1])
        bonus, gate = m.sb("bonus", [P, 4, T]), m.sb("gate", [P, 4, T])
        ps = m.psum()
        sets = [ps[:, 0:T], ps[:, 3 * BANK:3 * BANK + T]]
        eps_set, summed, centred, squared, sq_summed, logged, rooted = (
            m.sem(n) for n in ("eps_set", "summed", "centred", "squared", "sq_summed", "logged", "rooted"))
        bonus_in, gate_in, biased, scaled, raised = (m.sem(n) for n in ("bonus_in", "gate_in", "biased", "scaled", "raised"))
        block = ctx.enter_context(nc.Block())

        @block.sync
        def _(sp):
            sp.dma_start(bonus[:], bonus_d).then_inc(bonus_in, 16)
            sp.dma_start(gate[:], gate_d).then_inc(gate_in, 16)
            sp.dma_start(mem[:], mem_d).then_inc(mem_in, 16)
            sp.wait_ge(mem_in, 16)

        @block.tensor
        def _(pe):
            def head_sums(bank, src):
                for t0, tn in TOKEN_CHUNKS:
                    mm = nc.tensor.matmul(bank[:, t0:t0 + tn], consts["head_ones"], src[:, t0:t0 + tn], start=True, stop=True)
                return mm

            for t in range(4):
                if t >= 2:
                    pe.wait_ge(centred, t - 1)
                head_sums(sets[t % 2], out[:, t]).then_inc(summed, 1)
            for t in range(4):
                pe.wait_ge(squared, t + 1)
                if t < 2:
                    pe.wait_ge(centred, t + 3)
                else:
                    pe.wait_ge(logged, t - 1)
                head_sums(sets[t % 2], sq[:, t]).then_inc(sq_summed, 1)

        @block.scalar
        def _(act):
            for t in range(4):
                act.wait_ge(centred, t + 1)
                nc.scalar.activation(sq[:, t], out[:, t], ACT.Square).then_inc(squared, 1)
            act.wait_ge(eps_set, 1)
            for t in range(4):
                act.wait_ge(sq_summed, t + 1)
                nc.scalar.activation(rstd[:, t], sets[t % 2], ACT.Ln, bias=eps[:], scale=1 / C).then_inc(logged, 1)
            act.wait_ge(bonus_in, 16)
            for t in range(4):
                act.wait_ge(logged, t + 1)
                nc.scalar.activation(rstd[:, t], rstd[:, t], ACT.Exp, scale=-0.5).then_inc(rooted, 1)
                nc.scalar.activation(bonus[:, t], bonus[:, t], ACT.Identity, bias=vecs[:, LNX_B + t:LNX_B + t + 1]).then_inc(biased, 1)

        @block.vector
        def _(dve):
            nc.vector.memset(eps[:], RWKV_GN_EPS).then_inc(eps_set, 1)
            for t in range(4):
                dve.wait_ge(summed, t + 1)
                nc.vector.scalar_tensor_tensor(out[:, t], sets[t % 2], -1 / C, out[:, t], ALU.mult, ALU.add).then_inc(centred, 1)
            for t in range(4):
                dve.wait_ge(rooted, t + 1)
                nc.vector.scalar_tensor_tensor(out[:, t], out[:, t], vecs[:, LNX_G + t:LNX_G + t + 1], rstd[:, t],
                                               ALU.mult, ALU.mult).then_inc(scaled, 1)
                dve.wait_ge(scaled, t + 1)
                dve.wait_ge(biased, t + 1)
                nc.vector.tensor_tensor(out[:, t], out[:, t], bonus[:, t], ALU.add).then_inc(raised, 1)

        @block.gpsimd
        def _(pool):
            pool.wait_ge(gate_in, 16)
            for t in range(4):
                pool.wait_ge(raised, t + 1)
                nc.gpsimd.tensor_tensor(out[:, t], out[:, t], gate[:, t], ALU.mult)


def split_phase(nc, acc, xh, xl, weights):
    with ExitStack() as ctx:
        m = Memory(nc, ctx, "split")
        high = m.sem("high")
        block = ctx.enter_context(nc.Block())

        @block.sync
        def _(sp):
            weights.start(sp)

        @block.scalar
        def _(act):
            for k in range(KT):
                nc.scalar.copy(xh[:, k, :], acc[:, k, :]).then_inc(high, 1)

        @block.vector
        def _(dve):
            for k in range(KT):
                dve.wait_ge(high, k + 1)
                nc.vector.tensor_tensor(xl[:, k, :], acc[:, k, :], xh[:, k, :], ALU.subtract)


def attention_phase(nc, q, kv_d, xh, xl, ident_d):
    HEADS, M = 4, 256
    SCALE = 256.0 ** -0.5
    with ExitStack() as ctx:
        m = Memory(nc, ctx, "attn")
        keys = m.sb("keys", [P, KT, 2 * M])
        values = m.sb("values", [P, 4, D])
        q_now, ident_sb, ident_in = m.sb("q_now", [P, KT, P]), m.sb("ident", [P, P]), m.sem("ident_in")
        ident = ident_sb[:]
        probs, probs_t = m.sb("probs", [P, HEADS, M]), m.sb("probs_t", [P, 2 * HEADS, P])
        top, neg, total, inverse = (m.sb(n, [P, HEADS]) for n in ("top", "neg", "total", "inverse"))
        ps = m.psum()
        v_raw = [probs[:].rearrange("p h m -> p (h m)")[:, 0:2 * M], probs[:].rearrange("p h m -> p (h m)")[:, 2 * M:4 * M]]
        S_AT, T_AT, O_AT = 0, 2 * BANK, 4 * BANK
        keys_in, v_in = m.sem("keys_in"), [m.sem("v_in0"), m.sem("v_in1")]
        v_turned, v_set = m.sem("v_turned"), m.sem("v_set")
        staged, scored, topped, negated, expd, inverted, normed = (
            m.sem(n) for n in ("staged", "scored", "topped", "negated", "expd", "inverted", "normed"))
        turned, t_set, outed, high, low = (m.sem(n) for n in ("turned", "t_set", "outed", "high", "low"))
        block = ctx.enter_context(nc.Block())
        heads = lambda ap: ap.rearrange("p (h m) -> p h m", h=HEADS)

        N, N0 = T // P, T_PROMPT // P

        def tiles(engine, begin, end):
            begin(0, 0, True)
            for n in range(N0):
                begin(n + 1, int(n + 1 >= N0), False)
                end(n, 0, n == 0)
            with engine.Fori(N0, N - 1) as n:
                begin(n + 1, 1, False)
                end(n, 1, False)
            end(N - 1, 1, False)

        @block.sync
        def _(sp):
            sp.dma_start(ident, ident_d).then_inc(ident_in, 16)
            sp.dma_start(keys[:], kv_d[0:KT].rearrange("n p m -> p n m")).then_inc(keys_in, 16)
            for j in range(KT):
                if j >= 2:
                    sp.wait_ge(v_turned, j - 1)
                sp.dma_start(v_raw[j % 2], kv_d[KT + j]).then_inc(v_in[j % 2], 16)

        @block.gpsimd
        def _(pool):
            def stage(n, s, first):
                if not first:
                    pool.wait_ge(scored, n)
                nc.gpsimd.tensor_copy(q_now[:], q[:, :, bass.ds(n * P, P)]).then_inc(staged, 1)

            tiles(pool, stage, lambda n, s, first: None)

        @block.tensor
        def _(pe):
            pe.wait_ge(ident_in, 16)
            for j in range(KT):
                pe.wait_ge(v_in[j % 2], 16 * (j // 2 + 1))
                if j >= 2:
                    pe.wait_ge(v_set, j - 1)
                for i in range(4):
                    mm = nc.tensor.transpose(ps[:, j % 2 * BANK + i * P:j % 2 * BANK + (i + 1) * P], v_raw[j % 2][:, i * P:(i + 1) * P], ident)
                mm.then_inc(v_turned, 1)
            pe.wait_ge(v_set, KT)
            pe.wait_ge(keys_in, 16)

            def score(n, s, first):
                pe.wait_ge(staged, n + 1)
                if not first:
                    pe.wait_ge(expd, 4 * n)
                for h in range(HEADS):
                    for j in range(2):
                        mm = nc.tensor.matmul(ps[:, S_AT + h * M:S_AT + (h + 1) * M], q_now[:, 2 * h + j],
                                              keys[:, 2 * h + j, s * M:(s + 1) * M], start=(j == 0), stop=(j == 1))
                mm.then_inc(scored, 1)

            def answer(n, s, first):
                pe.wait_ge(normed, n + 1)
                if not first:
                    pe.wait_ge(t_set, n)
                for h in range(HEADS):
                    for j in range(2):
                        at = T_AT + (2 * h + j) * P
                        mm = nc.tensor.transpose(ps[:, at:at + P], probs[:, h, j * P:(j + 1) * P], ident)
                mm.then_inc(turned, 1)
                pe.wait_ge(t_set, n + 1)
                if not first:
                    pe.wait_ge(low, n)
                for o in range(KT):
                    for j in range(2):
                        mm = nc.tensor.matmul(ps[:, O_AT + o * P:O_AT + (o + 1) * P], values[:, 2 * s + j, o * P:(o + 1) * P],
                                              probs_t[:, o // 2 * 2 + j], start=(j == 0), stop=(j == 1))
                mm.then_inc(outed, 1)

            tiles(pe, score, answer)

        @block.scalar
        def _(act):
            for j in range(KT):
                act.wait_ge(v_turned, j + 1)
                nc.scalar.copy(values[:, :, j * P:(j + 1) * P], ps[:, j % 2 * BANK:(j % 2 + 1) * BANK].rearrange("p (i t) -> p i t", i=4)).then_inc(v_set, 1)

            def exponentials(n, s, first):
                act.wait_ge(negated, n + 1)
                if first:
                    act.wait_ge(v_turned, KT)
                for h in range(HEADS):
                    nc.scalar.activation(probs[:, h], ps[:, S_AT + h * M:S_AT + (h + 1) * M], ACT.Exp, bias=neg[:, h:h + 1],
                                         scale=SCALE, accum_out=total[:, h:h + 1]).then_inc(expd, 1)

            def turned_out(n, s, first):
                act.wait_ge(turned, n + 1)
                if not first:
                    act.wait_ge(outed, n)
                nc.scalar.copy(probs_t[:], ps[:, T_AT:T_AT + 2 * BANK].rearrange("p (o t) -> p o t", t=P)).then_inc(t_set, 1)

            def high_part(n, s, first):
                act.wait_ge(outed, n + 1)
                nc.scalar.copy(xh[:, :, bass.ds(n * P, P)], ps[:, O_AT:O_AT + 2 * BANK].rearrange("p (o t) -> p o t", t=P)).then_inc(high, 1)

            def begin(n, s, first):
                if not first:
                    turned_out(n - 1, s, isinstance(n, int) and n == 1)
                exponentials(n, s, first)

            def end(n, s, first):
                if isinstance(n, int) and n == N - 1:
                    turned_out(n, s, False)
                high_part(n, s, first)

            tiles(act, begin, end)

        @block.vector
        def _(dve):
            def softmax(n, s, first):
                dve.wait_ge(scored, n + 1)
                nc.vector.tensor_reduce(top[:], heads(ps[:, S_AT:S_AT + 2 * BANK]), mybir.AxisListType.X, ALU.max).then_inc(topped, 1)
                dve.wait_ge(topped, n + 1)
                nc.vector.tensor_scalar(neg[:], top[:], -SCALE, None, ALU.mult).then_inc(negated, 1)
                dve.wait_ge(expd, 4 * n + 4)
                nc.vector.reciprocal(inverse[:], total[:]).then_inc(inverted, 1)
                dve.wait_ge(inverted, n + 1)
                nc.vector.tensor_tensor(probs[:], probs[:], inverse[:].unsqueeze(2).broadcast_to([P, HEADS, M]), ALU.mult).then_inc(normed, 1)

            def low_part(n, s, first):
                dve.wait_ge(high, n + 1)
                at = bass.ds(n * P, P)
                nc.vector.tensor_tensor(xl[:, :, at], ps[:, O_AT:O_AT + 2 * BANK].rearrange("p (o t) -> p o t", t=P), xh[:, :, at],
                                        ALU.subtract).then_inc(low, 1)

            tiles(dve, softmax, low_part)


def memory_phases(nc, a, vecs, kv_d, mem, ones):
    with ExitStack() as ctx:
        m = Memory(nc, ctx, "mem")
        mh, ml = m.sb("h", [P, KT, MEM_T], F32R), m.sb("l", [P, KT, MEM_T], F32R)
        weights = LinearWeights(nc, ctx, "kv", a["ca_w_kv"])
        norm_phase(nc, "memln", mem, ones, vecs, VEC["mem_ln_g"], VEC["mem_ln_b"], tokens=MEM_T, xh=mh, xl=ml, weights=weights)
        linear_phase(nc, "kv", weights, 2 * KT, mh, ml, ((0, MEM_T),), "store", kv_d)


def mix_phases(nc, a, proj_d, pack_d, side_d, vecs, mix_o, mix_y, mem, mem_in):
    with ExitStack() as mixing:
        const_sb = Memory(nc, mixing, "mix").sb("consts", [P, a["consts"].shape[1]])
        consts = {n: const_sb[:, at:at + w] for n, (at, w) in CONST.items()}
        consts["pair"] = consts["pair"].rearrange("p (a t) -> p a t", t=C)
        with ExitStack() as ctx:
            m = Memory(nc, ctx, "gla")
            v = m.sb("v", [P, 4, T])
            q_in, k_in, q_st, k_out = ([m.sb(f"{n}{d}", [P, 2, T]) for d in range(2)] for n in ("q_in", "k_in", "q_st", "k_out"))
            decay = [m.sb(f"decay{d}", [P, 2, N_CHUNKS]) for d in range(2)]
            gla_prepare_phase(nc, a, proj_d, vecs, v, q_in, k_in, q_st, k_out, decay,
                              [o[:, j] for o in (mix_o, mix_y) for j in range(4)], const_sb)
            gla_scan_phase(nc, v, q_in, k_in, q_st, k_out, decay, mix_o, consts)
        gla_finish_phase(nc, proj_d, vecs, mix_o, consts)
        rwkv_prepare_phase(nc, a, proj_d, pack_d, vecs, side_d[0], side_d[1], consts)
        rwkv_scan_phase(nc, pack_d, mix_y, consts)
        rwkv_finish_phase(nc, vecs, mix_y, side_d[0], side_d[1], consts, mem, a["mem"], mem_in)


def build(nc, a, out_d):
    proj_d = nc.dram_tensor("proj", (MIX_TILES, P, T), F32, kind="Internal").ap()
    resid_d = nc.dram_tensor("resid", (P, KT, T), F32, kind="Internal").ap()
    pack_d = nc.dram_tensor("pack", (N_CHUNKS, P, 4, PACK), F32, kind="Internal").ap()
    side_d = nc.dram_tensor("side", (2, P, 4, T), F32, kind="Internal").ap()
    kv_d = nc.dram_tensor("kv", (2 * KT, P, MEM_T), F32, kind="Internal").ap()
    with ExitStack() as ctx:
        m = Memory(nc, ctx, "main")
        vecs = m.sb("vecs", [P, a["vecs"].shape[1]])
        mean_ones = m.sb("mean_ones", [P, P])
        acc = m.sb("acc", [P, KT, T])
        set_ones(nc, mean_ones)
        with ExitStack() as parts:
            mp = Memory(nc, parts, "x1")
            xh, xl = mp.sb("xh", [P, KT, T], F32R), mp.sb("xl", [P, KT, T], F32R)
            with ExitStack() as hold:
                weights = FfnWeights(nc, hold, "ffn1", a["ffn1_w_in"], a["ffn1_w_out"])
                load_phase(nc, a["x"], a["vecs"], acc, xh, xl, vecs, weights)
                ffn_phase(nc, "ffn1", weights, xh, xl, acc)
            weights = LinearWeights(nc, parts, "mixin", a["mix_w_in"])
            norm_phase(nc, "ln1", acc, mean_ones, vecs, VEC["ln_ffn1_g"], VEC["ln_ffn1_b"], scale=0.5, xh=xh, xl=xl, weights=weights)
            linear_phase(nc, "mixin", weights, MIX_TILES, xh, xl, TOKEN_CHUNKS, "store", proj_d, spill=(acc[:], resid_d))
        with ExitStack() as hold:
            mm = Memory(nc, hold, "memory")
            mem, mem_in = mm.sb("tokens", [P, KT, MEM_T]), mm.sem("in")
            mix_phases(nc, a, proj_d, pack_d, side_d, vecs, acc[:, 0:4], acc[:, 4:8], mem, mem_in)
            memory_phases(nc, a, vecs, kv_d, mem, mean_ones)
        with ExitStack() as parts:
            mp = Memory(nc, parts, "x2")
            xh, xl = mp.sb("xh", [P, KT, T], F32R), mp.sb("xl", [P, KT, T], F32R)
            with ExitStack() as hold:
                weights = LinearWeights(nc, hold, "mixout", a["mix_w_out"])
                split_phase(nc, acc, xh, xl, weights)
                linear_phase(nc, "mixout", weights, KT, xh, xl, TOKEN_CHUNKS, "add", acc, reload=resid_d, scale=ALPHA)
            with ExitStack() as queries:
                q = Memory(nc, queries, "attq").sb("q", [P, KT, T])
                with ExitStack() as hold:
                    weights = LinearWeights(nc, hold, "wq", a["ca_w_q"])
                    norm_phase(nc, "ln2", acc, mean_ones, vecs, VEC["ln_mix_g"], VEC["ln_mix_b"], xh=xh, xl=xl, weights=weights)
                    linear_phase(nc, "wq", weights, KT, xh, xl, TOKEN_CHUNKS, "keep", q)
                at, width = CONST["ident"]
                attention_phase(nc, q, kv_d, xh, xl, a["consts"][:, at:at + width])
            with ExitStack() as hold:
                weights = LinearWeights(nc, hold, "wo", a["ca_w_o"])
                linear_phase(nc, "wo", weights, KT, xh, xl, TOKEN_CHUNKS, "add", acc, scale=ALPHA, started=False)
            with ExitStack() as hold:
                weights = FfnWeights(nc, hold, "ffn2", a["ffn2_w_in"], a["ffn2_w_out"])
                norm_phase(nc, "ln3", acc, mean_ones, vecs, VEC["ln_ca_g"], VEC["ln_ca_b"], xh=xh, xl=xl, after=2 * ALPHA, weights=weights)
                ffn_phase(nc, "ffn2", weights, xh, xl, acc)
            norm_phase(nc, "ln4", acc, mean_ones, vecs, VEC["ln_ffn2_g"], VEC["ln_ffn2_b"], scale=0.5, out_d=out_d)


def set_ones(nc, ones):
    with ExitStack() as ctx:
        block = ctx.enter_context(nc.Block())

        @block.vector
        def _(dve):
            nc.vector.memset(ones[:], 1.0 / D)


def constant_table():
    row, tok = np.arange(P)[:, None], np.arange(C)[None, :]
    own = (row // C == np.arange(2)[None, :]).astype(np.float32)
    pair = np.repeat(own, C, 1)
    s = row % C
    upto = [s <= tok, s >= tok]
    before = [s < tok, s > tok]
    levels = []
    for level in range(LEVELS):
        b = 2 ** level
        levels += [(s // b % 2 == 1) & (tok // b == s // b - 1), (s // b % 2 == 0) & (tok // b == s // b + 1)]
    parts = {"ident": np.eye(P), "pair": pair, "ones": np.ones((P, P)), "head_ones": own @ own.T, "twice_ident": np.tile(s == tok, (1, 2)),
             "causal": np.concatenate([pair * np.tile(b, (1, 2)) for b in upto], 1),
             "before_pair": np.concatenate([pair * np.tile(b, (1, 2)) for b in before], 1),
             "upto": np.concatenate(upto, 1), "level": np.concatenate(levels, 1)}
    return {n: v.astype(np.float32) for n, v in parts.items()}


CONST = {}
for _name, _value in constant_table().items():
    CONST[_name] = (sum(w for _, w in CONST.values()), _value.shape[1])


def feature_major(x):
    t, d = x.shape
    return np.ascontiguousarray(x.T.reshape(d // P, P, t).transpose(1, 0, 2))


def column(v):
    return v.reshape(-1, P).T


def output_tiles(w):
    k, n = w.shape
    return w.reshape(k // P, P, n // P, P).transpose(2, 1, 0, 3).reshape(n // P, P, (k // P) * P)


def lay_out(i):
    g = {n: np.asarray(v) for n, v in i.items()}
    out = {"x": feature_major(np.concatenate([g["x_prompt"][0], g["x_sample"][0]], 0)),
           "vecs": np.concatenate([column(g[n][0]) for n in VEC_NAMES], 1)}
    for f in ("ffn1", "ffn2"):
        w = g[f + "_w_in"][0]
        out[f + "_w_in"] = np.concatenate([output_tiles(w[:, :D_FF]), output_tiles(w[:, D_FF:])], 2)
        out[f + "_w_out"] = g[f + "_w_out"][0].reshape(FT, P, D)
    out["mem"] = feature_major(np.concatenate([g["mem_prompt"][0], g["mem_sample"][0]], 0))
    for n in ("mix_w_out", "ca_w_q", "ca_w_kv", "ca_w_o"):
        out[n] = output_tiles(g[n][0])
    def mu_columns(v):
        rkv, wd, ad, gd = v[:1536], v[1536:1664], v[1664:1728], v[1728:]
        return column(np.concatenate([rkv, wd, ad, np.zeros(64, v.dtype), gd]))

    out["vecs"] = np.concatenate(
        [out["vecs"]] + [column(g[n][0]) for n in ("gla_gate_b_fwd", "gla_gate_b_bwd", "gla_norm_g")]
        + [mu_columns(g[n][0]) for n in ("rwkv_mu_prev", "rwkv_mu_next")]
        + [column(g[n][0].reshape(-1)) for n in ("rwkv_w0_fwd", "rwkv_w0_bwd", "rwkv_a0", "rwkv_k_k", "rwkv_k_a", "rwkv_r_k",
                                                 "rwkv_lnx_g", "rwkv_lnx_b")], 1)
    lora = np.zeros((4, P, 4, P), g["rwkv_g_up"].dtype)
    for j, (n, row) in enumerate((("rwkv_w_up_fwd", 0), ("rwkv_w_up_bwd", 64), ("rwkv_a_up", 0), ("rwkv_g_up", 0))):
        w = g[n][0]
        lora[:, row:row + w.shape[0], j] = w.reshape(w.shape[0], 4, P).transpose(1, 0, 2)
    out["lora"] = lora.reshape(4, P, 4 * P)
    w = g["mix_w_in"][0]
    starts = np.cumsum([0, 256, 256, 512, 512, 16, 16, 512, 512, 512, 64, 64, 64, 128])
    q, k, v, gg, gdf, gdb, r, kr, vr, wdf, wdb, ad, gd = (w[:, x:y] for x, y in zip(starts[:-1], starts[1:]))
    pad = np.zeros((D, 32), w.dtype)
    out["mix_w_in"] = output_tiles(np.concatenate([q, k, v, gg, r, kr, vr, wdf, wdb, ad, gdf, gdb, pad, gd], 1))
    up = np.zeros((P, 4 * P), w.dtype)
    up[64:80, :2 * P] = g["gla_gate_up_fwd"][0]
    up[80:96, 2 * P:] = g["gla_gate_up_bwd"][0]
    out["gla_up"] = up
    out["consts"] = np.concatenate(list(constant_table().values()), 1)
    out["keep"] = np.tile((np.arange(T) % C != 0).astype(np.float32), (P, 1))
    return {n: np.ascontiguousarray(v) for n, v in out.items()}


def kernel(**inputs):
    import concourse.bacc as bacc
    from concourse.bass_utils import run_bass_kernel_spmd as run

    nc = bacc.Bacc("TRN2", target_bir_lowering=False, num_devices=1)
    arrays = {n + "_dram": v for n, v in lay_out(inputs).items()}
    args = {n[:-5]: nc.dram_tensor(n, v.shape, F32, kind="ExternalInput").ap() for n, v in arrays.items()}
    out_d = nc.dram_tensor("y_dram", (P, KT, T), F32, kind="ExternalOutput").ap()
    build(nc, args, out_d)
    y = run(nc, [arrays], core_ids=[0]).results[0]["y_dram"]
    y = y.transpose(2, 1, 0).reshape(T, D)
    return y[None, :T_PROMPT], y[None, T_PROMPT:]
```
